# Optimizing a Trainium2 kernel written in Bass

```python
import math
import jax, jax.numpy as jnp
from jax import lax
import numpy as np

D_MODEL = 1024
BATCH = 1
SEQ = 1024
DEPTH = 2

CTX_LEN = 256
GRID_W = 64
F32 = jnp.float32

GLA_HEADS = 4
GLA_DK = 64
GLA_DV = 64
GLA_GATE_RANK = 16
GLA_GATE_NORM = 16.0
GLA_CHUNK = 64
DIFF_HEADS = 4
DIFF_DH = 32
DIFF_DV = 2 * DIFF_DH
SWA_HEADS = 8
SWA_KV_HEADS = 2
SWA_Q_PER_KV = SWA_HEADS // SWA_KV_HEADS
SWA_DH = 64
WINDOW = 128
BLOCK = 128
ROPE_BASE = 10000.0

GLA_QK_W = GLA_HEADS * GLA_DK
GLA_V_W = GLA_HEADS * GLA_DV
DIFF_QK_W = DIFF_HEADS * 2 * DIFF_DH
DIFF_V_W = DIFF_HEADS * DIFF_DV
SWA_Q_W = SWA_HEADS * SWA_DH
SWA_KV_W = SWA_KV_HEADS * SWA_DH
IN_SPLITS = (GLA_QK_W, GLA_QK_W, GLA_V_W, GLA_V_W, GLA_GATE_RANK, GLA_GATE_RANK,
             DIFF_QK_W, DIFF_QK_W, DIFF_V_W, SWA_Q_W, SWA_KV_W, SWA_KV_W)
IN_WIDTH = 2 * GLA_QK_W + 2 * GLA_V_W + 2 * GLA_GATE_RANK + 2 * DIFF_QK_W + DIFF_V_W + SWA_Q_W + 2 * SWA_KV_W
MIX_WIDTH = GLA_V_W + DIFF_V_W + SWA_Q_W

FFN_HIDDEN = ((8 * D_MODEL // 3 + 255) // 256) * 256
DN_ALPHA = (2.0 * DEPTH) ** 0.25
DN_BETA = (8.0 * DEPTH) ** -0.25

kernel_name = 'hybrid_gla_diff_swa_dit_block'

def _ln_plain(x, eps=1e-6):
    xf = x.astype(F32)
    mu = jnp.mean(xf, -1, keepdims=True)
    var = jnp.mean(jnp.square(xf - mu), -1, keepdims=True)
    return (xf - mu) * lax.rsqrt(var + eps)

def layer_norm(x, g, b):
    return (_ln_plain(x) * g.astype(F32) + b.astype(F32)).astype(x.dtype)

def rms_norm(x, g, eps=1e-6):
    xf = x.astype(F32)
    y = xf * lax.rsqrt(jnp.mean(jnp.square(xf), -1, keepdims=True) + eps)
    return (y * g.astype(F32)).astype(x.dtype)

def modulate(x, shift, scale):
    return (_ln_plain(x) * (1.0 + scale.astype(F32)) + shift.astype(F32)).astype(x.dtype)

def axial_rope(rows, dim):
    row = jnp.repeat(jnp.arange(rows, dtype=F32), GRID_W)
    col = jnp.tile(jnp.arange(GRID_W, dtype=F32), rows)
    n_freq = dim // 4
    inv = jnp.power(ROPE_BASE, -jnp.arange(n_freq, dtype=F32) / n_freq)
    ang = jnp.concatenate([row[:, None] * inv, col[:, None] * inv], axis=-1)
    return jnp.cos(ang), jnp.sin(ang)

def apply_rope(x, cos, sin):
    half = x.shape[-1] // 2
    x1 = x[..., :half].astype(F32)
    x2 = x[..., half:].astype(F32)
    return jnp.concatenate([x1 * cos - x2 * sin, x1 * sin + x2 * cos], -1).astype(x.dtype)

def project_heads(p, w_gate2, b_gate2, rope_d, rope_s):
    bsz, n, _ = p.shape
    offs = [int(o) for o in np.cumsum(IN_SPLITS)[:-1]]
    g_q, g_k, g_v, g_o, g_zf, g_zb, d_q, d_k, d_v, s_q, s_k, s_v = jnp.split(p, offs, axis=-1)

    def heads(a, h):
        return jnp.moveaxis(a.reshape(bsz, n, h, -1), 2, 1)

    def gla_gate(z, w, b):
        return jax.nn.log_sigmoid((z @ w + b).astype(F32)) / GLA_GATE_NORM

    out = {
        'gq': heads(g_q, GLA_HEADS) * GLA_DK ** -0.5,
        'gk': heads(g_k, GLA_HEADS),
        'gv': heads(g_v, GLA_HEADS),
        'go': g_o,
        'gf': heads(gla_gate(g_zf, w_gate2[0], b_gate2[0]), GLA_HEADS),
        'gb': heads(gla_gate(g_zb, w_gate2[1], b_gate2[1]), GLA_HEADS),
        'dq': d_q.reshape(bsz, n, DIFF_HEADS, 2, DIFF_DH).transpose(0, 2, 3, 1, 4),
        'dk': d_k.reshape(bsz, n, DIFF_HEADS, 2, DIFF_DH).transpose(0, 2, 3, 1, 4),
        'dv': heads(d_v, DIFF_HEADS),
        'sq': s_q.reshape(bsz, n, SWA_KV_HEADS, SWA_Q_PER_KV, SWA_DH).transpose(0, 2, 3, 1, 4),
        'sk': heads(s_k, SWA_KV_HEADS),
        'sv': heads(s_v, SWA_KV_HEADS),
    }
    if rope_d is not None:
        for name in ('dq', 'dk'):
            out[name] = apply_rope(out[name], *rope_d)
        for name in ('sq', 'sk'):
            out[name] = apply_rope(out[name], *rope_s)
    return out

def gla_chunked(q, k, v, g, s0):
    bsz, nh, n, _ = q.shape
    nc = n // GLA_CHUNK

    def to_chunks(a):
        a = a.astype(F32).reshape(bsz, nh, nc, GLA_CHUNK, a.shape[-1])
        return jnp.moveaxis(a, 2, 0)

    lower = jnp.tril(jnp.ones((GLA_CHUNK, GLA_CHUNK), dtype=bool))[:, :, None]

    def step(state, inp):
        qc, kc, vc, gc = inp
        b = jnp.cumsum(gc, axis=2)
        rel = jnp.exp(jnp.where(lower, b[:, :, :, None, :] - b[:, :, None, :, :], -jnp.inf))
        att = jnp.einsum('bhtk,bhsk,bhtsk->bhts', qc, kc, rel)
        o = (jnp.einsum('bhtk,bhkv->bhtv', qc * jnp.exp(b), state)
             + jnp.einsum('bhts,bhsv->bhtv', att, vc))
        b_end = b[:, :, -1:, :]
        new_state = (jnp.exp(b_end[:, :, 0, :])[..., None] * state
                     + jnp.einsum('bhsk,bhsv->bhkv', kc * jnp.exp(b_end - b), vc))
        return new_state, o

    s_fin, o = lax.scan(step, s0.astype(F32), (to_chunks(q), to_chunks(k), to_chunks(v), to_chunks(g)))
    o = jnp.moveaxis(o, 0, 2).reshape(bsz, nh, n, -1)
    return o.astype(v.dtype), s_fin

def gla_reverse(q, k, v, g, s0):
    o, s = gla_chunked(jnp.flip(q, 2), jnp.flip(k, 2), jnp.flip(v, 2), jnp.flip(g, 2), s0)
    return jnp.flip(o, 2), s

def gla_output(o, og, g):
    bsz, nh, n, dv = o.shape
    on = rms_norm(jnp.moveaxis(o, 1, 2), g)
    return (on * jax.nn.silu(og.reshape(bsz, n, nh, dv))).reshape(bsz, n, nh * dv)

def diff_attend(q, k, v, lam):
    s = jnp.einsum('bhctd,bhcmd->bhctm', q, k).astype(F32) * (DIFF_DH ** -0.5)
    p = jax.nn.softmax(s, axis=-1)
    w = p[:, :, 0] - lam * p[:, :, 1]
    return jnp.einsum('bhtm,bhmv->bhtv', w.astype(v.dtype), v)

def diff_latent(q, k_all, v_all, lam):
    bsz, nh, _, n, dh = q.shape
    nb = n // BLOCK
    qb = jnp.moveaxis(q.reshape(bsz, nh, 2, nb, BLOCK, dh), 3, 0)
    ob = lax.map(lambda qi: diff_attend(qi, k_all, v_all, lam), qb)
    return jnp.moveaxis(ob, 0, 2).reshape(bsz, nh, n, -1)

def diff_output(o, g, lam_init):
    bsz, nh, n, dv = o.shape
    on = rms_norm(o, g) * (1.0 - lam_init)
    return jnp.moveaxis(on, 1, 2).reshape(bsz, n, nh * dv)

def swa_latent(q, k, v, kc, vc, sink):
    bsz, ng, nr, n, dh = q.shape
    nb = n // BLOCK
    n_ctx = kc.shape[2]
    scale = dh ** -0.5
    pad = ((0, 0), (0, 0), (BLOCK, BLOCK), (0, 0))
    k_pad = jnp.pad(k, pad)
    v_pad = jnp.pad(v, pad)

    def one_block(i):
        start = i * BLOCK
        qi = lax.dynamic_slice_in_dim(q, start, BLOCK, axis=3)
        ki = lax.dynamic_slice_in_dim(k_pad, start, 3 * BLOCK, axis=2)
        vi = lax.dynamic_slice_in_dim(v_pad, start, 3 * BLOCK, axis=2)
        pos_q = start + jnp.arange(BLOCK)
        pos_k = start - BLOCK + jnp.arange(3 * BLOCK)
        valid = ((jnp.abs(pos_k[None, :] - pos_q[:, None]) <= WINDOW)
                 & (pos_k >= 0)[None, :] & (pos_k < n)[None, :])
        s_loc = jnp.einsum('bgrtd,bgjd->bgrtj', qi, ki).astype(F32) * scale
        s_loc = jnp.where(valid, s_loc, -jnp.inf)
        s_ctx = jnp.einsum('bgrtd,bgmd->bgrtm', qi, kc).astype(F32) * scale
        s_snk = jnp.broadcast_to(sink.astype(F32)[None, :, :, None, None], s_ctx.shape[:-1] + (1,))
        p = jax.nn.softmax(jnp.concatenate([s_ctx, s_loc, s_snk], axis=-1), axis=-1).astype(v.dtype)
        return (jnp.einsum('bgrtm,bgmd->bgrtd', p[..., :n_ctx], vc)
                + jnp.einsum('bgrtj,bgjd->bgrtd', p[..., n_ctx:n_ctx + 3 * BLOCK], vi))

    ob = lax.map(one_block, jnp.arange(nb))
    return jnp.moveaxis(ob, 0, 3).reshape(bsz, ng, nr, n, dh)

def swa_context(q, kc, vc, sink):
    s = jnp.einsum('bgrtd,bgmd->bgrtm', q, kc).astype(F32) * (q.shape[-1] ** -0.5)
    s_snk = jnp.broadcast_to(sink.astype(F32)[None, :, :, None, None], s.shape[:-1] + (1,))
    p = jax.nn.softmax(jnp.concatenate([s, s_snk], axis=-1), axis=-1)[..., :-1].astype(vc.dtype)
    return jnp.einsum('bgrtm,bgmd->bgrtd', p, vc)

def swa_output(o):
    bsz, ng, nr, n, dh = o.shape
    return o.transpose(0, 3, 1, 2, 4).reshape(bsz, n, ng * nr * dh)

def post_norm(h, y, gate, g, b):
    return layer_norm(DN_ALPHA * h + gate * y, g, b)

def swiglu_sublayer(h, shift, scale, gate, w_g, w_u, w_d, g, b):
    u = modulate(h, shift, scale)
    f = (jax.nn.silu(u @ w_g) * (u @ w_u)) @ w_d
    return post_norm(h, f, gate, g, b)

def setup_inputs(seed: int = 0) -> dict:
    key = jax.random.key(seed)
    ks = jax.random.split(key, 20)
    D = D_MODEL

    def nrm(k, shape, s):
        return jax.random.normal(k, shape, F32) * s

    return {
        'x': nrm(ks[0], (BATCH, SEQ, D), 1.0),
        'c': nrm(ks[1], (BATCH, D), 1.0),
        'ctx': nrm(ks[2], (BATCH, CTX_LEN, D), 1.0),
        'c_ctx': nrm(ks[3], (D,), 1.0),
        'w_ada': nrm(ks[4], (DEPTH, D, 6 * D), 0.5 * D ** -0.5),
        'b_ada': nrm(ks[5], (DEPTH, 6 * D), 0.02),
        'w_in': nrm(ks[6], (DEPTH, D, IN_WIDTH), D ** -0.5),
        'w_gla_gate': nrm(ks[7], (DEPTH, 2, GLA_GATE_RANK, GLA_QK_W), GLA_GATE_RANK ** -0.5),
        'b_gla_gate': nrm(ks[8], (DEPTH, 2, GLA_QK_W), 0.1),
        'gla_norm_g': 1.0 + nrm(ks[9], (DEPTH, GLA_DV), 0.02),
        'diff_lambda': nrm(ks[10], (DEPTH, 4, DIFF_DH), 0.1),
        'diff_norm_g': 1.0 + nrm(ks[11], (DEPTH, DIFF_DV), 0.02),
        'swa_sink': nrm(ks[12], (DEPTH, SWA_HEADS), 0.5),
        'w_out': nrm(ks[13], (DEPTH, MIX_WIDTH, D), MIX_WIDTH ** -0.5 * DN_BETA),
        'ln_g': 1.0 + nrm(ks[14], (DEPTH, 2, D), 0.02),
        'ln_b': nrm(ks[15], (DEPTH, 2, D), 0.02),
        'w_ffn_gate': nrm(ks[16], (DEPTH, D, FFN_HIDDEN), D ** -0.5),
        'w_ffn_up': nrm(ks[17], (DEPTH, D, FFN_HIDDEN), D ** -0.5),
        'w_ffn_down': nrm(ks[18], (DEPTH, FFN_HIDDEN, D), FFN_HIDDEN ** -0.5 * DN_BETA),
    }

def reference(x, c, ctx, c_ctx, w_ada, b_ada, w_in, w_gla_gate, b_gla_gate, gla_norm_g,
              diff_lambda, diff_norm_g, swa_sink, w_out, ln_g, ln_b, w_ffn_gate, w_ffn_up,
              w_ffn_down):
    bsz, n_lat, _ = x.shape
    rows = n_lat // GRID_W
    rope_d = axial_rope(rows, DIFF_DH)
    rope_s = axial_rope(rows, SWA_DH)
    silu_c = jax.nn.silu(c)
    silu_cc = jax.nn.silu(c_ctx)
    h_lat, h_ctx = x, ctx
    for layer in range(DEPTH):
        last = layer == DEPTH - 1
        lam_init = 0.8 - 0.6 * math.exp(-0.3 * layer)
        m_lat = jnp.split((silu_c @ w_ada[layer] + b_ada[layer])[:, None, :], 6, axis=-1)
        m_ctx = jnp.split(silu_cc @ w_ada[layer] + b_ada[layer], 6, axis=-1)

        pl = project_heads(modulate(h_lat, m_lat[0], m_lat[1]) @ w_in[layer],
                           w_gla_gate[layer], b_gla_gate[layer], rope_d, rope_s)
        pc = project_heads(modulate(h_ctx, m_ctx[0], m_ctx[1]) @ w_in[layer],
                           w_gla_gate[layer], b_gla_gate[layer], None, None)

        zero_state = jnp.zeros((bsz, GLA_HEADS, GLA_DK, GLA_DV), F32)
        oc_f, sc_f = gla_chunked(pc['gq'], pc['gk'], pc['gv'], pc['gf'], zero_state)
        oc_b, sc_b = gla_reverse(pc['gq'], pc['gk'], pc['gv'], pc['gb'], zero_state)
        ol_f, _ = gla_chunked(pl['gq'], pl['gk'], pl['gv'], pl['gf'], sc_f)
        ol_b, _ = gla_reverse(pl['gq'], pl['gk'], pl['gv'], pl['gb'], sc_b)
        gla_lat = gla_output(ol_f + ol_b, pl['go'], gla_norm_g[layer])

        lq1 = diff_lambda[layer, 0]
        lk1 = diff_lambda[layer, 1]
        lq2 = diff_lambda[layer, 2]
        lk2 = diff_lambda[layer, 3]
        lam = (jnp.exp(jnp.sum(lq1.astype(F32) * lk1.astype(F32)))
               - jnp.exp(jnp.sum(lq2.astype(F32) * lk2.astype(F32))) + lam_init)
        dk_all = jnp.concatenate([pc['dk'], pl['dk']], axis=3)
        dv_all = jnp.concatenate([pc['dv'], pl['dv']], axis=2)
        diff_lat = diff_output(diff_latent(pl['dq'], dk_all, dv_all, lam), diff_norm_g[layer], lam_init)

        sink = swa_sink[layer].reshape(SWA_KV_HEADS, SWA_Q_PER_KV)
        swa_lat = swa_output(swa_latent(pl['sq'], pl['sk'], pl['sv'], pc['sk'], pc['sv'], sink))

        y_lat = jnp.concatenate([gla_lat, diff_lat, swa_lat], axis=-1) @ w_out[layer]
        h_lat_mid = post_norm(h_lat, y_lat, m_lat[2], ln_g[layer, 0], ln_b[layer, 0])
        h_lat_next = swiglu_sublayer(h_lat_mid, m_lat[3], m_lat[4], m_lat[5], w_ffn_gate[layer],
                                     w_ffn_up[layer], w_ffn_down[layer], ln_g[layer, 1], ln_b[layer, 1])

        if not last:
            gla_ctx = gla_output(oc_f + oc_b, pc['go'], gla_norm_g[layer])
            diff_ctx = diff_output(diff_attend(pc['dq'], pc['dk'], pc['dv'], lam), diff_norm_g[layer], lam_init)
            swa_ctx = swa_output(swa_context(pc['sq'], pc['sk'], pc['sv'], sink))
            y_ctx = jnp.concatenate([gla_ctx, diff_ctx, swa_ctx], axis=-1) @ w_out[layer]
            h_ctx_mid = post_norm(h_ctx, y_ctx, m_ctx[2], ln_g[layer, 0], ln_b[layer, 0])
            h_ctx = swiglu_sublayer(h_ctx_mid, m_ctx[3], m_ctx[4], m_ctx[5], w_ffn_gate[layer],
                                    w_ffn_up[layer], w_ffn_down[layer], ln_g[layer, 1], ln_b[layer, 1])
        h_lat = h_lat_next
    return h_lat


_drawn_inputs = setup_inputs


def setup_inputs(seed=0):
    import zlib

    import numpy as np

    out = dict(_drawn_inputs(seed))
    spreads = {}
    factors = {'ctx': 5.035,
     'b_ada': 4.993,
     'w_gla_gate': 7.588,
     'b_gla_gate': 8.0,
     'gla_norm_g': 51.24,
     'diff_lambda': 8.0,
     'diff_norm_g': 44.266,
     'swa_sink': 200.0}
    for name, (base, spread) in spreads.items():
        noise = np.random.default_rng([zlib.crc32(name.encode()), seed]).standard_normal(out[name].shape)
        drawn = base * np.exp(spread * noise) if base else spread * noise
        out[name] = __import__('jax').numpy.asarray(drawn.astype(out[name].dtype))
    for name, factor in factors.items():
        out[name] = (out[name] * factor).astype(out[name].dtype)
    return out
```

```python
import math
from contextlib import ExitStack

import concourse.bass as bass
import concourse.mybir as mybir

F32 = mybir.dt.float32
F32R = mybir.dt.float32r
I32 = mybir.dt.int32
ALU = mybir.AluOpType
ACT = mybir.ActivationFunctionType
AX = mybir.AxisListType

P = 128
LAYERS = 2
D = 1024
KT = D // P
N_CTX, N_LAT = 256, 1024
T = N_CTX + N_LAT
CTX_TILES, LAT_TILES = N_CTX // P, N_LAT // P
TILES = CTX_TILES + LAT_TILES
BANK = 512
CHUNKS = [(256, 512), (768, 512), (0, 256)]
LAT_CHUNKS = CHUNKS[:2]

FFN = 2816
FFN_TILES = FFN // P
FFN_GROUPS = FFN_TILES // 2
ADA = 6 * D
ADA_CHUNKS = ADA // BANK

T_Z, T_GQ, T_GK, T_GV, T_GO, T_DV, T_SV = 0, 1, 3, 5, 7, 9, 11
T_DQ, T_DK, T_SQ, T_SK = 12, 14, 16, 20
IN_TILES = 21
PLAIN_TILES = 12
PAD_T = T + P

GATE_RANK = 16
GATE_NORM = 16.0
CH = 128
NCH = T // CH
LEVELS = [64, 32, 16, 8, 4, 2, 1]
DIFF_HEADS, DIFF_DH = 4, 32
SWA_HEADS, SWA_DH = 8, 64
SWA_KEYS = N_CTX + 3 * P
EPS = 1e-6
ALPHA = (2.0 * LAYERS) ** 0.25


def peeled(eng, first, end, body):
    body(first, True)
    if end - first > 1:
        with eng.Fori(first + 1, end) as i:
            body(i, False)


def wait_apart(eng, sem, value, passed):
    eng.wait_ge(sem, value)
    eng.sem_inc(passed, 1)


def allocators(nc, ctx, phase):
    def sb(name, shape, dt=F32):
        return ctx.enter_context(nc.sbuf_tensor(name, shape, dt))

    def ps(name, shape):
        return ctx.enter_context(nc.psum_tensor(name, shape, F32))

    def sem(name):
        return nc.alloc_semaphore(phase + name)
    return sb, ps, sem


def product(pe, out, st_hi, st_lo, mv_hi, mv_lo, start, stop):
    pe.matmul(out, st_hi, mv_hi, start=start, stop=False)
    pe.matmul(out, st_hi, mv_lo, start=False, stop=False)
    return pe.matmul(out, st_lo, mv_hi, start=False, stop=stop)


def modulation(nc, t):
    with nc.cleanup_on_exit(), ExitStack() as ctx:
        sb, ps, sem = allocators(nc, ctx, "ada_")
        cT = sb("ada_c", [P, KT, 2])
        cs = sb("ada_silu", [P, KT, 2])
        W = sb("ada_w", [P, 4, KT, BANK])
        B = sb("ada_b", [2, 4, BANK])
        R = sb("ada_rows", [2, 4, BANK])
        acc = ps("ada_acc", [P, 4, BANK])
        c_in, c_silu = sem("c_in"), sem("c_silu")
        w_in = [sem(f"ada_w_in{s}") for s in range(4)]
        product_done, row_done = sem("ada_product_done"), sem("ada_row_done")
        row_out = [sem(f"ada_row_out{s}") for s in range(4)]
        steps = LAYERS * ADA_CHUNKS // 4
        per_layer = ADA_CHUNKS // 4
        block = ctx.enter_context(nc.Block())

        @block.sync
        def _(sp):
            sp.dma_start(cT[:, :, :], t["cT"]).then_inc(c_in, 16)
            for l in range(LAYERS):
                def body(i, first):
                    for s in range(4):
                        col = i * 4 * BANK + s * BANK
                        if not first:
                            sp.wait_ge(product_done, 4 * (l * per_layer + i - 1) + s + 1)
                            sp.wait_ge(row_done, 4 * (l * per_layer + i - 1) + s + 1)
                        elif l:
                            sp.wait_ge(product_done, 4 * (l * per_layer - 1) + s + 1)
                            sp.wait_ge(row_done, 4 * (l * per_layer - 1) + s + 1)
                        sp.dma_start(W[:, s, :, :], t["w_ada"][l].rearrange("(k p) n -> p k n", p=P)[:, :, bass.ds(col, BANK)]).then_inc(w_in[s], 16)
                        sp.dma_start(B[:, s, :], t["b_ada"][l:l + 1, bass.ds(col, BANK)].to_broadcast([2, BANK])).then_inc(w_in[s], 16)
                peeled(sp, 0, per_layer, body)

        @block.scalar
        def _(act):
            act.wait_ge(c_in, 16)
            act.activation(cs[:, :, :], cT[:, :, :], ACT.Silu).then_inc(c_silu, 1)
            for l in range(LAYERS):
                with act.Fori(0, per_layer) as i:
                    for s in range(4):
                        act.wait_ge(row_done, 4 * (l * per_layer) + i * 4 + s + 1)
                        act.dma_start(t["mod"][l, :, bass.ds(i * 4 * BANK + s * BANK, BANK)], R[:, s, :]).then_inc(row_out[s], 16)
            for s in range(4):
                act.wait_ge(row_out[s], 16 * steps)

        @block.tensor
        def _(pe):
            pe.wait_ge(c_silu, 1)

            def body(i, first):
                for s in range(4):
                    pe.wait_ge(w_in[s], i * 32 + 32)
                    if not first:
                        pe.wait_ge(row_done, 4 * (i - 1) + s + 1)
                    for k in range(KT):
                        mm = pe.matmul(acc[0:2, s, :], cs[:, k, :], W[:, s, k, :], start=(k == 0), stop=(k == KT - 1))
                    mm.then_inc(product_done, 1)
            peeled(pe, 0, steps, body)

        @block.vector
        def _(dve):
            def body(i, first):
                for s in range(4):
                    dve.wait_ge(product_done, i * 4 + s + 1)
                    if not first:
                        dve.wait_ge(row_out[s], i * 16)
                    dve.tensor_tensor(R[:, s, :], acc[0:2, s, :], B[:, s, :], ALU.add).then_inc(row_done, 1)
            peeled(dve, 0, steps, body)


def norm_tiles(nc, t, res, kind, layer, tiles, last):
    with nc.cleanup_on_exit(), ExitStack() as ctx:
        sb, ps, sem = allocators(nc, ctx, f"norm_{kind}{layer}_")
        nm = f"norm_{kind}{layer}_"
        post = kind != "input"
        attn = kind == "attention"
        modulated = not last
        first_pair = tiles[0] // 2
        pairs = len(tiles) // 2
        streams = [0, 1] if tiles[0] == 0 else [1]
        next_mod = {"input": (layer, 0, 1), "attention": (layer, 3, 4), "ffn": (layer + 1, 0, 1)}[kind]
        gate_at = 2 if attn else 5
        ln_at = 0 if attn else 1

        uhi, ulo, ident = res["uhi"], res["ulo"], res["ident"]
        hres = sb(nm + "hres", [P, 2, D])
        r = sb(nm + "r", [P, 2, D])
        h = sb(nm + "h", [P, 2, D])
        gate = sb(nm + "gate", [P, 2, D]) if post else None
        lng = sb(nm + "lng", [P, D]) if post else None
        lnb = sb(nm + "lnb", [P, D]) if post else None
        shift = sb(nm + "shift", [P, 2, KT])
        scale = sb(nm + "scale", [P, 2, KT])
        stats = sb(nm + "stats", [P, 2, 2, 2, 6])
        mv = sb(nm + "mv", [P, 2, 2, 2])
        sd = sb(nm + "sd", [P, 2, 2])
        rstd = sb(nm + "rstd", [P, 2, 2])
        nmu = sb(nm + "nmu", [P, 2, 2])
        eps = sb(nm + "eps", [P, 1])
        if attn:
            wohi = sb(nm + "wohi", [P, KT, D], F32R)
            wolo = sb(nm + "wolo", [P, KT, D], F32R)
            mhi = sb(nm + "mhi", [P, 2, KT, P], F32R)
            mlo = sb(nm + "mlo", [P, 2, KT, P], F32R)
            Y = ps(nm + "y", [P, 2, D])
        TR = ps(nm + "tr", [P, 2, KT, P])

        passed, pool_passed = sem("passed"), sem("pool_passed")
        const_in, eps_set, one_plus = sem("const_in"), sem("eps_set"), sem("one_plus")
        h_in = [sem(f"h_in{s}") for s in range(2)]
        mix_in = [sem(f"mix_in{s}") for s in range(2)]
        wo_in = [sem(f"wo_in{s}") for s in range(2)]
        wo_hi, wo_lo = sem("wo_hi"), sem("wo_lo")
        mix_hi, mix_lo, y_done = sem("mix_hi"), sem("mix_lo"), sem("y_done")
        gated, summed = sem("gated"), sem("summed")
        st_done, mv_done, sd_done, rs_done, nm_done = (sem("st_done"), sem("mv_done"), sem("sd_done"), sem("rs_done"), sem("nm_done"))
        ln1, h_scaled, h_done = sem("ln1"), sem("h_scaled"), sem("h_done")
        ln2, turned, u_done, u_hi, u_lo = sem("ln2"), sem("turned"), sem("u_done"), sem("u_hi"), sem("u_lo")
        h_out = [sem(f"h_out{s}") for s in range(2)]
        block = ctx.enter_context(nc.Block())
        consts = 0

        def count(i, s):
            return (i - first_pair) * 2 + s + 1

        def src_rows(i, s):
            if kind == "input":
                return t["ctx"][s * P:(s + 1) * P, :] if i is first_pair and tiles[0] == 0 else t["x"][bass.ds(i * 2 * P + (s * P - N_CTX), P), :]
            if attn and layer == 0:
                return t["ctx"][s * P:(s + 1) * P, :] if i is first_pair and tiles[0] == 0 else t["x"][bass.ds(i * 2 * P + (s * P - N_CTX), P), :]
            return t["h_mid" if not attn else "h_next"][bass.ds(i * 2 * P + s * P, P), :]

        def dst_rows(i, s):
            if last:
                return t["out"][bass.ds(i * 2 * P + (s * P - N_CTX), P), :]
            return t["h_mid" if attn else "h_next"][bass.ds(i * 2 * P + s * P, P), :]

        @block.sync
        def _(sp):
            if attn:
                for k in range(KT):
                    if k >= 2:
                        sp.wait_ge(wo_lo, k - 1)
                    sp.dma_start(h[:, k % 2, :], t["w_out"][layer, k * P:(k + 1) * P, :]).then_inc(wo_in[k % 2], 16)

            def body(i, first):
                for s in range(2):
                    if not first and modulated:
                        sp.wait_ge(u_lo, count(i, s) - 2)
                        sp.wait_ge(turned, count(i, s) - 2)
                    elif not first:
                        sp.wait_ge(ln1, count(i, s) - 2)
                        sp.wait_ge(summed, count(i, s) - 2)
                    if attn:
                        sp.dma_start(r[:, s, :].rearrange("p (k n) -> p k n", k=KT),
                                     t["mix"].rearrange("(k p) n -> p k n", p=P)[:, :, bass.ds(i * 2 * P + s * P, P)]).then_inc(mix_in[s], 16)
                    sp.dma_start(hres[:, s, :], src_rows(i, s)).then_inc(h_in[s], 16)
            peeled(sp, first_pair, first_pair + pairs, body)

        @block.tensor
        def _(pe):
            if attn:
                pe.wait_ge(wo_lo, KT)

            def body(i, first):
                if attn:
                    for s in range(2):
                        pe.wait_ge(mix_lo, count(i, s))
                        if not first:
                            pe.wait_ge(gated, count(i, s) - 2)
                        for half in range(2):
                            for k in range(KT):
                                cols = slice(half * BANK, (half + 1) * BANK)
                                mm = product(pe, Y[:, s, cols], mhi[:, s, k, :], mlo[:, s, k, :],
                                             wohi[:, k, cols], wolo[:, k, cols], k == 0, k == KT - 1)
                        mm.then_inc(y_done, 1)
                if modulated:
                    for s in range(2):
                        pe.wait_ge(ln2, count(i, s))
                        if not first:
                            pe.wait_ge(u_done, count(i, s) - 2)
                        for k in range(KT):
                            mm = pe.transpose(TR[:, s, k, :], r[:, s, k * P:(k + 1) * P], ident[:, :])
                        mm.then_inc(turned, 1)
            if attn or modulated:
                peeled(pe, first_pair, first_pair + pairs, body)

        LN = post + modulated
        lnc = lambda i, s, j: (i - first_pair) * 2 * LN + j * 2 + s + 1

        @block.vector
        def _(dve):
            if modulated:
                dve.wait_ge(const_in, 16 * (2 * len(streams) + (2 + len(streams) if post else 0)))
                dve.tensor_scalar(scale[:, streams[0]:2, :], scale[:, streams[0]:2, :], 1.0, None, ALU.add).then_inc(one_plus, 1)

            def statistics(i, s, j, src):
                for half in range(2):
                    dve.bn_stats(stats[:, s, j, half, :], src[:, s, half * BANK:(half + 1) * BANK]).then_inc(st_done, 1)
                wait_apart(dve, st_done, 2 * lnc(i, s, j), passed)
                dve.bn_aggr(mv[:, s, j, :], stats[:, s, j, :, :]).then_inc(mv_done, 1)

            def normalizers(i, s, j):
                dve.wait_ge(sd_done, lnc(i, s, j))
                dve.reciprocal(rstd[:, s, j:j + 1], sd[:, s, j:j + 1]).then_inc(rs_done, 1)
                dve.wait_ge(rs_done, lnc(i, s, j))
                dve.scalar_tensor_tensor(nmu[:, s, j:j + 1], mv[:, s, j, 0:1], -1.0, rstd[:, s, j:j + 1], ALU.mult, ALU.mult).then_inc(nm_done, 1)

            def body(i, first):
                st = 0 if (first and tiles[0] == 0) else 1
                if post:
                    for s in range(2):
                        if attn:
                            dve.wait_ge(y_done, count(i, s))
                            dve.tensor_tensor(r[:, s, :], Y[:, s, :], gate[:, st, :], ALU.mult).then_inc(gated, 1)
                        else:
                            if not first:
                                dve.wait_ge(turned, count(i, s) - 2) if modulated else dve.wait_ge(ln1, count(i, s) - 2)
                            if not modulated:
                                dve.wait_ge(const_in, 16 * (2 * len(streams) + 2 + len(streams)))
                            y = res["y"][:, bass.ds(i * 2 + s, 1), :].rearrange("p a b -> p (a b)")
                            dve.tensor_tensor(r[:, s, :], y, gate[:, st, :], ALU.mult).then_inc(gated, 1)
                        dve.wait_ge(gated, count(i, s))
                        dve.wait_ge(h_in[s], (i - first_pair) * 16 + 16)
                        dve.scalar_tensor_tensor(r[:, s, :], hres[:, s, :], ALPHA, r[:, s, :], ALU.mult, ALU.add).then_inc(summed, 1)
                        dve.wait_ge(summed, count(i, s))
                        statistics(i, s, 0, r)
                    for s in range(2):
                        normalizers(i, s, 0)
                    if modulated:
                        for s in range(2):
                            dve.wait_ge(h_done, count(i, s))
                            statistics(i, s, 1, h)
                        for s in range(2):
                            normalizers(i, s, 1)
                else:
                    for s in range(2):
                        dve.wait_ge(h_in[s], (i - first_pair) * 16 + 16)
                        statistics(i, s, 0, hres)
                    for s in range(2):
                        normalizers(i, s, 0)
            peeled(dve, first_pair, first_pair + pairs, body)

        @block.scalar
        def _(act):
            act.wait_ge(eps_set, 1)
            if attn:
                for k in range(KT):
                    act.wait_ge(wo_in[k % 2], 16 * (k // 2 + 1))
                    act.copy(wohi[:, k, :], h[:, k % 2, :]).then_inc(wo_hi, 1)
                act.wait_ge(wo_lo, KT)
            if modulated:
                act.wait_ge(one_plus, 1)

            def deviation(i, s, j):
                act.wait_ge(mv_done, lnc(i, s, j))
                act.activation(sd[:, s, j:j + 1], mv[:, s, j, 1:2], ACT.Sqrt, bias=eps[:, 0:1]).then_inc(sd_done, 1)

            def body(i, first):
                st = 0 if (first and tiles[0] == 0) else 1
                if attn:
                    for s in range(2):
                        act.wait_ge(mix_in[s], (i - first_pair) * 16 + 16)
                        if not first:
                            act.wait_ge(y_done, count(i, s) - 2)
                        act.copy(mhi[:, s, :, :], r[:, s, :].rearrange("p (k n) -> p k n", k=KT)).then_inc(mix_hi, 1)
                if post:
                    for s in range(2):
                        deviation(i, s, 0)
                    for s in range(2):
                        act.wait_ge(nm_done, lnc(i, s, 0))
                        if not first:
                            act.wait_ge(h_out[s], (i - first_pair) * 16)
                        act.activation(h[:, s, :], r[:, s, :], ACT.Identity, scale=rstd[:, s, 0:1], bias=nmu[:, s, 0:1]).then_inc(ln1, 1)
                if modulated:
                    j = 1 if post else 0
                    src = h if post else hres
                    for s in range(2):
                        deviation(i, s, j)
                    for s in range(2):
                        act.wait_ge(nm_done, lnc(i, s, j))
                        if not post and not first:
                            act.wait_ge(turned, count(i, s) - 2)
                        act.activation(r[:, s, :], src[:, s, :], ACT.Identity, scale=rstd[:, s, j:j + 1], bias=nmu[:, s, j:j + 1]).then_inc(ln2, 1)
                    for s in range(2):
                        act.wait_ge(turned, count(i, s))
                        if not post:
                            act.wait_ge(ln2, count(i, s))
                        for k in range(KT):
                            a = act.activation(hres[:, s, k * P:(k + 1) * P], TR[:, s, k, :], ACT.Identity,
                                               scale=scale[:, st, k:k + 1], bias=shift[:, st, k:k + 1])
                        a.then_inc(u_done, 1)
            peeled(act, first_pair, first_pair + pairs, body)

        @block.gpsimd
        def _(pool):
            pool.memset(eps[:, :], EPS).then_inc(eps_set, 1)
            n = 0
            for st in streams:
                for dst, at in ((shift, next_mod[1]), (scale, next_mod[2])):
                    lay = min(next_mod[0], LAYERS - 1)
                    pool.dma_start(dst[:, st, :], t["mod"][lay, 1 - st, at * D:(at + 1) * D].rearrange("(k p) -> p k", p=P)).then_inc(const_in, 16)
                if post:
                    pool.dma_start(gate[:, st, :], t["mod"][layer, 1 - st:2 - st, gate_at * D:(gate_at + 1) * D].to_broadcast([P, D])).then_inc(const_in, 16)
            if post:
                pool.dma_start(lng[:, :], t["ln_g"][layer, ln_at:ln_at + 1, :].to_broadcast([P, D])).then_inc(const_in, 16)
                pool.dma_start(lnb[:, :], t["ln_b"][layer, ln_at:ln_at + 1, :].to_broadcast([P, D])).then_inc(const_in, 16)
            if attn:
                for k in range(KT):
                    pool.wait_ge(wo_hi, k + 1)
                    pool.tensor_tensor(wolo[:, k, :], h[:, k % 2, :], wohi[:, k, :].bitcast(F32), ALU.subtract).then_inc(wo_lo, 1)
            pool.wait_ge(const_in, 16 * (2 * len(streams) + (2 + len(streams) if post else 0)))

            def body(i, first):
                if attn:
                    for s in range(2):
                        pool.wait_ge(mix_hi, count(i, s))
                        pool.tensor_tensor(mlo[:, s, :, :], r[:, s, :].rearrange("p (k n) -> p k n", k=KT),
                                           mhi[:, s, :, :].bitcast(F32), ALU.subtract).then_inc(mix_lo, 1)
                if post:
                    for s in range(2):
                        pool.wait_ge(ln1, count(i, s))
                        pool.tensor_tensor(h[:, s, :], h[:, s, :], lng[:, :], ALU.mult).then_inc(h_scaled, 1)
                        pool.wait_ge(h_scaled, count(i, s))
                        pool.tensor_tensor(h[:, s, :], h[:, s, :], lnb[:, :], ALU.add).then_inc(h_done, 1)
                        pool.wait_ge(h_done, count(i, s))
                        pool.dma_start(dst_rows(i, s), h[:, s, :]).then_inc(h_out[s], 16)
                if modulated:
                    for s in range(2):
                        wait_apart(pool, u_done, count(i, s), pool_passed)
                        u = hres[:, s, :].rearrange("p (k n) -> p k n", k=KT)
                        at = bass.ds(i * 2 * P + s * P, P)
                        pool.tensor_copy(uhi[:, :, at], u).then_inc(u_hi, 1)
                        pool.wait_ge(u_hi, count(i, s))
                        pool.tensor_tensor(ulo[:, :, at], u, uhi[:, :, at].bitcast(F32), ALU.subtract).then_inc(u_lo, 1)
            peeled(pool, first_pair, first_pair + pairs, body)
            if post:
                for s in range(2):
                    pool.wait_ge(h_out[s], 16 * pairs)


def input_projection(nc, t, res, layer):
    with nc.cleanup_on_exit(), ExitStack() as ctx:
        sb, ps, sem = allocators(nc, ctx, f"in{layer}_")
        nm = f"in{layer}_"
        uhi, ulo = res["uhi"], res["ulo"]
        raw = sb(nm + "raw", [P, 2, D])
        whi = sb(nm + "whi", [P, 2, KT, P], F32R)
        wlo = sb(nm + "wlo", [P, 2, KT, P], F32R)
        stage = sb(nm + "stage", [P, 2, T])
        swap = sb(nm + "swap", [P, 2, N_LAT])
        cos = sb(nm + "cos", [P, 2, N_LAT])
        sin = sb(nm + "sin", [P, 2, N_LAT])
        zero = sb(nm + "zero", [P, P])
        acc = ps(nm + "acc", [P, 2, 3, BANK])
        raw_in = [sem(f"raw_in{s}") for s in range(2)]
        passed = sem("passed")
        rope_in, zero_set, pad_out = sem("rope_in"), sem("zero_set"), sem("pad_out")
        w_hi, w_ready, chunk_done, evacuated = sem("w_hi"), sem("w_ready"), sem("chunk_done"), sem("evacuated")
        swapped, cos_done, sin_done, roped = sem("swapped"), sem("cos_done"), sem("sin_done"), sem("roped")
        stored = [sem(f"stored{s}") for s in range(2)]
        NCHK = len(CHUNKS)
        block = ctx.enter_context(nc.Block())
        pairs = IN_TILES // 2
        MASK = list(range(16, 32)) + list(range(16))

        def each_tile(eng, body, pairs_from=0, pairs_to=pairs, tail=True):
            def two(i, first):
                for s in range(2):
                    body(i * 2 + s, i, s, first and pairs_from == 0)
            if pairs_from == 0:
                peeled(eng, 0, pairs_to, two)
            else:
                with eng.Fori(pairs_from, pairs_to) as i:
                    two(i, False)
            if tail:
                body(IN_TILES - 1, pairs, 0, False)

        @block.sync
        def _(sp):
            sp.dma_start(cos[:, :, :], t["rope_cos"].rearrange("a p n -> p a n")).then_inc(rope_in, 16)
            sp.dma_start(sin[:, :, :], t["rope_sin"].rearrange("a p n -> p a n")).then_inc(rope_in, 16)

            def body(n, i, s, first):
                if not first:
                    sp.wait_ge(w_ready, n - 1)
                sp.dma_start(raw[:, s, :], t["w_in"][layer][bass.ds(n * P, P), :]).then_inc(raw_in[s], 16)
            each_tile(sp, body)

        @block.gpsimd
        def _(pool):
            pool.memset(zero[:, :], 0.0).then_inc(zero_set, 1)
            pool.wait_ge(zero_set, 1)
            for tile in (T_SK, T_SV):
                pool.dma_start(t["proj"][tile * P:(tile + 1) * P, T:PAD_T], zero[:, :]).then_inc(pad_out, 16)
            pool.wait_ge(rope_in, 32)

            def split(n, i, s, first):
                pool.wait_ge(w_hi, n + 1)
                pool.tensor_tensor(wlo[:, s, :, :], raw[:, s, :].rearrange("p (k n) -> p k n", k=KT),
                                   whi[:, s, :, :].bitcast(F32), ALU.subtract).then_inc(w_ready, 1)
            each_tile(pool, split)
            pool.wait_ge(pad_out, 32)

        @block.tensor
        def _(pe):
            def body(n, i, s, first):
                pe.wait_ge(w_ready, n + 1)
                for c, (t0, tn) in enumerate(CHUNKS):
                    if not first:
                        pe.wait_ge(evacuated, (n - 2) * NCHK + c + 1)
                    for k in range(KT):
                        mm = product(pe, acc[:, s, c, 0:tn], whi[:, s, k, :], wlo[:, s, k, :],
                                     uhi[:, k, t0:t0 + tn], ulo[:, k, t0:t0 + tn], k == 0, k == KT - 1)
                    mm.then_inc(chunk_done, 1)
            each_tile(pe, body)

        @block.scalar
        def _(act):
            def body(n, i, s, first, rope=False):
                act.wait_ge(raw_in[s], i * 16 + 16)
                if not first:
                    act.wait_ge(chunk_done, (n - 1) * NCHK)
                    act.wait_ge(stored[s], i * 16)
                act.copy(whi[:, s, :, :], raw[:, s, :].rearrange("p (k n) -> p k n", k=KT)).then_inc(w_hi, 1)

            def finish(n, i, s, rope):
                for c, (t0, tn) in enumerate(CHUNKS):
                    act.wait_ge(chunk_done, n * NCHK + c + 1)
                    act.copy(stage[:, s, t0:t0 + tn], acc[:, s, c, 0:tn]).then_inc(evacuated, 1)
                act.wait_ge(evacuated, (n + 1) * NCHK)
                if rope:
                    act.wait_ge(roped, n - PLAIN_TILES + 1)
                act.dma_start(t["proj"][bass.ds(n * P, P), 0:T], stage[:, s, :]).then_inc(stored[s], 16)

            body(0, 0, 0, True)
            body(1, 0, 1, True)
            for lo, hi, rope in ((0, PLAIN_TILES // 2, False), (PLAIN_TILES // 2, pairs - 1, True)):
                with act.Fori(lo, hi) as i:
                    for s in range(2):
                        finish(i * 2 + s, i, s, rope)
                        body(i * 2 + s + 2, i + 1, s, False)
            finish(2 * pairs - 2, pairs - 1, 0, True)
            body(2 * pairs, pairs, 0, False)
            finish(2 * pairs - 1, pairs - 1, 1, True)
            finish(2 * pairs, pairs, 0, True)
            for s in range(2):
                act.wait_ge(stored[s], 16 * ((IN_TILES + 1 - s) // 2))

        @block.vector
        def _(dve):
            dve.wait_ge(rope_in, 32)

            def rope(n, s, table):
                m = n - PLAIN_TILES + 1
                x = stage[:, s, N_CTX:T]
                wait_apart(dve, evacuated, (n + 1) * NCHK, passed)
                dve.stream_shuffle(swap[:, s, :], x, MASK).then_inc(swapped, 1)
                dve.wait_ge(swapped, m)
                dve.tensor_tensor(x, x, cos[:, table, :], ALU.mult).then_inc(cos_done, 1)
                dve.tensor_tensor(swap[:, s, :], swap[:, s, :], sin[:, table, :], ALU.mult).then_inc(sin_done, 1)
                dve.wait_ge(cos_done, m)
                dve.wait_ge(sin_done, m)
                dve.tensor_tensor(x, x, swap[:, s, :], ALU.add).then_inc(roped, 1)
            for lo, hi, table in ((T_DQ // 2, T_SQ // 2, 0), (T_SQ // 2, pairs, 1)):
                with dve.Fori(lo, hi) as i:
                    for s in range(2):
                        rope(i * 2 + s, s, table)
            rope(IN_TILES - 1, 0, 1)


def gated_linear_attention(nc, t, res, layer):
    with nc.cleanup_on_exit(), ExitStack() as ctx:
        sb, ps, sem = allocators(nc, ctx, f"gla{layer}_")
        nm = f"gla{layer}_"
        ident = res["ident"]
        FLAT = [(0, 512), (512, 512), (1024, 256)]
        DI = [(d, i) for d in range(2) for i in range(2)]
        q = sb(nm + "q", [P, 2, T])
        k = sb(nm + "k", [P, 2, T])
        vT = sb(nm + "vT", [P, 2, T])
        V = sb(nm + "V", [P, TILES, 2 * P])
        z = sb(nm + "z", [2 * GATE_RANK, T])
        wg = sb(nm + "wg", [2 * GATE_RANK, 2, 2 * P])
        bg = sb(nm + "bg", [P, 2, 2])
        normg = sb(nm + "normg", [P, 1])
        reset = sb(nm + "reset", [P, T])
        B = sb(nm + "B", [P, 4, T])
        Dc = sb(nm + "D", [P, 2, T])
        X = sb(nm + "X", [P, 2, T])
        Qe = sb(nm + "Qe", [P, 4, T])
        KeT = sb(nm + "KeT", [P, 2, NCH, P])
        dec = sb(nm + "dec", [P, 4, NCH])
        S = sb(nm + "S", [P, 4, NCH, P])
        A = sb(nm + "A", [P, 2, 2, NCH, CH])
        masks = sb(nm + "masks", [P, 2 * len(LEVELS) + 1, CH], I32)
        block_mean = sb(nm + "block_mean", [P, P])
        eps = sb(nm + "eps", [P, 1])
        UNIT = ps(nm + "unit", [P, 2, 3 * BANK])
        TR = ps(nm + "tr", [P, 2, BANK])

        load = {n: sem(f"gla_{n}_in") for n in ("q", "k", "v", "z", "w", "b", "mask", "bm", "g", "go")}
        zeroed, wg_zero = sem("zeroed"), sem("wg_zero")
        reset_one, reset_set, q_scaled = sem("reset_one"), sem("reset_set"), sem("q_scaled")
        v_turned, v_copied = sem("v_turned"), sem("v_copied")
        logits, abs_done, exp_of_abs, log_done, min_done, gate_done, scanned = (
            sem("logits"), sem("abs_done"), sem("exp_of_abs"), sem("log_done"), sem("min_done"), sem("gate_done"), sem("scanned"))
        d_done, e_done, x_done, unit_done, copied = sem("d_done"), sem("e_done"), sem("x_done"), sem("unit_done"), sem("copied")
        qe_e, qe_done, ke_turned, ke_copied, dec_done = sem("qe_e"), sem("qe_done"), sem("ke_turned"), sem("ke_copied"), sem("dec_done")
        u_done, state = sem("u_done"), sem("state")
        o_done, o_copied, squared, mean_done, rms_done = sem("o_done"), sem("o_copied"), sem("squared"), sem("mean_done"), sem("rms_done")
        inv_done, silu_done, gate_ready, normed, gated, stored = (
            sem("inv_done"), sem("silu_done"), sem("gate_ready"), sem("normed"), sem("gated"), sem("stored"))
        block = ctx.enter_context(nc.Block())
        NL = len(LEVELS)
        UNITS0 = 4
        NPAIR = 4 * NL
        BORDER = [1, 0] + list(range(NCH - 1, 1, -1))
        ORDER = [list(range(NCH)), BORDER]

        def halves(ap, m):
            return ap.rearrange("p (n h m) -> p n h m", h=2, m=m)

        def min_steps(g):
            per = [4, 4, 1]
            return (g // 3) * (NCH - 1) + sum(per[:g % 3 + 1])

        proj = t["proj"]

        @block.sync
        def _(sp):
            sp.dma_start(z[:, :], proj[T_Z * P:T_Z * P + 2 * GATE_RANK, 0:T]).then_inc(load["z"], 16)
            sp.wait_ge(wg_zero, 1)
            for d in range(2):
                sp.dma_start(wg[d * GATE_RANK:(d + 1) * GATE_RANK, d, :], t["w_gate"][layer, d]).then_inc(load["w"], 16)
                sp.dma_start(bg[:, d, :], t["b_gate"][layer, d:d + 1, :].rearrange("a (i p) -> p (a i)", p=P)).then_inc(load["b"], 16)
            sp.dma_start(k[:, :, :], proj[T_GK * P:(T_GK + 2) * P, 0:T].rearrange("(i p) n -> p i n", p=P)).then_inc(load["k"], 16)
            sp.dma_start(q[:, :, :], proj[T_GQ * P:(T_GQ + 2) * P, 0:T].rearrange("(i p) n -> p i n", p=P)).then_inc(load["q"], 16)
            sp.dma_start(masks[:, :, :], t["gla_masks"]).then_inc(load["mask"], 16)
            sp.dma_start(vT[:, :, :], proj[T_GV * P:(T_GV + 2) * P, 0:T].rearrange("(i p) n -> p i n", p=P)).then_inc(load["v"], 16)
            sp.dma_start(block_mean[:, :], t["block_mean"]).then_inc(load["bm"], 16)
            for h in range(2):
                sp.dma_start(normg[h * 64:(h + 1) * 64, :], t["gla_norm_g"][layer].rearrange("(p a) -> p a", a=1)).then_inc(load["g"], 16)
            sp.wait_ge(v_turned, 6)
            sp.dma_start(vT[:, :, :], proj[T_GO * P:(T_GO + 2) * P, 0:T].rearrange("(i p) n -> p i n", p=P)).then_inc(load["go"], 16)
            for i in range(2):
                sp.wait_ge(gated, i + 1)
                sp.dma_start(t["mix"][i * P:(i + 1) * P, :], X[:, i, :]).then_inc(stored, 16)
            sp.wait_ge(stored, 32)

        @block.gpsimd
        def _(pool):
            pool.memset(wg[:, :, :], 0.0).then_inc(wg_zero, 1)
            pool.memset(eps[:, :], EPS).then_inc(zeroed, 1)
            pool.memset(A[:, :, :, :, :], 0.0).then_inc(zeroed, 1)
            pool.memset(S[:, :, :, :], 0.0).then_inc(zeroed, 1)
            pool.wait_ge(load["k"], 16)
            pool.wait_ge(q_scaled, 1)
            n = 0
            for i in range(2):
                for d in range(2):
                    for m in LEVELS:
                        pool.wait_ge(e_done, n + 1)
                        if n >= 2:
                            pool.wait_ge(unit_done, UNITS0 + 2 * (n - 1))
                        e, x = halves(Dc[:, n % 2, :], m), halves(X[:, n % 2, :], m)
                        kk, qq = halves(k[:, i, :], m), halves(q[:, i, :], m)
                        first, second = (kk, qq) if d == 0 else (qq, kk)
                        pool.tensor_tensor(x[:, :, 0, :], first[:, :, 0, :], e[:, :, 0, :], ALU.mult).then_inc(x_done, 1)
                        pool.tensor_tensor(x[:, :, 1, :], second[:, :, 1, :], e[:, :, 1, :], ALU.mult).then_inc(x_done, 1)
                        n += 1
            for j, (d, i) in enumerate(DI):
                pool.wait_ge(e_done, NPAIR + j + 1)
                pool.wait_ge(unit_done, UNITS0 + 2 * NPAIR)
                if j >= 2:
                    pool.wait_ge(ke_turned, j - 1)
                pool.tensor_tensor(X[:, j % 2, :], k[:, i, :], Dc[:, j % 2, :], ALU.mult).then_inc(x_done, 1)

        @block.tensor
        def _(pe):
            pe.wait_ge(load["z"], 16)
            pe.wait_ge(load["w"], 32)
            for n, (d, i) in enumerate(DI):
                if n >= 2:
                    pe.wait_ge(min_done, n - 1)
                    pe.wait_ge(abs_done, n - 1)
                for t0, tn in FLAT:
                    mm = pe.matmul(UNIT[:, n % 2, t0:t0 + tn], wg[:, d, i * P:(i + 1) * P], z[:, t0:t0 + tn], start=True, stop=True)
                mm.then_inc(logits, 1)
            pe.wait_ge(load["v"], 16)
            g = 0
            for i in range(2):
                for c0 in range(0, TILES, 4):
                    if g >= 2:
                        pe.wait_ge(v_copied, g - 1)
                    for c in range(c0, min(c0 + 4, TILES)):
                        mm = pe.transpose(TR[:, g % 2, (c - c0) * P:(c - c0 + 1) * P], vT[:, i, c * P:(c + 1) * P], ident[:, :])
                    mm.then_inc(v_turned, 1)
                    g += 1
            pe.wait_ge(q_scaled, 2)
            pe.wait_ge(min_done, 4)
            pe.wait_ge(abs_done, 4)
            for i in range(2):
                for h in range(2):
                    if i:
                        pe.wait_ge(copied, 2 * i + h - 1)
                    rows = slice(64 * h, 64 * h + 64)
                    for c in range(NCH):
                        cols = slice(c * CH, (c + 1) * CH)
                        mm = pe.matmul(UNIT[:, h, cols], k[rows, i, cols], Qe[rows, i, cols], start=True, stop=True)
                    mm.then_inc(unit_done, 1)
            with pe.Fori(0, NPAIR // 2) as j:
                for s in range(2):
                    pe.wait_ge(x_done, j * 4 + 2 * s + 2)
                    for h in range(2):
                        pe.wait_ge(copied, j * 4 + 2 * s + h + UNITS0 - 1)
                        rows = slice(64 * h, 64 * h + 64)
                        for c in range(NCH):
                            cols = slice(c * CH, (c + 1) * CH)
                            mm = pe.matmul(UNIT[:, h, cols], X[rows, s, cols], X[rows, s, cols], start=True, stop=True)
                        mm.then_inc(unit_done, 1)
            pe.wait_ge(v_copied, 6)
            pe.wait_ge(copied, UNITS0 + 2 * NPAIR)
            g = 0
            for j, (d, i) in enumerate(DI):
                pe.wait_ge(x_done, 2 * NPAIR + j + 1)
                if j >= 2:
                    pe.wait_ge(ke_copied, j - 1)
                for c in range(NCH):
                    mm = pe.transpose(UNIT[:, j % 2, c * P:(c + 1) * P], X[:, j % 2, c * P:(c + 1) * P], ident[:, :])
                mm.then_inc(ke_turned, 1)
                pe.wait_ge(ke_copied, j + 1)
                order = ORDER[d][:-1]
                for c0 in range(0, len(order), 4):
                    if g >= 2:
                        pe.wait_ge(state, 2 * min_steps(g - 2))
                    for a, c in enumerate(order[c0:c0 + 4]):
                        mm = pe.matmul(TR[:, g % 2, a * P:(a + 1) * P], KeT[:, j % 2, c, :], V[:, c, i * P:(i + 1) * P], start=True, stop=True)
                    mm.then_inc(u_done, 1)
                    g += 1
            pe.wait_ge(qe_done, 4)
            pe.wait_ge(state, 2 * 4 * (NCH - 1))
            pe.wait_ge(ke_copied, 4)
            for i in range(2):
                for c in range(NCH):
                    cols = slice(c * CH, (c + 1) * CH)
                    pe.matmul(UNIT[:, i, cols], S[:, i, c, :], Qe[:, i, cols], start=True, stop=False, skip_group_check=True)
                    pe.matmul(UNIT[:, i, cols], S[:, 2 + i, c, :], Qe[:, 2 + i, cols], start=False, stop=True, skip_group_check=True)
                    for h in range(2):
                        mm = pe.matmul(UNIT[64 * h:64 * h + 64, i, cols], V[:, c, i * P + 64 * h:i * P + 64 * h + 64], A[:, i, h, c, :],
                                       start=False, stop=True, skip_group_check=True)
                mm.then_inc(o_done, 1)
            pe.wait_ge(load["bm"], 16)
            for i in range(2):
                pe.wait_ge(squared, i + 1)
                pe.wait_ge(o_copied, i + 1)
                for t0, tn in FLAT:
                    mm = pe.matmul(UNIT[:, i, t0:t0 + tn], block_mean[:, :], Dc[:, i, t0:t0 + tn], start=True, stop=True)
                mm.then_inc(mean_done, 1)

        @block.scalar
        def _(act):
            act.wait_ge(load["b"], 32)
            for n, (d, i) in enumerate(DI):
                act.wait_ge(logits, n + 1)
                if n >= 2:
                    act.wait_ge(gate_done, n - 1)
                x = Dc[:, n % 2, :]
                act.activation(x, UNIT[:, n % 2, 0:T], ACT.Abs, bias=bg[:, d, i:i + 1]).then_inc(abs_done, 1)
                act.wait_ge(abs_done, n + 1)
                act.activation(x, x, ACT.Exp, scale=-1.0).then_inc(exp_of_abs, 1)
                act.wait_ge(exp_of_abs, n + 1)
                act.activation(x, x, ACT.Ln, bias=1.0).then_inc(log_done, 1)
            g = 0
            for i in range(2):
                for c0 in range(0, TILES, 4):
                    n = min(4, TILES - c0)
                    act.wait_ge(v_turned, g + 1)
                    act.copy(V[:, c0:c0 + n, i * P:(i + 1) * P], TR[:, g % 2, 0:n * P].rearrange("p (c f) -> p c f", f=P)).then_inc(v_copied, 1)
                    g += 1
            for n in range(NPAIR + 4):
                act.wait_ge(d_done, 2 * n + 2 if n < NPAIR else 2 * NPAIR + (n - NPAIR) + 1)
                act.activation(Dc[:, n % 2, :], Dc[:, n % 2, :], ACT.Exp, scale=1.0 / GATE_NORM).then_inc(e_done, 1)
            for j, (d, i) in enumerate(DI):
                end = B[:, j, :].rearrange("p (c n) -> p c n", n=CH)[:, :, CH - 1 if d == 0 else 0]
                act.activation(dec[:, j, :], end, ACT.Exp, scale=1.0 / GATE_NORM).then_inc(dec_done, 1)
            act.wait_ge(unit_done, UNITS0)
            for j in range(4):
                act.activation(Qe[:, j, :], B[:, j, :], ACT.Exp, scale=1.0 / GATE_NORM).then_inc(qe_e, 1)
                act.wait_ge(ke_turned, j + 1)
                if j >= 2:
                    act.wait_ge(u_done, 3 * (j - 1))
                act.copy(KeT[:, j % 2, :, :], UNIT[:, j % 2, 0:T].rearrange("p (c f) -> p c f", f=P)).then_inc(ke_copied, 1)
            act.wait_ge(load["go"], 16)
            act.activation(vT[:, :, :], vT[:, :, :], ACT.Silu).then_inc(silu_done, 1)
            act.wait_ge(zeroed, 3)
            for i in range(2):
                act.wait_ge(o_done, i + 1)
                act.copy(X[:, i, :], UNIT[:, i, 0:T]).then_inc(o_copied, 1)
                act.activation(Dc[:, i, :], UNIT[:, i, 0:T], ACT.Square).then_inc(squared, 1)
            for i in range(2):
                act.wait_ge(mean_done, i + 1)
                act.activation(Dc[:, i, :], UNIT[:, i, 0:T], ACT.Sqrt, bias=eps[:, 0:1]).then_inc(rms_done, 1)

        @block.vector
        def _(dve):
            dve.memset(reset[:, :], 1.0).then_inc(reset_one, 1)
            dve.wait_ge(reset_one, 1)
            dve.memset(reset[:, :].rearrange("p (c n) -> p c n", n=CH)[:, :, 0:1], 0.0).then_inc(reset_set, 1)
            dve.wait_ge(reset_set, 1)
            dve.wait_ge(load["b"], 32)
            for n, (d, i) in enumerate(DI):
                dve.wait_ge(abs_done, n + 1)
                dve.tensor_scalar(B[:, n, :], UNIT[:, n % 2, 0:T], bg[:, d, i:i + 1], 0.0, ALU.add, ALU.min).then_inc(min_done, 1)
                dve.wait_ge(min_done, n + 1)
                dve.wait_ge(log_done, n + 1)
                if n >= 2:
                    dve.wait_ge(scanned, n - 1)
                dve.tensor_tensor(X[:, n % 2, :], B[:, n, :], Dc[:, n % 2, :], ALU.subtract).then_inc(gate_done, 1)
                dve.wait_ge(gate_done, n + 1)
                step = 1 if d == 0 else -1
                dve.tensor_tensor_scan(B[:, n, ::step], reset[:, :], X[:, n % 2, ::step], 0.0, ALU.mult, ALU.add).then_inc(scanned, 1)
            dve.wait_ge(load["q"], 16)
            dve.tensor_scalar(q[:, :, :], q[:, :, :], 64 ** -0.5, None, ALU.mult).then_inc(q_scaled, 1)
            dve.wait_ge(q_scaled, 1)
            dve.tensor_scalar(Qe[:, 0:2, :], q[:, :, :], 2.0, None, ALU.mult).then_inc(q_scaled, 1)
            dve.wait_ge(scanned, 4)
            dve.wait_ge(load["mask"], 16)
            dve.wait_ge(zeroed, 3)

            def distances(n):
                i, d, m = n // (2 * NL), n // NL % 2, LEVELS[n % NL]
                b = halves(B[:, 2 * d + i, :], m)
                x = halves(Dc[:, n % 2, :], m)
                nb = T // (2 * m)
                mid = (b[:, :, 0, m - 1:m] if d == 0 else b[:, :, 1, 0:1]).to_broadcast([P, nb, m])
                if n >= 2:
                    dve.wait_ge(x_done, 2 * (n - 1))
                lo, hi = (0, 1) if d == 0 else (1, 0)
                dve.tensor_tensor(x[:, :, lo, :], mid, b[:, :, lo, :], ALU.subtract).then_inc(d_done, 1)
                dve.tensor_tensor(x[:, :, hi, :], b[:, :, hi, :], mid, ALU.subtract).then_inc(d_done, 1)

            def take(unit, i, h, mask):
                dve.wait_ge(unit_done, unit + 1)
                dve.copy_predicated(A[:, i, h, :, :], masks[:, mask:mask + 1, :].to_broadcast([P, NCH, CH]),
                                    UNIT[:, h, 0:T].rearrange("p (c n) -> p c n", n=CH)).then_inc(copied, 1)

            distances(0)
            distances(1)
            for i in range(2):
                for h in range(2):
                    if i or h:
                        dve.wait_ge(copied, 2 * i + h)
                    take(2 * i + h, i, h, 2 * NL)
            for n in range(NPAIR):
                if n + 2 < NPAIR:
                    distances(n + 2)
                for h in range(2):
                    dve.wait_ge(copied, UNITS0 + 2 * n + h)
                    take(UNITS0 + 2 * n + h, n // (2 * NL), h, n % (2 * NL))
            for j, (d, i) in enumerate(DI):
                dve.wait_ge(x_done, 2 * (NPAIR - 1) + 2 + max(0, j - 1))
                b = B[:, j, :].rearrange("p (c n) -> p c n", n=CH)
                end = (b[:, :, CH - 1:CH] if d == 0 else b[:, :, 0:1]).to_broadcast([P, NCH, CH])
                dve.tensor_tensor(Dc[:, j % 2, :].rearrange("p (c n) -> p c n", n=CH), end, b, ALU.subtract).then_inc(d_done, 1)
            dve.wait_ge(dec_done, 4)
            g, n = 0, 0
            for j, (d, i) in enumerate(DI):
                order = ORDER[d]
                for c0 in range(0, NCH - 1, 4):
                    dve.wait_ge(u_done, g + 1)
                    for a in range(min(4, NCH - 1 - c0)):
                        c, nxt = order[c0 + a], order[c0 + a + 1]
                        if n:
                            dve.wait_ge(state, n)
                        for h in range(2):
                            r = slice(64 * h, 64 * h + 64)
                            dve.scalar_tensor_tensor(S[r, j, nxt, r], S[r, j, c, r], dec[r, j, c:c + 1],
                                                     TR[r, g % 2, a * P + 64 * h:a * P + 64 * h + 64], ALU.mult, ALU.add).then_inc(state, 1)
                        n += 2
                    g += 1
            for j, (d, i) in enumerate(DI):
                dve.wait_ge(qe_e, j + 1)
                dve.tensor_tensor(Qe[:, j, :], Qe[:, j, :], q[:, i, :], ALU.mult).then_inc(qe_done, 1)
            dve.wait_ge(silu_done, 1)
            dve.wait_ge(load["g"], 32)
            dve.tensor_scalar(vT[:, :, :], vT[:, :, :], normg[:, 0:1], None, ALU.mult).then_inc(gate_ready, 1)
            for i in range(2):
                dve.wait_ge(rms_done, i + 1)
                dve.reciprocal(Dc[:, i, :], Dc[:, i, :]).then_inc(inv_done, 1)
                dve.wait_ge(inv_done, i + 1)
                dve.tensor_tensor(X[:, i, :], X[:, i, :], Dc[:, i, :], ALU.mult).then_inc(normed, 1)
                dve.wait_ge(normed, i + 1)
                dve.wait_ge(gate_ready, 1)
                dve.tensor_tensor(X[:, i, :], X[:, i, :], vT[:, i, :], ALU.mult).then_inc(gated, 1)


def sliding_window_attention(nc, t, res, layer, tiles):
    with nc.cleanup_on_exit(), ExitStack() as ctx:
        sb, ps, sem = allocators(nc, ctx, f"swa{layer}_")
        nm = f"swa{layer}_"
        ident = res["ident"]
        G = SWA_HEADS // 2
        WIN = 3 * P
        first_pair, pairs = tiles[0] // 2, len(tiles) // 2
        kctx = sb(nm + "kctx", [P, N_CTX])
        kwin = sb(nm + "kwin", [P, 2, WIN])
        qt = sb(nm + "q", [P, 2, G, P])
        bias = sb(nm + "bias", [P, 2, 2 * P])
        vT = sb(nm + "vT", [P, PAD_T])
        V = sb(nm + "V", [P, TILES + 1, P])
        sink = sb(nm + "sink", [P, SWA_HEADS])
        nsink = sb(nm + "nsink", [P, SWA_HEADS])
        mx = sb(nm + "mx", [P, 2])
        nm_ = sb(nm + "negmax", [P, 2])
        den = sb(nm + "den", [P, 2])
        es = sb(nm + "esink", [P, 2])
        rden = sb(nm + "rden", [P, 4])
        den2 = sb(nm + "den2", [P, 2])
        pr = sb(nm + "p", [P, 2, SWA_KEYS])
        pT = sb(nm + "pT", [P, 2, SWA_KEYS])
        o = sb(nm + "o", [P, 2, SWA_HEADS * SWA_DH])
        oT = sb(nm + "oT", [P, 2, G, P])
        SC = ps(nm + "scores", [P, 2, 2 * BANK])
        TR = ps(nm + "tr", [P, 2 * BANK])
        O = ps(nm + "o_acc", [P, 2, BANK])
        OT = TR[:, 0:BANK]
        const_in = sem("const_in")
        tile_in = [sem(f"tile_in{s}") for s in range(2)]
        nsink_done, v_turned, v_copied = sem("nsink_done"), sem("v_turned"), sem("v_copied")
        scores, masked, max_done, neg_done, exp_done, sink_done = (
            sem("scores"), sem("masked"), sem("max_done"), sem("neg_done"), sem("exp_done"), sem("sink_done"))
        den_done, rden_done, turned, copied, pv_done, o_done = (
            sem("den_done"), sem("rden_done"), sem("turned"), sem("copied"), sem("pv_done"), sem("o_done"))
        o_turned, o_copied = sem("o_turned"), sem("o_copied")
        stored = [sem(f"stored{s}") for s in range(2)]
        scale = SWA_DH ** -0.5
        H = SWA_HEADS
        block = ctx.enter_context(nc.Block())
        VG = [(0, 8), (8, 3)]

        def unit(i, s, h):
            return (i - first_pair) * 2 * H + s * H + h + 1

        def is_ctx(i):
            return isinstance(i, int) and i == 0

        @block.sync
        def _(sp):
            sp.dma_start(vT[:, :], t["proj"][T_SV * P:(T_SV + 1) * P, :]).then_inc(const_in, 16)
            sp.dma_start(kctx[:, :], t["proj"][T_SK * P:(T_SK + 1) * P, 0:N_CTX]).then_inc(const_in, 16)
            sp.dma_start(sink[:, :], t["swa_sink"][layer:layer + 1, :].to_broadcast([P, H])).then_inc(const_in, 16)

            def body(i, first):
                for s in range(2):
                    if not first:
                        sp.wait_ge(scores, unit(i, s, H - 1) - 2 * H)
                        sp.wait_ge(max_done, unit(i, s, H - 1) - 2 * H)
                    at = i * 2 * P + s * P
                    sp.dma_start(qt[:, s, :, :], t["proj"][T_SQ * P:(T_SQ + G) * P, bass.ds(at, P)].rearrange("(g p) n -> p g n", p=P)).then_inc(tile_in[s], 16)
                    sp.dma_start(kwin[:, s, :], t["proj"][T_SK * P:(T_SK + 1) * P, bass.ds(0 if is_ctx(i) else at - P, WIN)]).then_inc(tile_in[s], 16)
                    sp.dma_start(bias[:, s, :], t["swa_bias"][bass.ds(0 if is_ctx(i) else i * 2 * P + (s * P - N_CTX), P), :]).then_inc(tile_in[s], 16)
            peeled(sp, first_pair, first_pair + pairs, body)

        @block.tensor
        def _(pe):
            pe.wait_ge(const_in, 48)
            for g, (a, n) in enumerate(VG):
                if g:
                    pe.wait_ge(v_copied, g)
                for c in range(n):
                    mm = pe.transpose(TR[:, c * P:(c + 1) * P], vT[:, (a + c) * P:(a + c + 1) * P], ident[:, :])
                mm.then_inc(v_turned, 1)
            pe.wait_ge(v_copied, 2)

            def body(i, first):
                kt = 2 if is_ctx(i) else 5
                for s in range(2):
                    pe.wait_ge(tile_in[s], (i - first_pair) * 48 + 48)
                    for step in range(H + 2):
                        if step < H:
                            h = step
                            rows = slice(64 * (h // G), 64 * (h // G) + 64)
                            qh = qt[rows, s, h % G, :]
                            if not (first and s == 0 and h < 2):
                                pe.wait_ge(exp_done, unit(i, s, h) - 2)
                            mm = pe.matmul(SC[:, h % 2, 0:N_CTX], qh, kctx[rows, :], start=True, stop=True)
                            if kt == 5:
                                pe.matmul(SC[:, h % 2, N_CTX:N_CTX + 2 * P], qh, kwin[rows, s, 0:2 * P], start=True, stop=True)
                                mm = pe.matmul(SC[:, h % 2, BANK:BANK + P], qh, kwin[rows, s, 2 * P:WIN], start=True, stop=True)
                            mm.then_inc(scores, 1)
                        if 1 <= step < H + 1:
                            h = step - 1
                            pe.wait_ge(exp_done, unit(i, s, h))
                            if not (first and s == 0 and h == 0):
                                pe.wait_ge(copied, unit(i, s, h) - 1)
                            if not (first and s == 0) and h == 0:
                                pe.wait_ge(o_copied, (i - first_pair) * 2 + s)
                            for c in range(kt):
                                mm = pe.transpose(TR[:, c * P:(c + 1) * P], pr[:, h % 2, c * P:(c + 1) * P], ident[:, :])
                            mm.then_inc(turned, 1)
                        if step >= 2:
                            h = step - 2
                            pe.wait_ge(copied, unit(i, s, h))
                            if not (first and s == 0 and h < 2):
                                pe.wait_ge(o_done, unit(i, s, h) - 2)
                            vcols = slice(64 * (h // G), 64 * (h // G) + 64)
                            for c in range(kt):
                                if c < 2:
                                    v = V[:, c, vcols]
                                else:
                                    v = V[:, bass.ds(i * 2 + (s - 1 + c - 2), 1), vcols].rearrange("p a b -> p (a b)")
                                mm = pe.matmul(O[:, h % 2, 0:64], pT[:, h % 2, c * P:(c + 1) * P], v, start=(c == 0), stop=(c == kt - 1))
                            mm.then_inc(pv_done, 1)
                    pe.wait_ge(o_done, unit(i, s, H - 1))
                    for g in range(G):
                        mm = pe.transpose(OT[:, g * P:(g + 1) * P], o[:, s, g * P:(g + 1) * P], ident[:, :])
                    mm.then_inc(o_turned, 1)
            peeled(pe, first_pair, first_pair + pairs, body)

        @block.scalar
        def _(act):
            for g, (a, n) in enumerate(VG):
                act.wait_ge(v_turned, g + 1)
                act.copy(V[:, a:a + n, :], TR[:, 0:n * P].rearrange("p (c f) -> p c f", f=P)).then_inc(v_copied, 1)
            act.wait_ge(const_in, 48)

            def body(i, first):
                keys = N_CTX if is_ctx(i) else SWA_KEYS
                for s in range(2):
                    for step in range(H + 1):
                        if step < H:
                            h = step
                            u = unit(i, s, h)
                            act.wait_ge(neg_done, u)
                            if not (first and s == 0 and h < 2):
                                act.wait_ge(turned, u - 2)
                                act.wait_ge(den_done, u - 2)
                            act.activation(pr[:, h % 2, 0:keys], SC[:, h % 2, 0:keys], ACT.Exp, bias=nm_[:, h % 2:h % 2 + 1],
                                           scale=scale, accum_out=den[:, h % 2:h % 2 + 1]).then_inc(exp_done, 1)
                            act.activation(es[:, h % 2:h % 2 + 1], sink[:, h:h + 1], ACT.Exp, bias=nm_[:, h % 2:h % 2 + 1]).then_inc(sink_done, 1)
                        if step >= 1:
                            h = step - 1
                            u = unit(i, s, h)
                            act.wait_ge(turned, u)
                            if not (first and s == 0 and h < 2):
                                act.wait_ge(pv_done, u - 2)
                            act.copy(pT[:, h % 2, 0:keys], TR[:, 0:keys]).then_inc(copied, 1)
                    n = (i - first_pair) * 2 + s + 1
                    act.wait_ge(o_turned, n)
                    if not first:
                        act.wait_ge(stored[s], (i - first_pair) * 16)
                    act.copy(oT[:, s, :, :], OT[:, :].rearrange("p (g n) -> p g n", g=G)).then_inc(o_copied, 1)
                    act.wait_ge(o_copied, n)
                    act.dma_start(t["mix"][2 * 2 * P:D, bass.ds(i * 2 * P + s * P, P)].rearrange("(g p) n -> p g n", p=P), oT[:, s, :, :]).then_inc(stored[s], 16)
            peeled(act, first_pair, first_pair + pairs, body)
            for s in range(2):
                act.wait_ge(stored[s], 16 * pairs)

        @block.vector
        def _(dve):
            dve.wait_ge(const_in, 48)
            dve.tensor_scalar(nsink[:, :], sink[:, :], -1.0, None, ALU.mult).then_inc(nsink_done, 1)
            dve.wait_ge(nsink_done, 1)

            def body(i, first):
                for s in range(2):
                    dve.wait_ge(tile_in[s], (i - first_pair) * 48 + 48)
                    for step in range(H + 2):
                        if step < H:
                            h = step
                            u = unit(i, s, h)
                            b = h % 2
                            dve.wait_ge(scores, u)
                            keys = N_CTX
                            if not is_ctx(i):
                                keys = SWA_KEYS
                                for a, c in ((0, N_CTX), (P, BANK)):
                                    dve.tensor_tensor(SC[:, b, c:c + P], SC[:, b, c:c + P], bias[:, s, a:a + P], ALU.add).then_inc(masked, 1)
                                dve.wait_ge(masked, (u if first_pair else u - 2 * H) * 2)
                            dve.reduce_max(mx[:, b:b + 1], SC[:, b, 0:keys], AX.X).then_inc(max_done, 1)
                            dve.wait_ge(max_done, u)
                            dve.scalar_tensor_tensor(nm_[:, b:b + 1], mx[:, b:b + 1], -scale, nsink[:, h:h + 1], ALU.mult, ALU.min).then_inc(neg_done, 1)
                        if 1 <= step < H + 1:
                            h = step - 1
                            u = unit(i, s, h)
                            b = h % 2
                            dve.wait_ge(sink_done, u)
                            dve.tensor_tensor(den2[:, b:b + 1], den[:, b:b + 1], es[:, b:b + 1], ALU.add).then_inc(den_done, 1)
                            dve.wait_ge(den_done, u)
                            dve.reciprocal(rden[:, h % 4:h % 4 + 1], den2[:, b:b + 1]).then_inc(rden_done, 1)
                        if step >= 2:
                            h = step - 2
                            u = unit(i, s, h)
                            dve.wait_ge(pv_done, u)
                            dve.wait_ge(rden_done, u)
                            if not first:
                                dve.wait_ge(o_turned, (i - first_pair) * 2 + s - 1)
                            dve.tensor_scalar(o[:, s, 64 * h:64 * h + 64], O[:, h % 2, 0:64], rden[:, h % 4:h % 4 + 1], None, ALU.mult).then_inc(o_done, 1)
            peeled(dve, first_pair, first_pair + pairs, body)


def differential_attention(nc, t, res, layer, tiles):
    with nc.cleanup_on_exit(), ExitStack() as ctx:
        sb, ps, sem = allocators(nc, ctx, f"diff{layer}_")
        nm = f"diff{layer}_"
        ident = res["ident"]
        H = DIFF_HEADS
        lam_init = 0.8 - 0.6 * math.exp(-0.3 * layer)
        scale = DIFF_DH ** -0.5
        first_pair, pairs = tiles[0] // 2, len(tiles) // 2
        KEYCH = [(0, 512), (512, 512), (1024, 256)]
        kT = sb(nm + "k", [P, 2, T])
        qt = sb(nm + "q", [P, 2, 2, P])
        vT = sb(nm + "vT", [P, 2, T])
        V = sb(nm + "V", [P, TILES, 2 * P])
        lamv = sb(nm + "lamv", [P, 4, DIFF_DH])
        lprod = sb(nm + "lprod", [P, 2, DIFF_DH])
        lsum = sb(nm + "lsum", [P, 2])
        lexp = sb(nm + "lexp", [P, 2])
        ldiff = sb(nm + "ldiff", [P, 1])
        nlam = sb(nm + "nlam", [P, 1])
        g1 = sb(nm + "g", [P, 64])
        eps = sb(nm + "eps", [P, 1])
        mx = sb(nm + "mx", [P, 2])
        ng = sb(nm + "negmax", [P, 2])
        den = sb(nm + "den", [P, 2])
        rden = sb(nm + "rden", [P, 2])
        r1 = sb(nm + "r1", [P, 1])
        E = sb(nm + "e", [P, 2, T])
        W = sb(nm + "w", [P, 2, T])
        WT = sb(nm + "wT", [P, 2, T])
        o = sb(nm + "o", [P, 2, H, 64])
        sq = sb(nm + "sq", [P, H, 64])
        ss = sb(nm + "ss", [P, H])
        sd = sb(nm + "sd", [P, H])
        ri = sb(nm + "ri", [P, H])
        oT = sb(nm + "oT", [P, 2, 2, P])
        SC = ps(nm + "scores", [P, 2, 3 * BANK])
        TR = ps(nm + "tr", [P, 2, BANK])
        O = TR[:, 1, 0:64]
        const_in, eps_set = sem("const_in"), sem("eps_set")
        q_in = [sem(f"q_in{s}") for s in range(2)]
        lam = sem("lam")
        lam_exp = sem("lam_exp")
        v_turned, v_copied = sem("v_turned"), sem("v_copied")
        scores, max_done, neg_done, exp_done, rden_done, r1_done, w0_done, w_done = (
            sem("scores"), sem("max_done"), sem("neg_done"), sem("exp_done"), sem("rden_done"), sem("r1_done"), sem("w0_done"), sem("w_done"))
        turned, copied, pv_done, o_done = sem("turned"), sem("copied"), sem("pv_done"), sem("o_done")
        sq_done, ss_done, sd_done, ri_done, on_done, og_done = (
            sem("sq_done"), sem("ss_done"), sem("sd_done"), sem("ri_done"), sem("on_done"), sem("og_done"))
        o_turned, o_copied = sem("o_turned"), sem("o_copied")
        stored = [sem(f"stored{s}") for s in range(2)]
        block = ctx.enter_context(nc.Block())
        VG = [(i, a, min(4, TILES - a)) for i in range(2) for a in range(0, TILES, 4)]

        def unit(i, s, h):
            return (i - first_pair) * 2 * H + s * H + h + 1

        def is_ctx(i):
            return isinstance(i, int) and i == 0

        def groups(i):
            kt = CTX_TILES if is_ctx(i) else TILES
            return [(a, min(4, kt - a)) for a in range(0, kt, 4)]

        def turned_before(i, s, h):
            if first_pair:
                return (i - first_pair) * 2 * (3 * H + 1) + s * (3 * H + 1) + 3 * h
            if is_ctx(i):
                return s * (H + 1) + h
            return 2 * (H + 1) + (i - 1) * 2 * (3 * H + 1) + s * (3 * H + 1) + 3 * h

        @block.sync
        def _(sp):
            sp.dma_start(vT[:, :, :], t["proj"][T_DV * P:(T_DV + 2) * P, 0:T].rearrange("(i p) n -> p i n", p=P)).then_inc(const_in, 16)
            sp.dma_start(kT[:, :, :], t["proj"][T_DK * P:(T_DK + 2) * P, 0:T].rearrange("(i p) n -> p i n", p=P)).then_inc(const_in, 16)
            sp.dma_start(lamv[:, :, :].rearrange("p a b -> p (a b)"), t["diff_lambda"][layer:layer + 1, :, :].rearrange("l a b -> l (a b)").to_broadcast([P, 4 * DIFF_DH])).then_inc(const_in, 16)
            sp.dma_start(g1[:, :], t["diff_norm_g"][layer:layer + 1, :].to_broadcast([P, 64])).then_inc(const_in, 16)

            def body(i, first):
                for s in range(2):
                    if not first:
                        sp.wait_ge(scores, 2 * (unit(i, s, H - 1) - 2 * H))
                    sp.dma_start(qt[:, s, :, :], t["proj"][T_DQ * P:(T_DQ + 2) * P, bass.ds(i * 2 * P + s * P, P)].rearrange("(g p) n -> p g n", p=P)).then_inc(q_in[s], 16)
            peeled(sp, first_pair, first_pair + pairs, body)

        @block.tensor
        def _(pe):
            pe.wait_ge(const_in, 64)
            for g, (i, a, n) in enumerate(VG):
                if g >= 2:
                    pe.wait_ge(v_copied, g - 1)
                for c in range(n):
                    mm = pe.transpose(TR[:, g % 2, c * P:(c + 1) * P], vT[:, i, (a + c) * P:(a + c + 1) * P], ident[:, :])
                mm.then_inc(v_turned, 1)
            pe.wait_ge(v_copied, len(VG))

            def body(i, first):
                kt = CTX_TILES if is_ctx(i) else TILES
                for s in range(2):
                    pe.wait_ge(q_in[s], (i - first_pair) * 16 + 16)
                    for step in range(H + 2):
                        if step < H:
                            h = step
                            for c in range(2):
                                r0 = 64 * (h % 2) + 32 * c
                                rows = slice(r0, r0 + 32)
                                if not (first and s == 0 and h == 0):
                                    pe.wait_ge(exp_done, 2 * (unit(i, s, h) - 1) + c - 1)
                                for a, n in KEYCH[:1 if kt == 2 else 3]:
                                    n = min(n, kt * P)
                                    mm = pe.matmul(SC[:, c, a:a + n], qt[rows, s, h // 2, :], kT[rows, h // 2, a:a + n], start=True, stop=True)
                                mm.then_inc(scores, 1)
                        if 1 <= step < H + 1:
                            h = step - 1
                            pe.wait_ge(w_done, unit(i, s, h))
                            for g, (a, n) in enumerate(groups(i)):
                                b = g % 2
                                if g == 0 and not (first and s == 0 and h == 0):
                                    pe.wait_ge(copied, turned_before(i, s, h))
                                if g == 1 and h >= 2:
                                    pe.wait_ge(o_done, unit(i, s, h) - 2)
                                if g == 2:
                                    pe.wait_ge(copied, turned_before(i, s, h) + 1)
                                for c in range(n):
                                    mm = pe.transpose(TR[:, b, c * P:(c + 1) * P], W[:, h % 2, (a + c) * P:(a + c + 1) * P], ident[:, :])
                                mm.then_inc(turned, 1)
                        if step >= 2:
                            h = step - 2
                            pe.wait_ge(copied, turned_before(i, s, h) + len(groups(i)))
                            if h + 1 < H and kt > 4:
                                pe.wait_ge(copied, turned_before(i, s, h + 1) + 2)
                            if h:
                                pe.wait_ge(o_done, unit(i, s, h) - 1)
                            for c in range(kt):
                                mm = pe.matmul(O, WT[:, h % 2, c * P:(c + 1) * P], V[:, c, 64 * h:64 * h + 64],
                                               start=(c == 0), stop=(c == kt - 1))
                            mm.then_inc(pv_done, 1)
                    pe.wait_ge(og_done, (i - first_pair) * 2 + s + 1)
                    for g in range(2):
                        mm = pe.transpose(TR[:, 0, g * P:(g + 1) * P], o[:, s, 2 * g:2 * g + 2, :].rearrange("p a b -> p (a b)"), ident[:, :])
                    mm.then_inc(turned, 1)
            peeled(pe, first_pair, first_pair + pairs, body)

        @block.scalar
        def _(act):
            for g, (i, a, n) in enumerate(VG):
                act.wait_ge(v_turned, g + 1)
                act.copy(V[:, a:a + n, i * P:(i + 1) * P], TR[:, g % 2, 0:n * P].rearrange("p (c f) -> p c f", f=P)).then_inc(v_copied, 1)
            act.wait_ge(lam, 4)
            act.activation(lexp[:, :], lsum[:, :], ACT.Exp).then_inc(lam_exp, 1)
            act.wait_ge(eps_set, 1)

            def body(i, first):
                kt = CTX_TILES if is_ctx(i) else TILES
                keys = kt * P
                for s in range(2):
                    for step in range(H + 1):
                        if step < H:
                            h = step
                            u = unit(i, s, h)
                            for c in range(2):
                                act.wait_ge(neg_done, 2 * (u - 1) + c + 1)
                                if not (first and s == 0 and h == 0):
                                    act.wait_ge(w_done, u - 1)
                                act.activation(E[:, c, 0:keys], SC[:, c, 0:keys], ACT.Exp, bias=ng[:, c:c + 1], scale=scale,
                                               accum_out=den[:, c:c + 1]).then_inc(exp_done, 1)
                            act.wait_ge(rden_done, u)
                            if not (first and s == 0 and h < 2):
                                act.wait_ge(turned, turned_before(i, s, h) - (turned_gap(i, s, h)))
                            act.activation(W[:, h % 2, 0:keys], E[:, 0, 0:keys], ACT.Copy, scale=rden[:, 0:1]).then_inc(w0_done, 1)
                        if step >= 1:
                            h = step - 1
                            u = unit(i, s, h)
                            for g, (a, n) in enumerate(groups(i)):
                                act.wait_ge(turned, turned_before(i, s, h) + g + 1)
                                if g == 0 and not (first and s == 0 and h < 2):
                                    act.wait_ge(pv_done, u - 2)
                                act.copy(WT[:, h % 2, a * P:(a + n) * P], TR[:, g % 2, 0:n * P]).then_inc(copied, 1)
                    n = (i - first_pair) * 2 + s + 1
                    act.wait_ge(ss_done, n)
                    act.activation(sd[:, :], ss[:, :], ACT.Sqrt, bias=eps[:, 0:1], scale=1.0 / 64).then_inc(sd_done, 1)
                    done = turned_before(i, s, H)
                    act.wait_ge(turned, done + 1)
                    if not first:
                        act.wait_ge(stored[s], (i - first_pair) * 16)
                    act.copy(oT[:, s, :, :], TR[:, 0, 0:2 * P].rearrange("p (g n) -> p g n", g=2)).then_inc(copied, 1)
                    act.wait_ge(copied, done + 1)
                    act.dma_start(t["mix"][2 * P:4 * P, bass.ds(i * 2 * P + s * P, P)].rearrange("(g p) n -> p g n", p=P), oT[:, s, :, :]).then_inc(stored[s], 16)

            def turned_gap(i, s, h):
                n = len(groups(i))
                if h >= 2:
                    return n
                prev = n if (s == 1 or not is_ctx(i)) else n
                return 1 if h == 1 else 1 + prev
            peeled(act, first_pair, first_pair + pairs, body)
            for s in range(2):
                act.wait_ge(stored[s], 16 * pairs)

        @block.gpsimd
        def _(pool):
            pool.memset(eps[:, :], EPS).then_inc(eps_set, 1)

        @block.vector
        def _(dve):
            dve.wait_ge(const_in, 64)
            for a in range(2):
                dve.tensor_tensor(lprod[:, a, :], lamv[:, 2 * a, :], lamv[:, 2 * a + 1, :], ALU.mult).then_inc(lam, 1)
            dve.tensor_scalar(g1[:, :], g1[:, :], 1.0 - lam_init, None, ALU.mult).then_inc(lam, 1)
            dve.wait_ge(lam, 3)
            dve.reduce_sum(lsum[:, :], lprod[:, :, :], AX.X).then_inc(lam, 1)
            dve.wait_ge(lam_exp, 1)
            dve.tensor_tensor(ldiff[:, :], lexp[:, 1:2], lexp[:, 0:1], ALU.subtract).then_inc(lam, 1)
            dve.wait_ge(lam, 5)
            dve.tensor_scalar(nlam[:, :], ldiff[:, :], -lam_init, None, ALU.add).then_inc(lam, 1)
            dve.wait_ge(lam, 6)

            def body(i, first):
                keys = (CTX_TILES if is_ctx(i) else TILES) * P
                for s in range(2):
                    for step in range(H + 2):
                        if step < H:
                            h = step
                            u = unit(i, s, h)
                            for c in range(2):
                                n = 2 * (u - 1) + c + 1
                                dve.wait_ge(scores, n)
                                dve.reduce_max(mx[:, c:c + 1], SC[:, c, 0:keys], AX.X).then_inc(max_done, 1)
                                dve.wait_ge(max_done, n)
                                dve.tensor_scalar(ng[:, c:c + 1], mx[:, c:c + 1], -scale, None, ALU.mult).then_inc(neg_done, 1)
                            dve.wait_ge(exp_done, 2 * u)
                            dve.reciprocal(rden[:, :], den[:, :]).then_inc(rden_done, 1)
                            dve.wait_ge(rden_done, u)
                            dve.tensor_scalar(r1[:, :], rden[:, 1:2], nlam[:, 0:1], None, ALU.mult).then_inc(r1_done, 1)
                            dve.wait_ge(r1_done, u)
                            dve.wait_ge(w0_done, u)
                            dve.scalar_tensor_tensor(W[:, h % 2, 0:keys], E[:, 1, 0:keys], r1[:, 0:1], W[:, h % 2, 0:keys], ALU.mult, ALU.add).then_inc(w_done, 1)
                        if step >= 2:
                            h = step - 2
                            dve.wait_ge(pv_done, unit(i, s, h))
                            if not first:
                                dve.wait_ge(turned, turned_before(i, s, 0))
                            dve.tensor_copy(o[:, s, h, :], O).then_inc(o_done, 1)
                    n = (i - first_pair) * 2 + s + 1
                    dve.wait_ge(o_done, unit(i, s, H - 1))
                    dve.tensor_tensor(sq[:, :, :], o[:, s, :, :], o[:, s, :, :], ALU.mult).then_inc(sq_done, 1)
                    dve.wait_ge(sq_done, n)
                    dve.reduce_sum(ss[:, :], sq[:, :, :], AX.X).then_inc(ss_done, 1)
                    dve.wait_ge(sd_done, n)
                    dve.reciprocal(ri[:, :], sd[:, :]).then_inc(ri_done, 1)
                    dve.wait_ge(ri_done, n)
                    dve.tensor_tensor(o[:, s, :, :], o[:, s, :, :], ri[:, :].rearrange("p (h a) -> p h a", a=1).to_broadcast([P, H, 64]), ALU.mult).then_inc(on_done, 1)
                    dve.wait_ge(on_done, n)
                    dve.tensor_tensor(o[:, s, :, :], o[:, s, :, :], g1[:, :].rearrange("p (a n) -> p a n", a=1).to_broadcast([P, H, 64]), ALU.mult).then_inc(og_done, 1)
            peeled(dve, first_pair, first_pair + pairs, body)


def swiglu(nc, t, res, layer, chunks):
    with nc.cleanup_on_exit(), ExitStack() as ctx:
        sb, ps, sem = allocators(nc, ctx, f"ffn{layer}_")
        nm = f"ffn{layer}_"
        uhi, ulo, Y = res["uhi"], res["ulo"], res["y"]
        NC = len(chunks)
        order = [tt for t0, tn in chunks for tt in range(t0 // P, (t0 + tn) // P)]
        chunk_of = {tt: c for c, (t0, tn) in enumerate(chunks) for tt in range(t0 // P, (t0 + tn) // P)}
        NY = 2 * len(order)
        raw = sb(nm + "raw", [P, 3, D])
        whi = sb(nm + "whi", [P, 3, D], F32R)
        wlo = sb(nm + "wlo", [P, 3, D], F32R)
        sg = sb(nm + "silu", [P, NC, BANK])
        hf = sb(nm + "hid", [P, NC, BANK])
        hhi = sb(nm + "hhi", [P, 2, T], F32R)
        hlo = sb(nm + "hlo", [P, 2, T], F32R)
        GT = ps(nm + "gate", [P, 3, BANK])
        UP = ps(nm + "up", [P, 3, BANK])
        ACC = ps(nm + "acc", [P, 2, BANK])
        raw_in = [sem(f"raw_in{s}") for s in range(3)]
        passed = sem("passed")
        w_hi, w_ready = sem("w_hi"), sem("w_ready")
        gate_done, up_done, silu_done, mul_done = sem("gate_done"), sem("up_done"), sem("silu_done"), sem("mul_done")
        hid_hi, hid_ready, y_done, y_added, y_zero = sem("hid_hi"), sem("hid_ready"), sem("y_done"), sem("y_added"), sem("y_zero")
        block = ctx.enter_context(nc.Block())
        G = FFN_GROUPS

        def grouped(eng, body):
            body(0, True, False)
            with eng.Fori(1, G - 1) as g:
                body(g, False, False)
            body(G - 1, False, True)

        @block.sync
        def _(sp):
            def body(g, first, last):
                for j in range(6):
                    if not (first and j < 3):
                        sp.wait_ge(w_ready, g * 6 + j - 2)
                    sp.dma_start(raw[:, j % 3, :], t["w_ffn"][layer][bass.ds(g * 6 * P + j * P, P), :]).then_inc(raw_in[j % 3], 16)
            grouped(sp, body)

        def release(eng, g, j):
            if j == 0:
                eng.wait_ge(up_done, g * 2 * NC)
            elif j in (1, 2):
                eng.wait_ge(y_done, g * NY)
            elif j == 3:
                eng.wait_ge(gate_done, g * 2 * NC + NC)
            elif j == 4:
                eng.wait_ge(up_done, g * 2 * NC + NC)
            else:
                eng.wait_ge(gate_done, g * 2 * NC + 2 * NC)

        @block.scalar
        def _(act):
            def split(g, j, reused=True):
                if reused:
                    release(act, g, j)
                act.wait_ge(raw_in[j % 3], g * 32 + (j // 3) * 16 + 16)
                act.copy(whi[:, j % 3, :], raw[:, j % 3, :]).then_inc(w_hi, 1)

            def silu(g, f, first):
                for c, (t0, tn) in enumerate(chunks):
                    n = g * 2 * NC + f * NC + c
                    act.wait_ge(gate_done, n + 1)
                    if not (first and f == 0):
                        act.wait_ge(mul_done, n + 1 - NC)
                    act.activation(sg[:, c, 0:tn], GT[:, c, 0:tn], ACT.Silu).then_inc(silu_done, 1)

            def body(g, first, last):
                silu(g, 0, first)
                split(g, 3)
                split(g, 4)
                silu(g, 1, first)
                split(g, 5)
                if not last:
                    for j in range(3):
                        split(g + 1, j)
            for j in range(3):
                split(0, j, False)
            grouped(act, body)

        @block.gpsimd
        def _(pool):
            pool.memset(Y[:, :, :], 0.0).then_inc(y_zero, 1)

            def split(g, j):
                pool.wait_ge(w_hi, g * 6 + j + 1)
                pool.tensor_tensor(wlo[:, j % 3, :], raw[:, j % 3, :], whi[:, j % 3, :].bitcast(F32), ALU.subtract).then_inc(w_ready, 1)

            def hidden(g, f):
                for c, (t0, tn) in enumerate(chunks):
                    n = g * 2 * NC + f * NC + c + 1
                    wait_apart(pool, mul_done, n, passed)
                    pool.tensor_copy(hhi[:, f, t0:t0 + tn], hf[:, c, 0:tn]).then_inc(hid_hi, 1)
                    pool.wait_ge(hid_hi, n)
                    pool.tensor_tensor(hlo[:, f, t0:t0 + tn], hf[:, c, 0:tn], hhi[:, f, t0:t0 + tn].bitcast(F32), ALU.subtract).then_inc(hid_ready, 1)

            def body(g, first, last):
                split(g, 3)
                hidden(g, 0)
                split(g, 4)
                split(g, 5)
                hidden(g, 1)
                if not last:
                    for j in range(3):
                        split(g + 1, j)
            for j in range(3):
                split(0, j)
            grouped(pool, body)

        @block.tensor
        def _(pe):
            def body(g, first, last):
                for f in range(2):
                    for which, (bank, done, freed) in enumerate(((GT, gate_done, silu_done), (UP, up_done, mul_done))):
                        j = 2 * f + which
                        w = [x[:, j % 3, :].rearrange("p (k n) -> p k n", k=KT) for x in (whi, wlo)]
                        pe.wait_ge(w_ready, g * 6 + j + 1)
                        for c, (t0, tn) in enumerate(chunks):
                            if not (first and f == 0):
                                pe.wait_ge(freed, g * 2 * NC + f * NC + c + 1 - NC)
                            for k in range(KT):
                                mm = product(pe, bank[:, c, 0:tn], w[0][:, k, :], w[1][:, k, :],
                                             uhi[:, k, t0:t0 + tn], ulo[:, k, t0:t0 + tn], k == 0, k == KT - 1)
                            mm.then_inc(done, 1)
                pe.wait_ge(w_ready, g * 6 + 6)
                for n, tt in enumerate(order):
                    pe.wait_ge(hid_ready, g * 2 * NC + NC + chunk_of[tt] + 1)
                    for half in range(2):
                        if not (first and n == 0):
                            pe.wait_ge(y_added, g * NY + 2 * n + half - 1)
                        cols, rows = slice(half * BANK, (half + 1) * BANK), slice(tt * P, (tt + 1) * P)
                        for f in range(2):
                            s = (4 + f) % 3
                            mm = product(pe, ACC[:, half, :], hhi[:, f, rows], hlo[:, f, rows],
                                         whi[:, s, cols], wlo[:, s, cols], f == 0, f == 1)
                        mm.then_inc(y_done, 1)
            grouped(pe, body)

        @block.vector
        def _(dve):
            dve.wait_ge(y_zero, 1)

            def body(g, first, last):
                for f in range(2):
                    for c, (t0, tn) in enumerate(chunks):
                        n = g * 2 * NC + f * NC + c + 1
                        dve.wait_ge(silu_done, n)
                        dve.wait_ge(up_done, n)
                        if not (first and f == 0):
                            dve.wait_ge(hid_ready, n - NC)
                        dve.tensor_tensor(hf[:, c, 0:tn], UP[:, c, 0:tn], sg[:, c, 0:tn], ALU.mult).then_inc(mul_done, 1)
                for n, tt in enumerate(order):
                    for half in range(2):
                        cols = slice(half * BANK, (half + 1) * BANK)
                        dve.wait_ge(y_done, g * NY + 2 * n + half + 1)
                        dve.tensor_tensor(Y[:, tt, cols], ACC[:, half, :], Y[:, tt, cols], ALU.add).then_inc(y_added, 1)
            grouped(dve, body)


def build(nc, t):
    with ExitStack() as outer:
        outer.enter_context(nc.allow_non_contiguous_dma(reason="columns of modulation and gate biases: a few KB"))
        ident = outer.enter_context(nc.sbuf_tensor("ident", [P, P], F32))
        res = {"ident": ident}
        with nc.cleanup_on_exit(), ExitStack() as ctx:
            ident_in = nc.alloc_semaphore("ident_in")
            block = ctx.enter_context(nc.Block())

            @block.sync
            def _(sp):
                sp.dma_start(ident[:, :], t["ident"]).then_inc(ident_in, 16)
                sp.wait_ge(ident_in, 16)

        def operand(ctx, name):
            res["uhi"] = ctx.enter_context(nc.sbuf_tensor(name + "_uhi", [P, KT, T], F32R))
            res["ulo"] = ctx.enter_context(nc.sbuf_tensor(name + "_ulo", [P, KT, T], F32R))

        everything = list(range(TILES))
        modulation(nc, t)
        for layer in range(LAYERS):
            last = layer == LAYERS - 1
            tiles = everything[CTX_TILES:] if last else everything
            if layer == 0:
                with ExitStack() as ctx:
                    operand(ctx, "first")
                    norm_tiles(nc, t, res, "input", layer, everything, False)
                    input_projection(nc, t, res, layer)
            gated_linear_attention(nc, t, res, layer)
            differential_attention(nc, t, res, layer, tiles)
            sliding_window_attention(nc, t, res, layer, tiles)
            with ExitStack() as ctx:
                operand(ctx, f"second{layer}")
                norm_tiles(nc, t, res, "attention", layer, tiles, False)
                with ExitStack() as inner:
                    res["y"] = inner.enter_context(nc.sbuf_tensor(f"y{layer}", [P, TILES, D], F32))
                    swiglu(nc, t, res, layer, LAT_CHUNKS if last else CHUNKS)
                    norm_tiles(nc, t, res, "ffn", layer, tiles, last)
                if not last:
                    input_projection(nc, t, res, layer + 1)


def constants():
    import numpy as np
    f = np.float32
    out = {"ident": np.eye(P, dtype=f)}
    bm = np.zeros((P, P), f)
    bm[:64, :64] = bm[64:, 64:] = 1.0 / 64
    out["block_mean"] = bm
    grid_w, base = 64, 10000.0
    rows = N_LAT // grid_w
    row = np.repeat(np.arange(rows, dtype=f), grid_w)
    col = np.tile(np.arange(grid_w, dtype=f), rows)
    cos, sin = np.zeros((2, P, N_LAT), f), np.zeros((2, P, N_LAT), f)
    for which, dim in enumerate((DIFF_DH, SWA_DH)):
        nf = dim // 4
        inv = np.power(f(base), -np.arange(nf, dtype=f) / f(nf)).astype(f)
        ang = np.concatenate([row[:, None] * inv, col[:, None] * inv], axis=-1)
        for p in range(P):
            r = p % 32
            j = r % 16 + (16 * (p // 32 % 2) if dim == SWA_DH else 0)
            cos[which, p] = np.cos(ang[:, j])
            sin[which, p] = np.sin(ang[:, j]) * (-1.0 if r < 16 else 1.0)
    out["rope_cos"], out["rope_sin"] = cos, sin
    s, tt = np.arange(CH)[:, None], np.arange(CH)[None, :]
    masks = []
    for m in LEVELS:
        masks.append((s // (2 * m) == tt // (2 * m)) & (s % (2 * m) < m) & (tt % (2 * m) >= m))
    masks += [x.T for x in masks]
    masks.append(s == tt)
    out["gla_masks"] = np.ascontiguousarray(np.stack(masks, 1).astype(np.int32))
    q, kk = np.arange(P)[:, None], np.arange(P)[None, :]
    bias = np.zeros((LAT_TILES, P, 2 * P), f)
    bias[:, :, :P][:, kk < q] = -3e38
    bias[:, :, P:][:, kk > q] = -3e38
    bias[0, :, :P] = -3e38
    bias[LAT_TILES - 1, :, P:] = -3e38
    out["swa_bias"] = bias.reshape(LAT_TILES * P, 2 * P)
    return out


def kernel(x, c, ctx, c_ctx, w_ada, b_ada, w_in, w_gla_gate, b_gla_gate, gla_norm_g, diff_lambda,
           diff_norm_g, swa_sink, w_out, ln_g, ln_b, w_ffn_gate, w_ffn_up, w_ffn_down):
    import numpy as np
    import concourse.bacc as bacc
    from concourse.bass_utils import run_bass_kernel_spmd

    def tiled(w):
        L, d, n = w.shape
        return np.ascontiguousarray(w.reshape(L, KT, P, n // P, P).transpose(0, 3, 2, 1, 4)).reshape(L, n, D)

    at = np.cumsum([0, 256, 256, 256, 256, 16, 16, 256, 256, 256, 512, 128, 128])
    gq, gk, gv, go, z, _, dq, dk, dv, sq, sk, sv = [np.arange(a, b) for a, b in zip(at[:-1], at[1:])]
    z = np.arange(at[4], at[4] + P)
    turn = np.concatenate([np.arange(0, 16), np.arange(32, 48), np.arange(16, 32), np.arange(48, 64)])
    sq = np.concatenate([sq[h * 64 + turn] for j in range(4) for h in (j, 4 + j)])
    sk = np.concatenate([sk[h * 64 + turn] for h in range(2)])
    columns = np.concatenate([z, gq, gk, gv, go, dv, sv, dq, dk, sq, sk])
    groups = [tiled(np.asarray(w)).reshape(LAYERS, FFN_GROUPS, 2, P, D) for w in (w_ffn_gate, w_ffn_up)]
    down = np.asarray(w_ffn_down).reshape(LAYERS, FFN_GROUPS, 2, P, D)
    stream = np.stack([groups[0][:, :, 0], groups[1][:, :, 0], groups[0][:, :, 1], groups[1][:, :, 1],
                       down[:, :, 0], down[:, :, 1]], axis=2)
    arrays = {
        "x": np.asarray(x)[0], "ctx": np.asarray(ctx)[0],
        "cT": np.ascontiguousarray(np.stack([np.asarray(c)[0], np.asarray(c_ctx)]).reshape(2, KT, P).transpose(2, 1, 0)),
        "w_ada": np.asarray(w_ada), "b_ada": np.asarray(b_ada),
        "w_in": tiled(np.asarray(w_in)[:, :, columns]),
        "w_gate": np.asarray(w_gla_gate), "b_gate": np.asarray(b_gla_gate), "gla_norm_g": np.asarray(gla_norm_g),
        "diff_lambda": np.asarray(diff_lambda), "diff_norm_g": np.asarray(diff_norm_g), "swa_sink": np.asarray(swa_sink),
        "w_out": np.asarray(w_out), "ln_g": np.asarray(ln_g), "ln_b": np.asarray(ln_b),
        "w_ffn": stream.reshape(LAYERS, FFN_GROUPS * 6 * P, D),
        **constants(),
    }
    arrays = {n + "_dram": np.ascontiguousarray(a) for n, a in arrays.items()}
    nc = bacc.Bacc("TRN2", target_bir_lowering=False, num_devices=1)
    t = {n[:-5]: nc.dram_tensor(n, a.shape, mybir.dt.from_np(a.dtype), kind="ExternalInput").ap() for n, a in arrays.items()}
    for name, shape in (("mod", (LAYERS, 2, ADA)), ("proj", (IN_TILES * P, PAD_T)), ("mix", (D, T)), ("h_mid", (T, D)), ("h_next", (T, D))):
        t[name] = nc.dram_tensor(name + "_scratch", shape, F32, kind="Internal").ap()
    t["out"] = nc.dram_tensor("out_dram", (N_LAT, D), F32, kind="ExternalOutput").ap()
    build(nc, t)
    got = run_bass_kernel_spmd(nc, [arrays], core_ids=[0])
    return got.results[0]["out_dram"].reshape(1, N_LAT, D)
```

```python
import math
from contextlib import ExitStack

import concourse.bass as bass
import concourse.mybir as mybir

F32 = mybir.dt.float32
F32R = mybir.dt.float32r
I32 = mybir.dt.int32
ALU = mybir.AluOpType
ACT = mybir.ActivationFunctionType
AX = mybir.AxisListType

P = 128
LAYERS = 2
D = 1024
KT = D // P
N_CTX, N_LAT = 256, 1024
T = N_CTX + N_LAT
CTX_TILES, LAT_TILES = N_CTX // P, N_LAT // P
TILES = CTX_TILES + LAT_TILES
BANK = 512
CHUNKS = [(256, 512), (768, 512), (0, 256)]
LAT_CHUNKS = CHUNKS[:2]

FFN = 2816
FFN_TILES = FFN // P
FFN_GROUPS = FFN_TILES // 2
ADA = 6 * D
ADA_CHUNKS = ADA // BANK

T_Z, T_GQ, T_GK, T_GV, T_GO, T_DV, T_SV = 0, 1, 3, 5, 7, 9, 11
T_DQ, T_DK, T_SQ, T_SK = 12, 14, 16, 20
IN_TILES = 21
PLAIN_TILES = 12
HEAD_DQ, HEAD_DK, HEAD_SQ, HEAD_SK = 0, 2 * P, 4 * P, 8 * P
HEAD_ROWS = 9 * P
PAD_T = T + P

GATE_RANK = 16
GATE_NORM = 16.0
CH = 128
NCH = T // CH
LEVELS = [64, 32, 16, 8, 4, 2, 1]
DIFF_HEADS, DIFF_DH = 4, 32
SWA_HEADS, SWA_DH = 8, 64
SWA_KEYS = N_CTX + 3 * P
EPS = 1e-6
ALPHA = (2.0 * LAYERS) ** 0.25


def peeled(eng, first, end, body):
    body(first, True)
    if end - first > 1:
        with eng.Fori(first + 1, end) as i:
            body(i, False)


def wait_apart(eng, sem, value, passed):
    eng.wait_ge(sem, value)
    eng.sem_inc(passed, 1)


def wait_count(eng, sem, value):
    if not isinstance(value, int) or value > 0:
        eng.wait_ge(sem, value)


class Live:

    def __init__(self, r, units, starts):
        self.r, self.units, self.starts = r, units, starts

    def __call__(self, lag):
        return self.r - lag < self.units and (self.r >= lag or not self.starts)


def staggered(eng, first, end, units, lag, step):
    for r in range(units):
        step(first, r, Live(r, units, True))
    if end - first > 1:
        with eng.Fori(first + 1, end) as i:
            for r in range(units):
                step(i, r, Live(r, units, False))
    for r in range(units, units + lag):
        step(end - 1, r, Live(r, units, end - first == 1))


def allocators(nc, ctx, phase):
    def sb(name, shape, dt=F32):
        return ctx.enter_context(nc.sbuf_tensor(name, shape, dt))

    def ps(name, shape):
        return ctx.enter_context(nc.psum_tensor(name, shape, F32))

    def sem(name):
        return nc.alloc_semaphore(phase + name)
    return sb, ps, sem


def product(pe, out, st_hi, st_lo, mv_hi, mv_lo, start, stop):
    pe.matmul(out, st_hi, mv_hi, start=start, stop=False)
    pe.matmul(out, st_hi, mv_lo, start=False, stop=False)
    return pe.matmul(out, st_lo, mv_hi, start=False, stop=stop)


def modulation(nc, t):
    with nc.cleanup_on_exit(), ExitStack() as ctx:
        sb, ps, sem = allocators(nc, ctx, "ada_")
        cT = sb("ada_c", [P, KT, 2])
        cs = sb("ada_silu", [P, KT, 2])
        W = sb("ada_w", [P, 4, KT, BANK])
        B = sb("ada_b", [2, 4, BANK])
        R = sb("ada_rows", [2, 4, BANK])
        acc = ps("ada_acc", [P, 4, BANK])
        c_in, c_silu = sem("c_in"), sem("c_silu")
        w_in = [sem(f"ada_w_in{s}") for s in range(4)]
        product_done, row_done = sem("ada_product_done"), sem("ada_row_done")
        row_out = [sem(f"ada_row_out{s}") for s in range(4)]
        steps = LAYERS * ADA_CHUNKS // 4
        per_layer = ADA_CHUNKS // 4
        block = ctx.enter_context(nc.Block())

        @block.sync
        def _(sp):
            sp.dma_start(cT[:, :, :], t["cT"]).then_inc(c_in, 16)
            for l in range(LAYERS):
                def body(i, first):
                    for s in range(4):
                        col = i * 4 * BANK + s * BANK
                        if not first:
                            sp.wait_ge(product_done, 4 * (l * per_layer + i - 1) + s + 1)
                            sp.wait_ge(row_done, 4 * (l * per_layer + i - 1) + s + 1)
                        elif l:
                            sp.wait_ge(product_done, 4 * (l * per_layer - 1) + s + 1)
                            sp.wait_ge(row_done, 4 * (l * per_layer - 1) + s + 1)
                        sp.dma_start(W[:, s, :, :], t["w_ada"][l].rearrange("(k p) n -> p k n", p=P)[:, :, bass.ds(col, BANK)]).then_inc(w_in[s], 16)
                        sp.dma_start(B[:, s, :], t["b_ada"][l:l + 1, bass.ds(col, BANK)].to_broadcast([2, BANK])).then_inc(w_in[s], 16)
                peeled(sp, 0, per_layer, body)

        @block.scalar
        def _(act):
            act.wait_ge(c_in, 16)
            act.activation(cs[:, :, :], cT[:, :, :], ACT.Silu).then_inc(c_silu, 1)
            for l in range(LAYERS):
                with act.Fori(0, per_layer) as i:
                    for s in range(4):
                        act.wait_ge(row_done, 4 * (l * per_layer) + i * 4 + s + 1)
                        act.dma_start(t["mod"][l, :, bass.ds(i * 4 * BANK + s * BANK, BANK)], R[:, s, :]).then_inc(row_out[s], 16)
            for s in range(4):
                act.wait_ge(row_out[s], 16 * steps)

        @block.tensor
        def _(pe):
            pe.wait_ge(c_silu, 1)

            def body(i, first):
                for s in range(4):
                    pe.wait_ge(w_in[s], i * 32 + 32)
                    if not first:
                        pe.wait_ge(row_done, 4 * (i - 1) + s + 1)
                    for k in range(KT):
                        mm = pe.matmul(acc[0:2, s, :], cs[:, k, :], W[:, s, k, :], start=(k == 0), stop=(k == KT - 1))
                    mm.then_inc(product_done, 1)
            peeled(pe, 0, steps, body)

        @block.vector
        def _(dve):
            def body(i, first):
                for s in range(4):
                    dve.wait_ge(product_done, i * 4 + s + 1)
                    if not first:
                        dve.wait_ge(row_out[s], i * 16)
                    dve.tensor_tensor(R[:, s, :], acc[0:2, s, :], B[:, s, :], ALU.add).then_inc(row_done, 1)
            peeled(dve, 0, steps, body)


def norm_tiles(nc, t, res, kind, layer, tiles, last):
    with nc.cleanup_on_exit(), ExitStack() as ctx:
        sb, ps, sem = allocators(nc, ctx, f"norm_{kind}{layer}_")
        nm = f"norm_{kind}{layer}_"
        post = kind != "input"
        attn = kind == "attention"
        modulated = not last
        first_pair = tiles[0] // 2
        pairs = len(tiles) // 2
        streams = [0, 1] if tiles[0] == 0 else [1]
        next_mod = {"input": (layer, 0, 1), "attention": (layer, 3, 4), "ffn": (layer + 1, 0, 1)}[kind]
        gate_at = 2 if attn else 5
        ln_at = 0 if attn else 1

        uhi, ulo, ident = res["uhi"], res["ulo"], res["ident"]
        hres = sb(nm + "hres", [P, 2, D])
        r = sb(nm + "r", [P, 2, D])
        h = sb(nm + "h", [P, 2, D])
        gate = sb(nm + "gate", [P, 2, D]) if post else None
        lng = sb(nm + "lng", [P, D]) if post else None
        lnb = sb(nm + "lnb", [P, D]) if post else None
        shift = sb(nm + "shift", [P, 2, KT])
        scale = sb(nm + "scale", [P, 2, KT])
        stats = sb(nm + "stats", [P, 2, 2, 2, 6])
        mv = sb(nm + "mv", [P, 2, 2, 2])
        sd = sb(nm + "sd", [P, 2, 2])
        rstd = sb(nm + "rstd", [P, 2, 2])
        nmu = sb(nm + "nmu", [P, 2, 2])
        eps = sb(nm + "eps", [P, 1])
        if attn:
            wohi = sb(nm + "wohi", [P, KT, D], F32R)
            wolo = sb(nm + "wolo", [P, KT, D], F32R)
            mhi = sb(nm + "mhi", [P, 2, KT, P], F32R)
            mlo = sb(nm + "mlo", [P, 2, KT, P], F32R)
            Y = ps(nm + "y", [P, 2, D])
        TR = ps(nm + "tr", [P, 2, KT, P])

        passed, pool_passed = sem("passed"), sem("pool_passed")
        const_in, eps_set, one_plus = sem("const_in"), sem("eps_set"), sem("one_plus")
        h_in = [sem(f"h_in{s}") for s in range(2)]
        mix_in = [sem(f"mix_in{s}") for s in range(2)]
        wo_in = [sem(f"wo_in{s}") for s in range(2)]
        wo_hi, wo_lo = sem("wo_hi"), sem("wo_lo")
        mix_hi, mix_lo, y_done = sem("mix_hi"), sem("mix_lo"), sem("y_done")
        gated, summed = sem("gated"), sem("summed")
        st_done, mv_done, sd_done, rs_done, nm_done = (sem("st_done"), sem("mv_done"), sem("sd_done"), sem("rs_done"), sem("nm_done"))
        ln1, h_scaled, h_done = sem("ln1"), sem("h_scaled"), sem("h_done")
        ln2, turned, u_done, u_hi, u_lo = sem("ln2"), sem("turned"), sem("u_done"), sem("u_hi"), sem("u_lo")
        h_out = [sem(f"h_out{s}") for s in range(2)]
        block = ctx.enter_context(nc.Block())
        consts = 0

        def count(i, s):
            return (i - first_pair) * 2 + s + 1

        def src_rows(i, s):
            if kind == "input":
                return t["ctx"][s * P:(s + 1) * P, :] if i is first_pair and tiles[0] == 0 else t["x"][bass.ds(i * 2 * P + (s * P - N_CTX), P), :]
            if attn and layer == 0:
                return t["ctx"][s * P:(s + 1) * P, :] if i is first_pair and tiles[0] == 0 else t["x"][bass.ds(i * 2 * P + (s * P - N_CTX), P), :]
            return t["h_mid" if not attn else "h_next"][bass.ds(i * 2 * P + s * P, P), :]

        def dst_rows(i, s):
            if last:
                return t["out"][bass.ds(i * 2 * P + (s * P - N_CTX), P), :]
            return t["h_mid" if attn else "h_next"][bass.ds(i * 2 * P + s * P, P), :]

        @block.sync
        def _(sp):
            if attn:
                for k in range(KT):
                    if k >= 2:
                        sp.wait_ge(wo_lo, k - 1)
                    sp.dma_start(h[:, k % 2, :], t["w_out"][layer, k * P:(k + 1) * P, :]).then_inc(wo_in[k % 2], 16)

            def body(i, first):
                for s in range(2):
                    if not first and modulated:
                        sp.wait_ge(u_lo, count(i, s) - 2)
                        sp.wait_ge(turned, count(i, s) - 2)
                    elif not first:
                        sp.wait_ge(ln1, count(i, s) - 2)
                        sp.wait_ge(summed, count(i, s) - 2)
                    if attn:
                        sp.dma_start(r[:, s, :].rearrange("p (k n) -> p k n", k=KT),
                                     t["mix"].rearrange("(k p) n -> p k n", p=P)[:, :, bass.ds(i * 2 * P + s * P, P)]).then_inc(mix_in[s], 16)
                    sp.dma_start(hres[:, s, :], src_rows(i, s)).then_inc(h_in[s], 16)
            peeled(sp, first_pair, first_pair + pairs, body)

        @block.tensor
        def _(pe):
            if attn:
                pe.wait_ge(wo_lo, KT)

            def body(i, first):
                if attn:
                    for s in range(2):
                        pe.wait_ge(mix_lo, count(i, s))
                        if not first:
                            pe.wait_ge(gated, count(i, s) - 2)
                        for half in range(2):
                            for k in range(KT):
                                cols = slice(half * BANK, (half + 1) * BANK)
                                mm = product(pe, Y[:, s, cols], mhi[:, s, k, :], mlo[:, s, k, :],
                                             wohi[:, k, cols], wolo[:, k, cols], k == 0, k == KT - 1)
                        mm.then_inc(y_done, 1)
                if modulated:
                    for s in range(2):
                        pe.wait_ge(ln2, count(i, s))
                        if not first:
                            pe.wait_ge(u_done, count(i, s) - 2)
                        for k in range(KT):
                            mm = pe.transpose(TR[:, s, k, :], r[:, s, k * P:(k + 1) * P], ident[:, :])
                        mm.then_inc(turned, 1)
            if attn or modulated:
                peeled(pe, first_pair, first_pair + pairs, body)

        LN = post + modulated
        lnc = lambda i, s, j: (i - first_pair) * 2 * LN + j * 2 + s + 1

        @block.vector
        def _(dve):
            if modulated:
                dve.wait_ge(const_in, 16 * (2 * len(streams) + (2 + len(streams) if post else 0)))
                dve.tensor_scalar(scale[:, streams[0]:2, :], scale[:, streams[0]:2, :], 1.0, None, ALU.add).then_inc(one_plus, 1)

            def statistics(i, s, j, src):
                for half in range(2):
                    dve.bn_stats(stats[:, s, j, half, :], src[:, s, half * BANK:(half + 1) * BANK]).then_inc(st_done, 1)
                wait_apart(dve, st_done, 2 * lnc(i, s, j), passed)
                dve.bn_aggr(mv[:, s, j, :], stats[:, s, j, :, :]).then_inc(mv_done, 1)

            def normalizers(i, s, j):
                dve.wait_ge(sd_done, lnc(i, s, j))
                dve.reciprocal(rstd[:, s, j:j + 1], sd[:, s, j:j + 1]).then_inc(rs_done, 1)
                dve.wait_ge(rs_done, lnc(i, s, j))
                dve.scalar_tensor_tensor(nmu[:, s, j:j + 1], mv[:, s, j, 0:1], -1.0, rstd[:, s, j:j + 1], ALU.mult, ALU.mult).then_inc(nm_done, 1)

            def body(i, first):
                st = 0 if (first and tiles[0] == 0) else 1
                if post:
                    for s in range(2):
                        if attn:
                            dve.wait_ge(y_done, count(i, s))
                            dve.tensor_tensor(r[:, s, :], Y[:, s, :], gate[:, st, :], ALU.mult).then_inc(gated, 1)
                        else:
                            if not first:
                                dve.wait_ge(turned, count(i, s) - 2) if modulated else dve.wait_ge(ln1, count(i, s) - 2)
                            if not modulated:
                                dve.wait_ge(const_in, 16 * (2 * len(streams) + 2 + len(streams)))
                            y = res["y"][:, bass.ds(i * 2 + s, 1), :].rearrange("p a b -> p (a b)")
                            dve.tensor_tensor(r[:, s, :], y, gate[:, st, :], ALU.mult).then_inc(gated, 1)
                        dve.wait_ge(gated, count(i, s))
                        dve.wait_ge(h_in[s], (i - first_pair) * 16 + 16)
                        dve.scalar_tensor_tensor(r[:, s, :], hres[:, s, :], ALPHA, r[:, s, :], ALU.mult, ALU.add).then_inc(summed, 1)
                        dve.wait_ge(summed, count(i, s))
                        statistics(i, s, 0, r)
                    for s in range(2):
                        normalizers(i, s, 0)
                    if modulated:
                        for s in range(2):
                            dve.wait_ge(h_done, count(i, s))
                            statistics(i, s, 1, h)
                        for s in range(2):
                            normalizers(i, s, 1)
                else:
                    for s in range(2):
                        dve.wait_ge(h_in[s], (i - first_pair) * 16 + 16)
                        statistics(i, s, 0, hres)
                    for s in range(2):
                        normalizers(i, s, 0)
            peeled(dve, first_pair, first_pair + pairs, body)

        @block.scalar
        def _(act):
            act.wait_ge(eps_set, 1)
            if attn:
                for k in range(KT):
                    act.wait_ge(wo_in[k % 2], 16 * (k // 2 + 1))
                    act.copy(wohi[:, k, :], h[:, k % 2, :]).then_inc(wo_hi, 1)
                act.wait_ge(wo_lo, KT)
            if modulated:
                act.wait_ge(one_plus, 1)

            def deviation(i, s, j):
                act.wait_ge(mv_done, lnc(i, s, j))
                act.activation(sd[:, s, j:j + 1], mv[:, s, j, 1:2], ACT.Sqrt, bias=eps[:, 0:1]).then_inc(sd_done, 1)

            def body(i, first):
                st = 0 if (first and tiles[0] == 0) else 1
                if attn:
                    for s in range(2):
                        act.wait_ge(mix_in[s], (i - first_pair) * 16 + 16)
                        if not first:
                            act.wait_ge(y_done, count(i, s) - 2)
                        act.copy(mhi[:, s, :, :], r[:, s, :].rearrange("p (k n) -> p k n", k=KT)).then_inc(mix_hi, 1)
                if post:
                    for s in range(2):
                        deviation(i, s, 0)
                    for s in range(2):
                        act.wait_ge(nm_done, lnc(i, s, 0))
                        if not first:
                            act.wait_ge(h_out[s], (i - first_pair) * 16)
                        act.activation(h[:, s, :], r[:, s, :], ACT.Identity, scale=rstd[:, s, 0:1], bias=nmu[:, s, 0:1]).then_inc(ln1, 1)
                if modulated:
                    j = 1 if post else 0
                    src = h if post else hres
                    for s in range(2):
                        deviation(i, s, j)
                    for s in range(2):
                        act.wait_ge(nm_done, lnc(i, s, j))
                        if not post and not first:
                            act.wait_ge(turned, count(i, s) - 2)
                        act.activation(r[:, s, :], src[:, s, :], ACT.Identity, scale=rstd[:, s, j:j + 1], bias=nmu[:, s, j:j + 1]).then_inc(ln2, 1)
                    for s in range(2):
                        act.wait_ge(turned, count(i, s))
                        if not post:
                            act.wait_ge(ln2, count(i, s))
                        for k in range(KT):
                            a = act.activation(hres[:, s, k * P:(k + 1) * P], TR[:, s, k, :], ACT.Identity,
                                               scale=scale[:, st, k:k + 1], bias=shift[:, st, k:k + 1])
                        a.then_inc(u_done, 1)
            peeled(act, first_pair, first_pair + pairs, body)

        @block.gpsimd
        def _(pool):
            pool.memset(eps[:, :], EPS).then_inc(eps_set, 1)
            n = 0
            for st in streams:
                for dst, at in ((shift, next_mod[1]), (scale, next_mod[2])):
                    lay = min(next_mod[0], LAYERS - 1)
                    pool.dma_start(dst[:, st, :], t["mod"][lay, 1 - st, at * D:(at + 1) * D].rearrange("(k p) -> p k", p=P)).then_inc(const_in, 16)
                if post:
                    pool.dma_start(gate[:, st, :], t["mod"][layer, 1 - st:2 - st, gate_at * D:(gate_at + 1) * D].to_broadcast([P, D])).then_inc(const_in, 16)
            if post:
                pool.dma_start(lng[:, :], t["ln_g"][layer, ln_at:ln_at + 1, :].to_broadcast([P, D])).then_inc(const_in, 16)
                pool.dma_start(lnb[:, :], t["ln_b"][layer, ln_at:ln_at + 1, :].to_broadcast([P, D])).then_inc(const_in, 16)
            if attn:
                for k in range(KT):
                    pool.wait_ge(wo_hi, k + 1)
                    pool.tensor_tensor(wolo[:, k, :], h[:, k % 2, :], wohi[:, k, :].bitcast(F32), ALU.subtract).then_inc(wo_lo, 1)
            pool.wait_ge(const_in, 16 * (2 * len(streams) + (2 + len(streams) if post else 0)))

            def body(i, first):
                if attn:
                    for s in range(2):
                        pool.wait_ge(mix_hi, count(i, s))
                        pool.tensor_tensor(mlo[:, s, :, :], r[:, s, :].rearrange("p (k n) -> p k n", k=KT),
                                           mhi[:, s, :, :].bitcast(F32), ALU.subtract).then_inc(mix_lo, 1)
                if post:
                    for s in range(2):
                        pool.wait_ge(ln1, count(i, s))
                        pool.tensor_tensor(h[:, s, :], h[:, s, :], lng[:, :], ALU.mult).then_inc(h_scaled, 1)
                        pool.wait_ge(h_scaled, count(i, s))
                        pool.tensor_tensor(h[:, s, :], h[:, s, :], lnb[:, :], ALU.add).then_inc(h_done, 1)
                        pool.wait_ge(h_done, count(i, s))
                        pool.dma_start(dst_rows(i, s), h[:, s, :]).then_inc(h_out[s], 16)
                if modulated:
                    for s in range(2):
                        wait_apart(pool, u_done, count(i, s), pool_passed)
                        u = hres[:, s, :].rearrange("p (k n) -> p k n", k=KT)
                        at = bass.ds(i * 2 * P + s * P, P)
                        pool.tensor_copy(uhi[:, :, at], u).then_inc(u_hi, 1)
                        pool.wait_ge(u_hi, count(i, s))
                        pool.tensor_tensor(ulo[:, :, at], u, uhi[:, :, at].bitcast(F32), ALU.subtract).then_inc(u_lo, 1)
            peeled(pool, first_pair, first_pair + pairs, body)
            if post:
                for s in range(2):
                    pool.wait_ge(h_out[s], 16 * pairs)


def input_projection(nc, t, res, layer):
    with nc.cleanup_on_exit(), ExitStack() as ctx:
        sb, ps, sem = allocators(nc, ctx, f"in{layer}_")
        nm = f"in{layer}_"
        uhi, ulo = res["uhi"], res["ulo"]
        raw = sb(nm + "raw", [P, 2, D])
        whi = sb(nm + "whi", [P, 2, KT, P], F32R)
        wlo = sb(nm + "wlo", [P, 2, KT, P], F32R)
        stage = sb(nm + "stage", [P, 2, T])
        swap = sb(nm + "swap", [P, 2, N_LAT])
        cos = sb(nm + "cos", [P, 2, N_LAT])
        sin = sb(nm + "sin", [P, 2, N_LAT])
        zero = sb(nm + "zero", [P, P])
        shi = sb(nm + "shi", [P, 2, T], F32R)
        slo = sb(nm + "slo", [P, 2, T], F32R)
        acc = ps(nm + "acc", [P, 2, 3, BANK])
        raw_in = [sem(f"raw_in{s}") for s in range(2)]
        passed = sem("passed")
        rope_in, zero_set, pad_out = sem("rope_in"), sem("zero_set"), sem("pad_out")
        w_hi, w_ready, chunk_done, evacuated = sem("w_hi"), sem("w_ready"), sem("chunk_done"), sem("evacuated")
        swapped, cos_done, sin_done, roped = sem("swapped"), sem("cos_done"), sem("sin_done"), sem("roped")
        out_hi, out_lo = sem("out_hi"), sem("out_lo")
        stored = [sem(f"stored{s}") for s in range(2)]
        stored_hl = [sem(f"stored_hl{s}") for s in range(2)]
        NCHK = len(CHUNKS)
        block = ctx.enter_context(nc.Block())
        pairs = IN_TILES // 2
        MASK = list(range(16, 32)) + list(range(16))

        def each_tile(eng, body, pairs_from=0, pairs_to=pairs, tail=True):
            def two(i, first):
                for s in range(2):
                    body(i * 2 + s, i, s, first and pairs_from == 0)
            if pairs_from == 0:
                peeled(eng, 0, pairs_to, two)
            else:
                with eng.Fori(pairs_from, pairs_to) as i:
                    two(i, False)
            if tail:
                body(IN_TILES - 1, pairs, 0, False)

        @block.sync
        def _(sp):
            sp.dma_start(cos[:, :, :], t["rope_cos"].rearrange("a p n -> p a n")).then_inc(rope_in, 16)
            sp.dma_start(sin[:, :, :], t["rope_sin"].rearrange("a p n -> p a n")).then_inc(rope_in, 16)

            def body(n, i, s, first):
                if not first:
                    sp.wait_ge(w_ready, n - 1)
                sp.dma_start(raw[:, s, :], t["w_in"][layer][bass.ds(n * P, P), :]).then_inc(raw_in[s], 16)
            each_tile(sp, body)

        @block.gpsimd
        def _(pool):
            pool.memset(zero[:, :], 0.0).then_inc(zero_set, 1)
            pool.wait_ge(zero_set, 1)
            pool.dma_start(t["proj"][T_SV * P:(T_SV + 1) * P, T:PAD_T], zero[:, :]).then_inc(pad_out, 16)
            for part in range(2):
                pool.dma_start(t["heads"][part, HEAD_SK:HEAD_SK + P, T:PAD_T], zero[:, :]).then_inc(pad_out, 16)
            pool.wait_ge(rope_in, 32)

            def split(n, i, s, first):
                pool.wait_ge(w_hi, n + 1)
                pool.tensor_tensor(wlo[:, s, :, :], raw[:, s, :].rearrange("p (k n) -> p k n", k=KT),
                                   whi[:, s, :, :].bitcast(F32), ALU.subtract).then_inc(w_ready, 1)
            each_tile(pool, split)
            pool.wait_ge(pad_out, 48)

        @block.tensor
        def _(pe):
            def body(n, i, s, first):
                pe.wait_ge(w_ready, n + 1)
                for c, (t0, tn) in enumerate(CHUNKS):
                    if not first:
                        pe.wait_ge(evacuated, (n - 2) * NCHK + c + 1)
                    for k in range(KT):
                        mm = product(pe, acc[:, s, c, 0:tn], whi[:, s, k, :], wlo[:, s, k, :],
                                     uhi[:, k, t0:t0 + tn], ulo[:, k, t0:t0 + tn], k == 0, k == KT - 1)
                    mm.then_inc(chunk_done, 1)
            each_tile(pe, body)

        @block.scalar
        def _(act):
            def split(n, i, s, first):
                act.wait_ge(raw_in[s], i * 16 + 16)
                if not first:
                    act.wait_ge(chunk_done, (n - 1) * NCHK)
                act.copy(whi[:, s, :, :], raw[:, s, :].rearrange("p (k n) -> p k n", k=KT)).then_inc(w_hi, 1)

            def evacuate(n, s):
                for c, (t0, tn) in enumerate(CHUNKS):
                    act.wait_ge(chunk_done, n * NCHK + c + 1)
                    act.copy(stage[:, s, t0:t0 + tn], acc[:, s, c, 0:tn]).then_inc(evacuated, 1)

            def finish_plain(n, i, s, first):
                if not first:
                    act.wait_ge(stored[s], i * 16)
                evacuate(n, s)
                act.wait_ge(evacuated, (n + 1) * NCHK)
                act.dma_start(t["proj"][bass.ds(n * P, P), 0:T], stage[:, s, :]).then_inc(stored[s], 16)

            def finish_rope(n, i, s, first):
                if first:
                    act.wait_ge(stored[s], PLAIN_TILES // 2 * 16)
                else:
                    act.wait_ge(out_lo, n - PLAIN_TILES - 1)
                evacuate(n, s)
                act.wait_ge(out_lo, n - PLAIN_TILES + 1)
                at = bass.ds((n - PLAIN_TILES) * P, P)
                act.dma_start(t["heads"][0, at, 0:T], shi[:, s, :].bitcast(F32)).then_inc(stored_hl[s], 16)
                act.dma_start(t["heads"][1, at, 0:T], slo[:, s, :].bitcast(F32)).then_inc(stored_hl[s], 16)

            split(0, 0, 0, True)
            split(1, 0, 1, True)
            for finish, lo, hi in ((finish_plain, 0, PLAIN_TILES // 2), (finish_rope, PLAIN_TILES // 2, pairs - 1)):
                def two(i, first):
                    for s in range(2):
                        finish(i * 2 + s, i, s, first)
                        split(i * 2 + s + 2, i + 1, s, False)
                peeled(act, lo, hi, two)
            finish_rope(2 * pairs - 2, pairs - 1, 0, False)
            split(2 * pairs, pairs, 0, False)
            finish_rope(2 * pairs - 1, pairs - 1, 1, False)
            finish_rope(2 * pairs, pairs, 0, False)
            for s in range(2):
                act.wait_ge(stored[s], 16 * PLAIN_TILES // 2)
                act.wait_ge(stored_hl[s], 32 * ((IN_TILES - PLAIN_TILES + 1 - s) // 2))

        @block.vector
        def _(dve):
            dve.wait_ge(rope_in, 32)

            def rope(n, i, s, table, first=False):
                m = n - PLAIN_TILES + 1
                x = stage[:, s, N_CTX:T]
                wait_apart(dve, evacuated, (n + 1) * NCHK, passed)
                dve.stream_shuffle(swap[:, s, :], x, MASK).then_inc(swapped, 1)
                dve.wait_ge(swapped, m)
                dve.tensor_tensor(x, x, cos[:, table, :], ALU.mult).then_inc(cos_done, 1)
                dve.tensor_tensor(swap[:, s, :], swap[:, s, :], sin[:, table, :], ALU.mult).then_inc(sin_done, 1)
                dve.wait_ge(cos_done, m)
                dve.wait_ge(sin_done, m)
                dve.tensor_tensor(x, x, swap[:, s, :], ALU.add).then_inc(roped, 1)
                dve.wait_ge(roped, m)
                if not first:
                    dve.wait_ge(stored_hl[s], (i - PLAIN_TILES // 2) * 32)
                dve.tensor_copy(shi[:, s, :], stage[:, s, :]).then_inc(out_hi, 1)
                dve.wait_ge(out_hi, m)
                dve.tensor_tensor(slo[:, s, :], stage[:, s, :], shi[:, s, :].bitcast(F32), ALU.subtract).then_inc(out_lo, 1)
            for s in range(2):
                rope(PLAIN_TILES + s, PLAIN_TILES // 2, s, 0, True)
            for lo, hi, table in ((T_DQ // 2 + 1, T_SQ // 2, 0), (T_SQ // 2, pairs, 1)):
                with dve.Fori(lo, hi) as i:
                    for s in range(2):
                        rope(i * 2 + s, i, s, table)
            rope(IN_TILES - 1, pairs, 0, 1)


def gated_linear_attention(nc, t, res, layer):
    with nc.cleanup_on_exit(), ExitStack() as ctx:
        sb, ps, sem = allocators(nc, ctx, f"gla{layer}_")
        nm = f"gla{layer}_"
        ident = res["ident"]
        FLAT = [(0, 512), (512, 512), (1024, 256)]
        DI = [(d, i) for d in range(2) for i in range(2)]
        q = sb(nm + "q", [P, 2, T])
        k = sb(nm + "k", [P, 2, T])
        vT = sb(nm + "vT", [P, 2, T])
        V = sb(nm + "V", [P, TILES, 2 * P])
        z = sb(nm + "z", [2 * GATE_RANK, T])
        wg = sb(nm + "wg", [2 * GATE_RANK, 2, 2 * P])
        bg = sb(nm + "bg", [P, 2, 2])
        normg = sb(nm + "normg", [P, 1])
        reset = sb(nm + "reset", [P, T])
        B = sb(nm + "B", [P, 4, T])
        Dc = sb(nm + "D", [P, 2, T])
        X = sb(nm + "X", [P, 2, T])
        Qe = sb(nm + "Qe", [P, 4, T])
        KeT = sb(nm + "KeT", [P, 2, NCH, P])
        dec = sb(nm + "dec", [P, 4, NCH])
        S = sb(nm + "S", [P, 4, NCH, P])
        A = sb(nm + "A", [P, 2, 2, NCH, CH])
        masks = sb(nm + "masks", [P, 2 * len(LEVELS) + 1, CH], I32)
        block_mean = sb(nm + "block_mean", [P, P])
        eps = sb(nm + "eps", [P, 1])
        UNIT = ps(nm + "unit", [P, 2, 3 * BANK])
        TR = ps(nm + "tr", [P, 2, BANK])

        load = {n: sem(f"gla_{n}_in") for n in ("q", "k", "v", "z", "w", "b", "mask", "bm", "g", "go")}
        zeroed, wg_zero = sem("zeroed"), sem("wg_zero")
        reset_one, reset_set, q_scaled = sem("reset_one"), sem("reset_set"), sem("q_scaled")
        v_turned, v_copied = sem("v_turned"), sem("v_copied")
        logits, abs_done, exp_of_abs, log_done, min_done, gate_done, scanned = (
            sem("logits"), sem("abs_done"), sem("exp_of_abs"), sem("log_done"), sem("min_done"), sem("gate_done"), sem("scanned"))
        d_done, e_done, x_done, unit_done, copied = sem("d_done"), sem("e_done"), sem("x_done"), sem("unit_done"), sem("copied")
        qe_e, qe_done, ke_turned, ke_copied, dec_done = sem("qe_e"), sem("qe_done"), sem("ke_turned"), sem("ke_copied"), sem("dec_done")
        u_done, state = sem("u_done"), sem("state")
        o_done, o_copied, squared, mean_done, rms_done = sem("o_done"), sem("o_copied"), sem("squared"), sem("mean_done"), sem("rms_done")
        inv_done, silu_done, gate_ready, normed, gated, stored = (
            sem("inv_done"), sem("silu_done"), sem("gate_ready"), sem("normed"), sem("gated"), sem("stored"))
        block = ctx.enter_context(nc.Block())
        NL = len(LEVELS)
        UNITS0 = 4
        NPAIR = 4 * NL
        BORDER = [1, 0] + list(range(NCH - 1, 1, -1))
        ORDER = [list(range(NCH)), BORDER]

        def halves(ap, m):
            return ap.rearrange("p (n h m) -> p n h m", h=2, m=m)

        def min_steps(g):
            per = [4, 4, 1]
            return (g // 3) * (NCH - 1) + sum(per[:g % 3 + 1])

        proj = t["proj"]

        @block.sync
        def _(sp):
            sp.dma_start(z[:, :], proj[T_Z * P:T_Z * P + 2 * GATE_RANK, 0:T]).then_inc(load["z"], 16)
            sp.wait_ge(wg_zero, 1)
            for d in range(2):
                sp.dma_start(wg[d * GATE_RANK:(d + 1) * GATE_RANK, d, :], t["w_gate"][layer, d]).then_inc(load["w"], 16)
                sp.dma_start(bg[:, d, :], t["b_gate"][layer, d:d + 1, :].rearrange("a (i p) -> p (a i)", p=P)).then_inc(load["b"], 16)
            sp.dma_start(k[:, :, :], proj[T_GK * P:(T_GK + 2) * P, 0:T].rearrange("(i p) n -> p i n", p=P)).then_inc(load["k"], 16)
            sp.dma_start(q[:, :, :], proj[T_GQ * P:(T_GQ + 2) * P, 0:T].rearrange("(i p) n -> p i n", p=P)).then_inc(load["q"], 16)
            sp.dma_start(masks[:, :, :], t["gla_masks"]).then_inc(load["mask"], 16)
            sp.dma_start(vT[:, :, :], proj[T_GV * P:(T_GV + 2) * P, 0:T].rearrange("(i p) n -> p i n", p=P)).then_inc(load["v"], 16)
            sp.dma_start(block_mean[:, :], t["block_mean"]).then_inc(load["bm"], 16)
            for h in range(2):
                sp.dma_start(normg[h * 64:(h + 1) * 64, :], t["gla_norm_g"][layer].rearrange("(p a) -> p a", a=1)).then_inc(load["g"], 16)
            sp.wait_ge(v_turned, 6)
            sp.dma_start(vT[:, :, :], proj[T_GO * P:(T_GO + 2) * P, 0:T].rearrange("(i p) n -> p i n", p=P)).then_inc(load["go"], 16)
            for i in range(2):
                sp.wait_ge(gated, i + 1)
                sp.dma_start(t["mix"][i * P:(i + 1) * P, :], X[:, i, :]).then_inc(stored, 16)
            sp.wait_ge(stored, 32)

        @block.gpsimd
        def _(pool):
            pool.memset(wg[:, :, :], 0.0).then_inc(wg_zero, 1)
            pool.memset(eps[:, :], EPS).then_inc(zeroed, 1)
            pool.memset(A[:, :, :, :, :], 0.0).then_inc(zeroed, 1)
            pool.memset(S[:, :, :, :], 0.0).then_inc(zeroed, 1)
            pool.wait_ge(load["k"], 16)
            pool.wait_ge(q_scaled, 1)
            n = 0
            for i in range(2):
                for d in range(2):
                    for m in LEVELS:
                        pool.wait_ge(e_done, n + 1)
                        if n >= 2:
                            pool.wait_ge(unit_done, UNITS0 + 2 * (n - 1))
                        e, x = halves(Dc[:, n % 2, :], m), halves(X[:, n % 2, :], m)
                        kk, qq = halves(k[:, i, :], m), halves(q[:, i, :], m)
                        first, second = (kk, qq) if d == 0 else (qq, kk)
                        pool.tensor_tensor(x[:, :, 0, :], first[:, :, 0, :], e[:, :, 0, :], ALU.mult).then_inc(x_done, 1)
                        pool.tensor_tensor(x[:, :, 1, :], second[:, :, 1, :], e[:, :, 1, :], ALU.mult).then_inc(x_done, 1)
                        n += 1
            for j, (d, i) in enumerate(DI):
                pool.wait_ge(e_done, NPAIR + j + 1)
                pool.wait_ge(unit_done, UNITS0 + 2 * NPAIR)
                if j >= 2:
                    pool.wait_ge(ke_turned, j - 1)
                pool.tensor_tensor(X[:, j % 2, :], k[:, i, :], Dc[:, j % 2, :], ALU.mult).then_inc(x_done, 1)

        @block.tensor
        def _(pe):
            pe.wait_ge(load["z"], 16)
            pe.wait_ge(load["w"], 32)
            for n, (d, i) in enumerate(DI):
                if n >= 2:
                    pe.wait_ge(min_done, n - 1)
                    pe.wait_ge(abs_done, n - 1)
                for t0, tn in FLAT:
                    mm = pe.matmul(UNIT[:, n % 2, t0:t0 + tn], wg[:, d, i * P:(i + 1) * P], z[:, t0:t0 + tn], start=True, stop=True)
                mm.then_inc(logits, 1)
            pe.wait_ge(load["v"], 16)
            g = 0
            for i in range(2):
                for c0 in range(0, TILES, 4):
                    if g >= 2:
                        pe.wait_ge(v_copied, g - 1)
                    for c in range(c0, min(c0 + 4, TILES)):
                        mm = pe.transpose(TR[:, g % 2, (c - c0) * P:(c - c0 + 1) * P], vT[:, i, c * P:(c + 1) * P], ident[:, :])
                    mm.then_inc(v_turned, 1)
                    g += 1
            pe.wait_ge(q_scaled, 2)
            pe.wait_ge(min_done, 4)
            pe.wait_ge(abs_done, 4)
            for i in range(2):
                for h in range(2):
                    if i:
                        pe.wait_ge(copied, 2 * i + h - 1)
                    rows = slice(64 * h, 64 * h + 64)
                    for c in range(NCH):
                        cols = slice(c * CH, (c + 1) * CH)
                        mm = pe.matmul(UNIT[:, h, cols], k[rows, i, cols], Qe[rows, i, cols], start=True, stop=True)
                    mm.then_inc(unit_done, 1)
            with pe.Fori(0, NPAIR // 2) as j:
                for s in range(2):
                    pe.wait_ge(x_done, j * 4 + 2 * s + 2)
                    for h in range(2):
                        pe.wait_ge(copied, j * 4 + 2 * s + h + UNITS0 - 1)
                        rows = slice(64 * h, 64 * h + 64)
                        for c in range(NCH):
                            cols = slice(c * CH, (c + 1) * CH)
                            mm = pe.matmul(UNIT[:, h, cols], X[rows, s, cols], X[rows, s, cols], start=True, stop=True)
                        mm.then_inc(unit_done, 1)
            pe.wait_ge(v_copied, 6)
            pe.wait_ge(copied, UNITS0 + 2 * NPAIR)
            g = 0
            for j, (d, i) in enumerate(DI):
                pe.wait_ge(x_done, 2 * NPAIR + j + 1)
                if j >= 2:
                    pe.wait_ge(ke_copied, j - 1)
                for c in range(NCH):
                    mm = pe.transpose(UNIT[:, j % 2, c * P:(c + 1) * P], X[:, j % 2, c * P:(c + 1) * P], ident[:, :])
                mm.then_inc(ke_turned, 1)
                pe.wait_ge(ke_copied, j + 1)
                order = ORDER[d][:-1]
                for c0 in range(0, len(order), 4):
                    if g >= 2:
                        pe.wait_ge(state, 2 * min_steps(g - 2))
                    for a, c in enumerate(order[c0:c0 + 4]):
                        mm = pe.matmul(TR[:, g % 2, a * P:(a + 1) * P], KeT[:, j % 2, c, :], V[:, c, i * P:(i + 1) * P], start=True, stop=True)
                    mm.then_inc(u_done, 1)
                    g += 1
            pe.wait_ge(qe_done, 4)
            pe.wait_ge(state, 2 * 4 * (NCH - 1))
            pe.wait_ge(ke_copied, 4)
            for i in range(2):
                for c in range(NCH):
                    cols = slice(c * CH, (c + 1) * CH)
                    pe.matmul(UNIT[:, i, cols], S[:, i, c, :], Qe[:, i, cols], start=True, stop=False, skip_group_check=True)
                    pe.matmul(UNIT[:, i, cols], S[:, 2 + i, c, :], Qe[:, 2 + i, cols], start=False, stop=True, skip_group_check=True)
                    for h in range(2):
                        mm = pe.matmul(UNIT[64 * h:64 * h + 64, i, cols], V[:, c, i * P + 64 * h:i * P + 64 * h + 64], A[:, i, h, c, :],
                                       start=False, stop=True, skip_group_check=True)
                mm.then_inc(o_done, 1)
            pe.wait_ge(load["bm"], 16)
            for i in range(2):
                pe.wait_ge(squared, i + 1)
                pe.wait_ge(o_copied, i + 1)
                for t0, tn in FLAT:
                    mm = pe.matmul(UNIT[:, i, t0:t0 + tn], block_mean[:, :], Dc[:, i, t0:t0 + tn], start=True, stop=True)
                mm.then_inc(mean_done, 1)

        @block.scalar
        def _(act):
            act.wait_ge(load["b"], 32)
            for n, (d, i) in enumerate(DI):
                act.wait_ge(logits, n + 1)
                if n >= 2:
                    act.wait_ge(gate_done, n - 1)
                x = Dc[:, n % 2, :]
                act.activation(x, UNIT[:, n % 2, 0:T], ACT.Abs, bias=bg[:, d, i:i + 1]).then_inc(abs_done, 1)
                act.wait_ge(abs_done, n + 1)
                act.activation(x, x, ACT.Exp, scale=-1.0).then_inc(exp_of_abs, 1)
                act.wait_ge(exp_of_abs, n + 1)
                act.activation(x, x, ACT.Ln, bias=1.0).then_inc(log_done, 1)
            g = 0
            for i in range(2):
                for c0 in range(0, TILES, 4):
                    n = min(4, TILES - c0)
                    act.wait_ge(v_turned, g + 1)
                    act.copy(V[:, c0:c0 + n, i * P:(i + 1) * P], TR[:, g % 2, 0:n * P].rearrange("p (c f) -> p c f", f=P)).then_inc(v_copied, 1)
                    g += 1
            for n in range(NPAIR + 4):
                act.wait_ge(d_done, 2 * n + 2 if n < NPAIR else 2 * NPAIR + (n - NPAIR) + 1)
                act.activation(Dc[:, n % 2, :], Dc[:, n % 2, :], ACT.Exp, scale=1.0 / GATE_NORM).then_inc(e_done, 1)
            for j, (d, i) in enumerate(DI):
                end = B[:, j, :].rearrange("p (c n) -> p c n", n=CH)[:, :, CH - 1 if d == 0 else 0]
                act.activation(dec[:, j, :], end, ACT.Exp, scale=1.0 / GATE_NORM).then_inc(dec_done, 1)
            act.wait_ge(unit_done, UNITS0)
            for j in range(4):
                act.activation(Qe[:, j, :], B[:, j, :], ACT.Exp, scale=1.0 / GATE_NORM).then_inc(qe_e, 1)
                act.wait_ge(ke_turned, j + 1)
                if j >= 2:
                    act.wait_ge(u_done, 3 * (j - 1))
                act.copy(KeT[:, j % 2, :, :], UNIT[:, j % 2, 0:T].rearrange("p (c f) -> p c f", f=P)).then_inc(ke_copied, 1)
            act.wait_ge(load["go"], 16)
            act.activation(vT[:, :, :], vT[:, :, :], ACT.Silu).then_inc(silu_done, 1)
            act.wait_ge(zeroed, 3)
            for i in range(2):
                act.wait_ge(o_done, i + 1)
                act.copy(X[:, i, :], UNIT[:, i, 0:T]).then_inc(o_copied, 1)
                act.activation(Dc[:, i, :], UNIT[:, i, 0:T], ACT.Square).then_inc(squared, 1)
            for i in range(2):
                act.wait_ge(mean_done, i + 1)
                act.activation(Dc[:, i, :], UNIT[:, i, 0:T], ACT.Sqrt, bias=eps[:, 0:1]).then_inc(rms_done, 1)

        @block.vector
        def _(dve):
            dve.memset(reset[:, :], 1.0).then_inc(reset_one, 1)
            dve.wait_ge(reset_one, 1)
            dve.memset(reset[:, :].rearrange("p (c n) -> p c n", n=CH)[:, :, 0:1], 0.0).then_inc(reset_set, 1)
            dve.wait_ge(reset_set, 1)
            dve.wait_ge(load["b"], 32)
            for n, (d, i) in enumerate(DI):
                dve.wait_ge(abs_done, n + 1)
                dve.tensor_scalar(B[:, n, :], UNIT[:, n % 2, 0:T], bg[:, d, i:i + 1], 0.0, ALU.add, ALU.min).then_inc(min_done, 1)
                dve.wait_ge(min_done, n + 1)
                dve.wait_ge(log_done, n + 1)
                if n >= 2:
                    dve.wait_ge(scanned, n - 1)
                dve.tensor_tensor(X[:, n % 2, :], B[:, n, :], Dc[:, n % 2, :], ALU.subtract).then_inc(gate_done, 1)
                dve.wait_ge(gate_done, n + 1)
                step = 1 if d == 0 else -1
                dve.tensor_tensor_scan(B[:, n, ::step], reset[:, :], X[:, n % 2, ::step], 0.0, ALU.mult, ALU.add).then_inc(scanned, 1)
            dve.wait_ge(load["q"], 16)
            dve.tensor_scalar(q[:, :, :], q[:, :, :], 64 ** -0.5, None, ALU.mult).then_inc(q_scaled, 1)
            dve.wait_ge(q_scaled, 1)
            dve.tensor_scalar(Qe[:, 0:2, :], q[:, :, :], 2.0, None, ALU.mult).then_inc(q_scaled, 1)
            dve.wait_ge(scanned, 4)
            dve.wait_ge(load["mask"], 16)
            dve.wait_ge(zeroed, 3)

            def distances(n):
                i, d, m = n // (2 * NL), n // NL % 2, LEVELS[n % NL]
                b = halves(B[:, 2 * d + i, :], m)
                x = halves(Dc[:, n % 2, :], m)
                nb = T // (2 * m)
                mid = (b[:, :, 0, m - 1:m] if d == 0 else b[:, :, 1, 0:1]).to_broadcast([P, nb, m])
                if n >= 2:
                    dve.wait_ge(x_done, 2 * (n - 1))
                lo, hi = (0, 1) if d == 0 else (1, 0)
                dve.tensor_tensor(x[:, :, lo, :], mid, b[:, :, lo, :], ALU.subtract).then_inc(d_done, 1)
                dve.tensor_tensor(x[:, :, hi, :], b[:, :, hi, :], mid, ALU.subtract).then_inc(d_done, 1)

            def take(unit, i, h, mask):
                dve.wait_ge(unit_done, unit + 1)
                dve.copy_predicated(A[:, i, h, :, :], masks[:, mask:mask + 1, :].to_broadcast([P, NCH, CH]),
                                    UNIT[:, h, 0:T].rearrange("p (c n) -> p c n", n=CH)).then_inc(copied, 1)

            distances(0)
            distances(1)
            for i in range(2):
                for h in range(2):
                    if i or h:
                        dve.wait_ge(copied, 2 * i + h)
                    take(2 * i + h, i, h, 2 * NL)
            for n in range(NPAIR):
                if n + 2 < NPAIR:
                    distances(n + 2)
                for h in range(2):
                    dve.wait_ge(copied, UNITS0 + 2 * n + h)
                    take(UNITS0 + 2 * n + h, n // (2 * NL), h, n % (2 * NL))
            for j, (d, i) in enumerate(DI):
                dve.wait_ge(x_done, 2 * (NPAIR - 1) + 2 + max(0, j - 1))
                b = B[:, j, :].rearrange("p (c n) -> p c n", n=CH)
                end = (b[:, :, CH - 1:CH] if d == 0 else b[:, :, 0:1]).to_broadcast([P, NCH, CH])
                dve.tensor_tensor(Dc[:, j % 2, :].rearrange("p (c n) -> p c n", n=CH), end, b, ALU.subtract).then_inc(d_done, 1)
            dve.wait_ge(dec_done, 4)
            g, n = 0, 0
            for j, (d, i) in enumerate(DI):
                order = ORDER[d]
                for c0 in range(0, NCH - 1, 4):
                    dve.wait_ge(u_done, g + 1)
                    for a in range(min(4, NCH - 1 - c0)):
                        c, nxt = order[c0 + a], order[c0 + a + 1]
                        if n:
                            dve.wait_ge(state, n)
                        for h in range(2):
                            r = slice(64 * h, 64 * h + 64)
                            dve.scalar_tensor_tensor(S[r, j, nxt, r], S[r, j, c, r], dec[r, j, c:c + 1],
                                                     TR[r, g % 2, a * P + 64 * h:a * P + 64 * h + 64], ALU.mult, ALU.add).then_inc(state, 1)
                        n += 2
                    g += 1
            for j, (d, i) in enumerate(DI):
                dve.wait_ge(qe_e, j + 1)
                dve.tensor_tensor(Qe[:, j, :], Qe[:, j, :], q[:, i, :], ALU.mult).then_inc(qe_done, 1)
            dve.wait_ge(silu_done, 1)
            dve.wait_ge(load["g"], 32)
            dve.tensor_scalar(vT[:, :, :], vT[:, :, :], normg[:, 0:1], None, ALU.mult).then_inc(gate_ready, 1)
            for i in range(2):
                dve.wait_ge(rms_done, i + 1)
                dve.reciprocal(Dc[:, i, :], Dc[:, i, :]).then_inc(inv_done, 1)
                dve.wait_ge(inv_done, i + 1)
                dve.tensor_tensor(X[:, i, :], X[:, i, :], Dc[:, i, :], ALU.mult).then_inc(normed, 1)
                dve.wait_ge(normed, i + 1)
                dve.wait_ge(gate_ready, 1)
                dve.tensor_tensor(X[:, i, :], X[:, i, :], vT[:, i, :], ALU.mult).then_inc(gated, 1)


def sliding_window_attention(nc, t, res, layer, tiles):
    with nc.cleanup_on_exit(), ExitStack() as ctx:
        sb, ps, sem = allocators(nc, ctx, f"swa{layer}_")
        nm = f"swa{layer}_"
        ident = res["ident"]
        H, G = SWA_HEADS, SWA_HEADS // 2
        UN = 2 * H
        first_pair, pairs = tiles[0] // 2, len(tiles) // 2
        khh = sb(nm + "khh", [P, 2, PAD_T], F32R)
        klo = sb(nm + "klo", [64, 2, PAD_T], F32R)
        qhl = sb(nm + "qhl", [P, 2, H, P], F32R)
        bias = sb(nm + "bias", [P, 2, 2 * P])
        vT = sb(nm + "vT", [P, PAD_T])
        V = sb(nm + "V", [P, TILES + 1, P])
        sink = sb(nm + "sink", [P, H])
        nsink = sb(nm + "nsink", [P, H])
        mx = sb(nm + "mx", [P, 2])
        neg = sb(nm + "negmax", [P, 2])
        den = sb(nm + "den", [P, 2])
        es = sb(nm + "esink", [P, 2])
        rden = sb(nm + "rden", [P, 4])
        den2 = sb(nm + "den2", [P, 2])
        pr = sb(nm + "p", [P, 2, SWA_KEYS])
        pT = sb(nm + "pT", [P, 2, SWA_KEYS])
        o = sb(nm + "o", [P, 2, H * SWA_DH])
        oT = sb(nm + "oT", [P, 2, G, P])
        SC = ps(nm + "scores", [P, 2, 2 * BANK])
        TR = ps(nm + "tr", [P, 2 * BANK])
        O = ps(nm + "o_acc", [P, 2, BANK])
        OT = TR[:, 0:BANK]
        const_in, k_in = sem("const_in"), sem("k_in")
        tile_in = [sem(f"tile_in{s}") for s in range(2)]
        nsink_done, v_turned, v_copied = sem("nsink_done"), sem("v_turned"), sem("v_copied")
        scores, masked, max_done, neg_done, exp_done, sink_done = (
            sem("scores"), sem("masked"), sem("max_done"), sem("neg_done"), sem("exp_done"), sem("sink_done"))
        den_done, rden_done, turned, copied, pv_done, o_done = (
            sem("den_done"), sem("rden_done"), sem("turned"), sem("copied"), sem("pv_done"), sem("o_done"))
        o_turned, o_copied = sem("o_turned"), sem("o_copied")
        stored = [sem(f"stored{s}") for s in range(2)]
        scale = SWA_DH ** -0.5
        block = ctx.enter_context(nc.Block())
        VG = [(0, 8), (8, 3)]

        def done(i, u):
            return (i - first_pair) * UN + u + 1

        def blocks(i, s):
            return (i - first_pair) * 2 + s + 1

        def is_ctx(i):
            return isinstance(i, int) and i == 0

        OUT_STEP = {H + 2: 0, UN + 1: 1}

        @block.sync
        def _(sp):
            heads = t["heads"]
            for half in range(2):
                sp.dma_start(khh[64 * half:64 * half + 64, :, :].bitcast(F32), heads[0, HEAD_SK:HEAD_SK + P, :].rearrange("(g p) n -> p g n", p=64)).then_inc(k_in, 16)
            sp.dma_start(klo[:, :, :].bitcast(F32), heads[1, HEAD_SK:HEAD_SK + P, :].rearrange("(g p) n -> p g n", p=64)).then_inc(k_in, 16)

            def body(i, first):
                for s in range(2):
                    if not first:
                        sp.wait_ge(scores, done(i, s * H + H - 1) - UN)
                        sp.wait_ge(max_done, done(i, s * H + H - 1) - UN)
                    at = i * 2 * P + s * P
                    for part in range(2):
                        sp.dma_start(qhl[64 * part:64 * part + 64, s, :, :].bitcast(F32),
                                     heads[part, HEAD_SQ:HEAD_SQ + G * P, bass.ds(at, P)].rearrange("(a p) n -> p a n", p=64)).then_inc(tile_in[s], 16)
                    sp.dma_start(bias[:, s, :], t["swa_bias"][bass.ds(0 if is_ctx(i) else at - N_CTX, P), :]).then_inc(tile_in[s], 16)
            peeled(sp, first_pair, first_pair + pairs, body)

        @block.gpsimd
        def _(pool):
            pool.dma_start(vT[:, :], t["proj"][T_SV * P:(T_SV + 1) * P, :]).then_inc(const_in, 16)
            pool.dma_start(sink[:, :], t["swa_sink"][layer:layer + 1, :].to_broadcast([P, H])).then_inc(const_in, 16)
            pool.wait_ge(const_in, 32)

        @block.tensor
        def _(pe):
            pe.wait_ge(const_in, 32)
            for g, (a, n) in enumerate(VG):
                if g:
                    pe.wait_ge(v_copied, g)
                for c in range(n):
                    mm = pe.transpose(TR[:, c * P:(c + 1) * P], vT[:, (a + c) * P:(a + c + 1) * P], ident[:, :])
                mm.then_inc(v_turned, 1)
            pe.wait_ge(v_copied, 2)
            pe.wait_ge(k_in, 48)

            def body(i, first):
                kt = 2 if is_ctx(i) else 5

                def score(u):
                    s, h = u // H, u % H
                    g, j = h // G, h % G
                    if h == 0:
                        pe.wait_ge(tile_in[s], (i - first_pair) * 48 + 48)
                    if not (first and u < 2):
                        pe.wait_ge(exp_done, done(i, u) - 2)
                    parts = [(slice(0, N_CTX), slice(0, N_CTX))]
                    if kt == 5:
                        at = i * 2 * P + (s - 1) * P
                        parts += [(slice(N_CTX, BANK), bass.ds(at, 2 * P)), (slice(BANK, BANK + P), bass.ds(at + 2 * P, P))]
                    for cols, keys in parts:
                        pe.matmul(SC[:, u % 2, cols], qhl[:, s, 2 * j + g, :], khh[:, g, keys], start=True, stop=False)
                        mm = pe.matmul(SC[:, u % 2, cols], qhl[0:64, s, 2 * j + g, :], klo[:, g, keys], start=False, stop=True)
                    mm.then_inc(scores, 1)

                def turn(u):
                    pe.wait_ge(exp_done, done(i, u))
                    if not (first and u == 0):
                        pe.wait_ge(copied, done(i, u) - 1)
                    if u == 0 and not first:
                        pe.wait_ge(o_copied, blocks(i, 0) - 1)
                    if u == H + 2:
                        pe.wait_ge(o_copied, blocks(i, 0))
                    for c in range(kt):
                        mm = pe.transpose(TR[:, c * P:(c + 1) * P], pr[:, u % 2, c * P:(c + 1) * P], ident[:, :])
                    mm.then_inc(turned, 1)

                def weigh(u):
                    s, h = u // H, u % H
                    pe.wait_ge(copied, done(i, u))
                    if not (first and u < 2):
                        pe.wait_ge(o_done, done(i, u) - 2)
                    vcols = slice(64 * (h // G), 64 * (h // G) + 64)
                    for c in range(kt):
                        v = V[:, c, vcols] if c < 2 else V[:, bass.ds(i * 2 + (s - 1 + c - 2), 1), vcols].rearrange("p a b -> p (a b)")
                        mm = pe.matmul(O[:, u % 2, 0:64], pT[:, u % 2, c * P:(c + 1) * P], v, start=(c == 0), stop=(c == kt - 1))
                    mm.then_inc(pv_done, 1)

                for step in range(UN + 2):
                    if step < UN:
                        score(step)
                    if 1 <= step < UN + 1:
                        turn(step - 1)
                    if step >= 2:
                        weigh(step - 2)
                    if step in OUT_STEP:
                        s = OUT_STEP[step]
                        pe.wait_ge(o_done, done(i, s * H + H - 1))
                        pe.wait_ge(copied, done(i, min(step - 1, UN - 1)))
                        for g in range(G):
                            mm = pe.transpose(OT[:, g * P:(g + 1) * P], o[:, s, g * P:(g + 1) * P], ident[:, :])
                        mm.then_inc(o_turned, 1)
            peeled(pe, first_pair, first_pair + pairs, body)

        @block.scalar
        def _(act):
            for g, (a, n) in enumerate(VG):
                act.wait_ge(v_turned, g + 1)
                act.copy(V[:, a:a + n, :], TR[:, 0:n * P].rearrange("p (c f) -> p c f", f=P)).then_inc(v_copied, 1)
            act.wait_ge(const_in, 32)

            def body(i, first):
                keys = N_CTX if is_ctx(i) else SWA_KEYS
                for step in range(UN + 2):
                    if step < UN:
                        u, b = step, step % 2
                        act.wait_ge(neg_done, done(i, u))
                        if not (first and u < 2):
                            act.wait_ge(turned, done(i, u) - 2)
                            act.wait_ge(den_done, done(i, u) - 2)
                        act.activation(pr[:, b, 0:keys], SC[:, b, 0:keys], ACT.Exp, bias=neg[:, b:b + 1],
                                       scale=scale, accum_out=den[:, b:b + 1]).then_inc(exp_done, 1)
                        act.activation(es[:, b:b + 1], sink[:, u % H:u % H + 1], ACT.Exp, bias=neg[:, b:b + 1]).then_inc(sink_done, 1)
                    if 1 <= step < UN + 1:
                        u = step - 1
                        act.wait_ge(turned, done(i, u))
                        if not (first and u < 2):
                            act.wait_ge(pv_done, done(i, u) - 2)
                        act.copy(pT[:, u % 2, 0:keys], TR[:, 0:keys]).then_inc(copied, 1)
                    if step in OUT_STEP:
                        s = OUT_STEP[step]
                        act.wait_ge(o_turned, blocks(i, s))
                        if not first:
                            act.wait_ge(stored[s], (i - first_pair) * 16)
                        act.copy(oT[:, s, :, :], OT.rearrange("p (g n) -> p g n", g=G)).then_inc(o_copied, 1)
                        act.wait_ge(o_copied, blocks(i, s))
                        act.dma_start(t["mix"][4 * P:D, bass.ds(i * 2 * P + s * P, P)].rearrange("(g p) n -> p g n", p=P), oT[:, s, :, :]).then_inc(stored[s], 16)
            peeled(act, first_pair, first_pair + pairs, body)
            for s in range(2):
                act.wait_ge(stored[s], 16 * pairs)

        @block.vector
        def _(dve):
            dve.wait_ge(const_in, 32)
            dve.tensor_scalar(nsink[:, :], sink[:, :], -1.0, None, ALU.mult).then_inc(nsink_done, 1)
            dve.wait_ge(nsink_done, 1)

            def body(i, first):
                for step in range(UN + 2):
                    if step < UN:
                        u, b = step, step % 2
                        s, h = u // H, u % H
                        if h == 0:
                            dve.wait_ge(tile_in[s], (i - first_pair) * 48 + 48)
                        dve.wait_ge(scores, done(i, u))
                        keys = N_CTX
                        if not is_ctx(i):
                            keys = SWA_KEYS
                            for a, c in ((0, N_CTX), (P, BANK)):
                                dve.tensor_tensor(SC[:, b, c:c + P], SC[:, b, c:c + P], bias[:, s, a:a + P], ALU.add).then_inc(masked, 1)
                            dve.wait_ge(masked, (done(i, u) if first_pair else done(i, u) - UN) * 2)
                        dve.reduce_max(mx[:, b:b + 1], SC[:, b, 0:keys], AX.X).then_inc(max_done, 1)
                        dve.wait_ge(max_done, done(i, u))
                        dve.scalar_tensor_tensor(neg[:, b:b + 1], mx[:, b:b + 1], -scale, nsink[:, h:h + 1], ALU.mult, ALU.min).then_inc(neg_done, 1)
                    if 1 <= step < UN + 1:
                        u, b = step - 1, (step - 1) % 2
                        dve.wait_ge(sink_done, done(i, u))
                        dve.tensor_tensor(den2[:, b:b + 1], den[:, b:b + 1], es[:, b:b + 1], ALU.add).then_inc(den_done, 1)
                        dve.wait_ge(den_done, done(i, u))
                        dve.reciprocal(rden[:, u % 4:u % 4 + 1], den2[:, b:b + 1]).then_inc(rden_done, 1)
                    if step >= 2:
                        u = step - 2
                        s, h = u // H, u % H
                        dve.wait_ge(pv_done, done(i, u))
                        dve.wait_ge(rden_done, done(i, u))
                        if not first and h == 0:
                            dve.wait_ge(o_turned, blocks(i, s) - 2)
                        dve.tensor_scalar(o[:, s, 64 * h:64 * h + 64], O[:, u % 2, 0:64], rden[:, u % 4:u % 4 + 1], None, ALU.mult).then_inc(o_done, 1)
            peeled(dve, first_pair, first_pair + pairs, body)


def differential_attention(nc, t, res, layer, tiles):
    with nc.cleanup_on_exit(), ExitStack() as ctx:
        sb, ps, sem = allocators(nc, ctx, f"diff{layer}_")
        nm = f"diff{layer}_"
        ident = res["ident"]
        H = DIFF_HEADS
        UN = 2 * H
        LAG = 3
        lam_init = 0.8 - 0.6 * math.exp(-0.3 * layer)
        scale = DIFF_DH ** -0.5
        first_pair, end_pair = tiles[0] // 2, tiles[-1] // 2 + 1
        first_latent = CTX_TILES // 2
        KEYCH = [(0, 512), (512, 512), (1024, 256)]
        t0, tn = tiles[0] * P, len(tiles) * P
        ks = sb(nm + "k", [96, UN, T], F32R)
        qs = sb(nm + "q", [96, 2, UN, P], F32R)
        vT = sb(nm + "vT", [P, 2, T])
        V = sb(nm + "V", [P, TILES, 2 * P])
        lamv = sb(nm + "lamv", [P, 4, DIFF_DH])
        lprod = sb(nm + "lprod", [P, 2, DIFF_DH])
        lsum = sb(nm + "lsum", [P, 2])
        lexp = sb(nm + "lexp", [P, 2])
        ldiff = sb(nm + "ldiff", [P, 1])
        nlam = sb(nm + "nlam", [P, 1])
        g1 = sb(nm + "g", [P, 1])
        block_mean = sb(nm + "block_mean", [P, P])
        eps = sb(nm + "eps", [P, 1])
        mx = sb(nm + "mx", [P, 2])
        ng = sb(nm + "negmax", [P, 2])
        den = sb(nm + "den", [P, 2, 2])
        rden = sb(nm + "rden", [P, 2, 2])
        r1 = sb(nm + "r1", [P, 2])
        E = sb(nm + "e", [P, 2, 2, T])
        W = sb(nm + "w", [P, 2, T])
        WT = sb(nm + "wT", [P, 2, T])
        oT = sb(nm + "oT", [P, 2, T])
        SC = ps(nm + "scores", [P, 2, 3 * BANK])
        TR = ps(nm + "tr", [P, 2, BANK])
        const_in, k_in, eps_set = sem("const_in"), sem("k_in"), sem("eps_set")
        q_in = [sem(f"q_in{s}") for s in range(2)]
        lam, lam_exp = sem("lam"), sem("lam_exp")
        v_turned, v_copied = sem("v_turned"), sem("v_copied")
        scores, max_done, neg_done, exp_done, rden_done, r1_done, w0_done, w_done = (
            sem("scores"), sem("max_done"), sem("neg_done"), sem("exp_done"), sem("rden_done"), sem("r1_done"), sem("w0_done"), sem("w_done"))
        turned = [sem(f"turned{g}") for g in range(3)]
        copied = [sem(f"copied{g}") for g in range(3)]
        pv_done, o_done, passed = sem("pv_done"), sem("o_done"), sem("passed")
        sq_done, mean_done, rms_done, inv_done, normed, stored = (
            sem("sq_done"), sem("mean_done"), sem("rms_done"), sem("inv_done"), sem("normed"), sem("stored"))
        block = ctx.enter_context(nc.Block())
        VG = [(i, a, min(4, TILES - a)) for i in range(2) for a in range(0, TILES, 4)]
        units = (end_pair - first_pair) * UN

        def done(i, u):
            return (i - first_pair) * UN + u + 1

        def is_ctx(i):
            return isinstance(i, int) and i == 0

        def groups(i):
            return [(0, 1), (1, 1)] if is_ctx(i) else [(0, 3), (3, 4), (7, 3)]

        def third(i, u):
            return done(i, u) - (first_latent - first_pair) * UN

        def stagger(eng, step):
            if first_pair < first_latent:
                staggered(eng, first_pair, first_latent, UN, LAG, step)
            staggered(eng, first_latent, end_pair, UN, LAG, step)

        @block.sync
        def _(sp):
            heads = t["heads"]
            for j, part in enumerate((0, 1, 0)):
                sp.dma_start(ks[32 * j:32 * j + 32, :, :].bitcast(F32), heads[part, HEAD_DK:HEAD_DK + 2 * P, 0:T].rearrange("(a p) n -> p a n", p=32)).then_inc(k_in, 16)

            def body(i, first):
                for s in range(2):
                    if not first:
                        sp.wait_ge(scores, 2 * (done(i, s * H + H - 1) - UN))
                    for j, part in enumerate((0, 0, 1)):
                        sp.dma_start(qs[32 * j:32 * j + 32, s, :, :].bitcast(F32),
                                     heads[part, HEAD_DQ:HEAD_DQ + 2 * P, bass.ds(i * 2 * P + s * P, P)].rearrange("(a p) n -> p a n", p=32)).then_inc(q_in[s], 16)
            peeled(sp, first_pair, end_pair, body)
            for i in range(2):
                sp.wait_ge(normed, i + 1)
                sp.dma_start(t["mix"][(2 + i) * P:(3 + i) * P, t0:t0 + tn], oT[:, i, t0:t0 + tn]).then_inc(stored, 16)
            sp.wait_ge(stored, 32)

        @block.tensor
        def _(pe):
            pe.wait_ge(const_in, 80)
            for g, (i, a, n) in enumerate(VG):
                if g >= 2:
                    pe.wait_ge(v_copied, g - 1)
                for c in range(n):
                    mm = pe.transpose(TR[:, g % 2, c * P:(c + 1) * P], vT[:, i, (a + c) * P:(a + c + 1) * P], ident[:, :])
                mm.then_inc(v_turned, 1)
            pe.wait_ge(v_copied, len(VG))
            pe.wait_ge(k_in, 48)

            def turn(i, u, g):
                a, n = groups(i)[g]
                for c in range(n):
                    mm = pe.transpose(TR[:, g % 2, c * P:(c + 1) * P], W[:, u % 2, (a + c) * P:(a + c + 1) * P], ident[:, :])
                mm.then_inc(turned[g], 1)

            def step(i, r, live):
                if live(0):
                    s, h = r // H, r % H
                    if h == 0:
                        pe.wait_ge(q_in[s], (i - first_pair) * 48 + 48)
                    for c in range(2):
                        wait_count(pe, exp_done, 2 * (done(i, r) - 1) + c - 1)
                        for a, n in KEYCH[:1 if is_ctx(i) else 3]:
                            n = min(n, N_CTX) if is_ctx(i) else n
                            mm = pe.matmul(SC[:, c, a:a + n], qs[:, s, 2 * h + c, :], ks[:, 2 * h + c, a:a + n], start=True, stop=True)
                        mm.then_inc(scores, 1)
                if live(2):
                    u = r - 2
                    wait_count(pe, o_done, done(i, u) - (1 if live.starts and u == 0 else 2))
                    turn(i, u, 1)
                    if not is_ctx(i):
                        pe.wait_ge(copied[0], done(i, u))
                        turn(i, u, 2)
                if live(3):
                    u, h = r - 3, (r - 3) % H
                    pe.wait_ge(copied[1], done(i, u) + (1 if live(2) else 0))
                    wait_count(pe, o_done, done(i, u) - 1)
                    if not is_ctx(i):
                        pe.wait_ge(copied[2], third(i, u))
                    tiles_ = groups(i)[-1][0] + groups(i)[-1][1]
                    for c in range(tiles_):
                        mm = pe.matmul(TR[64 * (h % 2):64 * (h % 2) + 64, 1, 0:P], V[:, c, 64 * h:64 * h + 64],
                                       WT[:, u % 2, c * P:(c + 1) * P], start=(c == 0), stop=(c == tiles_ - 1))
                    mm.then_inc(pv_done, 1)
                if live(1):
                    u = r - 1
                    pe.wait_ge(w_done, done(i, u))
                    wait_count(pe, copied[0], done(i, u) - 1)
                    if not is_ctx(i):
                        wait_count(pe, copied[2], third(i, u) - 1)
                    turn(i, u, 0)
            stagger(pe, step)

            for i in range(2):
                pe.wait_ge(sq_done, i + 1)
                for a, n in KEYCH:
                    n = min(n, tn - a)
                    if n > 0:
                        mm = pe.matmul(SC[:, i, a:a + n], block_mean[:, :], E[:, 0, i, a:a + n], start=True, stop=True)
                mm.then_inc(mean_done, 1)

        @block.scalar
        def _(act):
            for g, (i, a, n) in enumerate(VG):
                act.wait_ge(v_turned, g + 1)
                act.copy(V[:, a:a + n, i * P:(i + 1) * P], TR[:, g % 2, 0:n * P].rearrange("p (c f) -> p c f", f=P)).then_inc(v_copied, 1)
            act.wait_ge(lam, 4)
            act.activation(lexp[:, :], lsum[:, :], ACT.Exp).then_inc(lam_exp, 1)
            act.wait_ge(eps_set, 1)

            def step(i, r, live):
                keys = (CTX_TILES if is_ctx(i) else TILES) * P

                def exponentials(c):
                    act.wait_ge(neg_done, 2 * (done(i, r) - 1) + c + 1)
                    if c == 0:
                        wait_count(act, w_done, done(i, r) - 2)
                    act.activation(E[:, r % 2, c, 0:keys], SC[:, c, 0:keys], ACT.Exp, bias=ng[:, c:c + 1], scale=scale,
                                   accum_out=den[:, r % 2, c:c + 1]).then_inc(exp_done, 1)

                def take(u, g):
                    a, n = groups(i)[g]
                    act.wait_ge(turned[g], third(i, u) if g == 2 else done(i, u))
                    if g == 0:
                        wait_count(act, pv_done, done(i, u) - 2)
                    act.copy(WT[:, u % 2, a * P:(a + n) * P], TR[:, g % 2, 0:n * P]).then_inc(copied[g], 1)

                if live(2):
                    take(r - 2, 1)
                if live(0):
                    exponentials(0)
                if live(2) and not is_ctx(i):
                    take(r - 2, 2)
                if live(0):
                    exponentials(1)
                if live(1):
                    take(r - 1, 0)
            stagger(act, step)

            act.wait_ge(o_done, units)
            act.wait_ge(w_done, units)
            for i in range(2):
                act.activation(E[:, 0, i, 0:tn], oT[:, i, t0:t0 + tn], ACT.Square).then_inc(sq_done, 1)
            for i in range(2):
                act.wait_ge(mean_done, i + 1)
                act.activation(E[:, 1, i, 0:tn], SC[:, i, 0:tn], ACT.Sqrt, bias=eps[:, 0:1]).then_inc(rms_done, 1)

        @block.gpsimd
        def _(pool):
            pool.dma_start(vT[:, :, :], t["proj"][T_DV * P:(T_DV + 2) * P, 0:T].rearrange("(i p) n -> p i n", p=P)).then_inc(const_in, 16)
            pool.dma_start(lamv[:, :, :].rearrange("p a b -> p (a b)"), t["diff_lambda"][layer:layer + 1, :, :].rearrange("l a b -> l (a b)").to_broadcast([P, 4 * DIFF_DH])).then_inc(const_in, 16)
            for h in range(2):
                pool.dma_start(g1[h * 64:(h + 1) * 64, :], t["diff_norm_g"][layer].rearrange("(p a) -> p a", a=1)).then_inc(const_in, 16)
            pool.dma_start(block_mean[:, :], t["block_mean"]).then_inc(const_in, 16)
            pool.memset(eps[:, :], EPS).then_inc(eps_set, 1)
            pool.wait_ge(const_in, 80)

            def step(i, r, live):
                keys = (CTX_TILES if is_ctx(i) else TILES) * P
                if live(1):
                    u = r - 1
                    if is_ctx(i) or (live.starts and u < 2):
                        wait_count(pool, turned[1], done(i, u) - 2)
                    else:
                        pool.wait_ge(turned[2], third(i, u) - 2)
                    wait_apart(pool, rden_done, done(i, u), passed)
                    pool.tensor_scalar(W[:, u % 2, 0:keys], E[:, u % 2, 0, 0:keys], rden[:, u % 2, 0:1], 1.0, ALU.mult, ALU.mult).then_inc(w0_done, 1)
            stagger(pool, step)

        @block.vector
        def _(dve):
            dve.wait_ge(const_in, 80)
            for a in range(2):
                dve.tensor_tensor(lprod[:, a, :], lamv[:, 2 * a, :], lamv[:, 2 * a + 1, :], ALU.mult).then_inc(lam, 1)
            dve.tensor_scalar(g1[:, :], g1[:, :], 1.0 - lam_init, None, ALU.mult).then_inc(lam, 1)
            dve.wait_ge(lam, 3)
            dve.reduce_sum(lsum[:, :], lprod[:, :, :], AX.X).then_inc(lam, 1)
            dve.wait_ge(lam_exp, 1)
            dve.tensor_tensor(ldiff[:, :], lexp[:, 1:2], lexp[:, 0:1], ALU.subtract).then_inc(lam, 1)
            dve.wait_ge(lam, 5)
            dve.tensor_scalar(nlam[:, :], ldiff[:, :], -lam_init, None, ALU.add).then_inc(lam, 1)
            dve.wait_ge(lam, 6)

            def step(i, r, live):
                keys = (CTX_TILES if is_ctx(i) else TILES) * P
                for c in range(2):
                    if live(0):
                        n = 2 * (done(i, r) - 1) + c + 1
                        dve.wait_ge(scores, n)
                        dve.reduce_max(mx[:, c:c + 1], SC[:, c, 0:keys], AX.X).then_inc(max_done, 1)
                        dve.wait_ge(max_done, n)
                        dve.tensor_scalar(ng[:, c:c + 1], mx[:, c:c + 1], -scale, None, ALU.mult).then_inc(neg_done, 1)
                    if live(1) and c == 0:
                        u, b = r - 1, (r - 1) % 2
                        dve.wait_ge(exp_done, 2 * done(i, u))
                        dve.reciprocal(rden[:, b, :], den[:, b, :]).then_inc(rden_done, 1)
                        dve.wait_ge(rden_done, done(i, u))
                        dve.tensor_scalar(r1[:, b:b + 1], rden[:, b, 1:2], nlam[:, 0:1], None, ALU.mult).then_inc(r1_done, 1)
                if live(1):
                    u, b = r - 1, (r - 1) % 2
                    dve.wait_ge(w0_done, done(i, u))
                    dve.wait_ge(r1_done, done(i, u))
                    dve.scalar_tensor_tensor(W[:, b, 0:keys], E[:, b, 1, 0:keys], r1[:, b:b + 1], W[:, b, 0:keys], ALU.mult, ALU.add).then_inc(w_done, 1)
                if live(3):
                    u = r - 3
                    h, rows = u % H, slice(64 * (u % 2), 64 * (u % 2) + 64)
                    dve.wait_ge(pv_done, done(i, u))
                    dve.tensor_copy(oT[rows, h // 2, bass.ds(i * 2 * P + u // H * P, P)], TR[rows, 1, 0:P]).then_inc(o_done, 1)
            stagger(dve, step)

            for i in range(2):
                o = oT[:, i, t0:t0 + tn]
                dve.wait_ge(rms_done, i + 1)
                dve.reciprocal(E[:, 1, i, 0:tn], E[:, 1, i, 0:tn]).then_inc(inv_done, 1)
                dve.wait_ge(inv_done, i + 1)
                dve.scalar_tensor_tensor(o, o, g1[:, 0:1], E[:, 1, i, 0:tn], ALU.mult, ALU.mult).then_inc(normed, 1)


def swiglu(nc, t, res, layer, chunks):
    with nc.cleanup_on_exit(), ExitStack() as ctx:
        sb, ps, sem = allocators(nc, ctx, f"ffn{layer}_")
        nm = f"ffn{layer}_"
        uhi, ulo, Y = res["uhi"], res["ulo"], res["y"]
        NC = len(chunks)
        order = [tt for t0, tn in chunks for tt in range(t0 // P, (t0 + tn) // P)]
        chunk_of = {tt: c for c, (t0, tn) in enumerate(chunks) for tt in range(t0 // P, (t0 + tn) // P)}
        NY = 2 * len(order)
        raw = sb(nm + "raw", [P, 3, D])
        whi = sb(nm + "whi", [P, 3, D], F32R)
        wlo = sb(nm + "wlo", [P, 3, D], F32R)
        sg = sb(nm + "silu", [P, NC, BANK])
        hf = sb(nm + "hid", [P, NC, BANK])
        hhi = sb(nm + "hhi", [P, 2, T], F32R)
        hlo = sb(nm + "hlo", [P, 2, T], F32R)
        GT = ps(nm + "gate", [P, 3, BANK])
        UP = ps(nm + "up", [P, 3, BANK])
        ACC = ps(nm + "acc", [P, 2, BANK])
        raw_in = [sem(f"raw_in{s}") for s in range(3)]
        passed = sem("passed")
        w_hi, w_ready = sem("w_hi"), sem("w_ready")
        gate_done, up_done, silu_done, mul_done = sem("gate_done"), sem("up_done"), sem("silu_done"), sem("mul_done")
        hid_hi, hid_ready, y_done, y_added, y_zero = sem("hid_hi"), sem("hid_ready"), sem("y_done"), sem("y_added"), sem("y_zero")
        block = ctx.enter_context(nc.Block())
        G = FFN_GROUPS

        def grouped(eng, body):
            body(0, True, False)
            with eng.Fori(1, G - 1) as g:
                body(g, False, False)
            body(G - 1, False, True)

        @block.sync
        def _(sp):
            def body(g, first, last):
                for j in range(6):
                    if not (first and j < 3):
                        sp.wait_ge(w_ready, g * 6 + j - 2)
                    sp.dma_start(raw[:, j % 3, :], t["w_ffn"][layer][bass.ds(g * 6 * P + j * P, P), :]).then_inc(raw_in[j % 3], 16)
            grouped(sp, body)

        def release(eng, g, j):
            if j == 0:
                eng.wait_ge(up_done, g * 2 * NC)
            elif j in (1, 2):
                eng.wait_ge(y_done, g * NY)
            elif j == 3:
                eng.wait_ge(gate_done, g * 2 * NC + NC)
            elif j == 4:
                eng.wait_ge(up_done, g * 2 * NC + NC)
            else:
                eng.wait_ge(gate_done, g * 2 * NC + 2 * NC)

        @block.scalar
        def _(act):
            def split(g, j, reused=True):
                if reused:
                    release(act, g, j)
                act.wait_ge(raw_in[j % 3], g * 32 + (j // 3) * 16 + 16)
                act.copy(whi[:, j % 3, :], raw[:, j % 3, :]).then_inc(w_hi, 1)

            def silu(g, f, first):
                for c, (t0, tn) in enumerate(chunks):
                    n = g * 2 * NC + f * NC + c
                    act.wait_ge(gate_done, n + 1)
                    if not (first and f == 0):
                        act.wait_ge(mul_done, n + 1 - NC)
                    act.activation(sg[:, c, 0:tn], GT[:, c, 0:tn], ACT.Silu).then_inc(silu_done, 1)

            def body(g, first, last):
                silu(g, 0, first)
                split(g, 3)
                split(g, 4)
                silu(g, 1, first)
                split(g, 5)
                if not last:
                    for j in range(3):
                        split(g + 1, j)
            for j in range(3):
                split(0, j, False)
            grouped(act, body)

        @block.gpsimd
        def _(pool):
            pool.memset(Y[:, :, :], 0.0).then_inc(y_zero, 1)

            def split(g, j):
                pool.wait_ge(w_hi, g * 6 + j + 1)
                pool.tensor_tensor(wlo[:, j % 3, :], raw[:, j % 3, :], whi[:, j % 3, :].bitcast(F32), ALU.subtract).then_inc(w_ready, 1)

            def hidden(g, f):
                for c, (t0, tn) in enumerate(chunks):
                    n = g * 2 * NC + f * NC + c + 1
                    wait_apart(pool, mul_done, n, passed)
                    pool.tensor_copy(hhi[:, f, t0:t0 + tn], hf[:, c, 0:tn]).then_inc(hid_hi, 1)
                    pool.wait_ge(hid_hi, n)
                    pool.tensor_tensor(hlo[:, f, t0:t0 + tn], hf[:, c, 0:tn], hhi[:, f, t0:t0 + tn].bitcast(F32), ALU.subtract).then_inc(hid_ready, 1)

            def body(g, first, last):
                split(g, 3)
                hidden(g, 0)
                split(g, 4)
                split(g, 5)
                hidden(g, 1)
                if not last:
                    for j in range(3):
                        split(g + 1, j)
            for j in range(3):
                split(0, j)
            grouped(pool, body)

        @block.tensor
        def _(pe):
            def body(g, first, last):
                for f in range(2):
                    for which, (bank, done, freed) in enumerate(((GT, gate_done, silu_done), (UP, up_done, mul_done))):
                        j = 2 * f + which
                        w = [x[:, j % 3, :].rearrange("p (k n) -> p k n", k=KT) for x in (whi, wlo)]
                        pe.wait_ge(w_ready, g * 6 + j + 1)
                        for c, (t0, tn) in enumerate(chunks):
                            if not (first and f == 0):
                                pe.wait_ge(freed, g * 2 * NC + f * NC + c + 1 - NC)
                            for k in range(KT):
                                mm = product(pe, bank[:, c, 0:tn], w[0][:, k, :], w[1][:, k, :],
                                             uhi[:, k, t0:t0 + tn], ulo[:, k, t0:t0 + tn], k == 0, k == KT - 1)
                            mm.then_inc(done, 1)
                pe.wait_ge(w_ready, g * 6 + 6)
                for n, tt in enumerate(order):
                    pe.wait_ge(hid_ready, g * 2 * NC + NC + chunk_of[tt] + 1)
                    for half in range(2):
                        if not (first and n == 0):
                            pe.wait_ge(y_added, g * NY + 2 * n + half - 1)
                        cols, rows = slice(half * BANK, (half + 1) * BANK), slice(tt * P, (tt + 1) * P)
                        for f in range(2):
                            s = (4 + f) % 3
                            mm = product(pe, ACC[:, half, :], hhi[:, f, rows], hlo[:, f, rows],
                                         whi[:, s, cols], wlo[:, s, cols], f == 0, f == 1)
                        mm.then_inc(y_done, 1)
            grouped(pe, body)

        @block.vector
        def _(dve):
            dve.wait_ge(y_zero, 1)

            def body(g, first, last):
                for f in range(2):
                    for c, (t0, tn) in enumerate(chunks):
                        n = g * 2 * NC + f * NC + c + 1
                        dve.wait_ge(silu_done, n)
                        dve.wait_ge(up_done, n)
                        if not (first and f == 0):
                            dve.wait_ge(hid_ready, n - NC)
                        dve.tensor_tensor(hf[:, c, 0:tn], UP[:, c, 0:tn], sg[:, c, 0:tn], ALU.mult).then_inc(mul_done, 1)
                for n, tt in enumerate(order):
                    for half in range(2):
                        cols = slice(half * BANK, (half + 1) * BANK)
                        dve.wait_ge(y_done, g * NY + 2 * n + half + 1)
                        dve.tensor_tensor(Y[:, tt, cols], ACC[:, half, :], Y[:, tt, cols], ALU.add).then_inc(y_added, 1)
            grouped(dve, body)


def build(nc, t):
    with ExitStack() as outer:
        outer.enter_context(nc.allow_non_contiguous_dma(reason="columns of modulation and gate biases: a few KB"))
        ident = outer.enter_context(nc.sbuf_tensor("ident", [P, P], F32))
        res = {"ident": ident}
        with nc.cleanup_on_exit(), ExitStack() as ctx:
            ident_in = nc.alloc_semaphore("ident_in")
            block = ctx.enter_context(nc.Block())

            @block.sync
            def _(sp):
                sp.dma_start(ident[:, :], t["ident"]).then_inc(ident_in, 16)
                sp.wait_ge(ident_in, 16)

        def operand(ctx, name):
            res["uhi"] = ctx.enter_context(nc.sbuf_tensor(name + "_uhi", [P, KT, T], F32R))
            res["ulo"] = ctx.enter_context(nc.sbuf_tensor(name + "_ulo", [P, KT, T], F32R))

        everything = list(range(TILES))
        modulation(nc, t)
        for layer in range(LAYERS):
            last = layer == LAYERS - 1
            tiles = everything[CTX_TILES:] if last else everything
            if layer == 0:
                with ExitStack() as ctx:
                    operand(ctx, "first")
                    norm_tiles(nc, t, res, "input", layer, everything, False)
                    input_projection(nc, t, res, layer)
            gated_linear_attention(nc, t, res, layer)
            differential_attention(nc, t, res, layer, tiles)
            sliding_window_attention(nc, t, res, layer, tiles)
            with ExitStack() as ctx:
                operand(ctx, f"second{layer}")
                norm_tiles(nc, t, res, "attention", layer, tiles, False)
                with ExitStack() as inner:
                    res["y"] = inner.enter_context(nc.sbuf_tensor(f"y{layer}", [P, TILES, D], F32))
                    swiglu(nc, t, res, layer, LAT_CHUNKS if last else CHUNKS)
                    norm_tiles(nc, t, res, "ffn", layer, tiles, last)
                if not last:
                    input_projection(nc, t, res, layer + 1)


def constants():
    import numpy as np
    f = np.float32
    out = {"ident": np.eye(P, dtype=f)}
    bm = np.zeros((P, P), f)
    bm[:64, :64] = bm[64:, 64:] = 1.0 / 64
    out["block_mean"] = bm
    grid_w, base = 64, 10000.0
    rows = N_LAT // grid_w
    row = np.repeat(np.arange(rows, dtype=f), grid_w)
    col = np.tile(np.arange(grid_w, dtype=f), rows)
    cos, sin = np.zeros((2, P, N_LAT), f), np.zeros((2, P, N_LAT), f)
    for which, dim in enumerate((DIFF_DH, SWA_DH)):
        nf = dim // 4
        inv = np.power(f(base), -np.arange(nf, dtype=f) / f(nf)).astype(f)
        ang = np.concatenate([row[:, None] * inv, col[:, None] * inv], axis=-1)
        for p in range(P):
            r = p % 32
            j = r % 16 + (16 * (p // 32 % 2) if dim == SWA_DH else 0)
            cos[which, p] = np.cos(ang[:, j])
            sin[which, p] = np.sin(ang[:, j]) * (-1.0 if r < 16 else 1.0)
    out["rope_cos"], out["rope_sin"] = cos, sin
    s, tt = np.arange(CH)[:, None], np.arange(CH)[None, :]
    masks = []
    for m in LEVELS:
        masks.append((s // (2 * m) == tt // (2 * m)) & (s % (2 * m) < m) & (tt % (2 * m) >= m))
    masks += [x.T for x in masks]
    masks.append(s == tt)
    out["gla_masks"] = np.ascontiguousarray(np.stack(masks, 1).astype(np.int32))
    q, kk = np.arange(P)[:, None], np.arange(P)[None, :]
    bias = np.zeros((LAT_TILES, P, 2 * P), f)
    bias[:, :, :P][:, kk < q] = -3e38
    bias[:, :, P:][:, kk > q] = -3e38
    bias[0, :, :P] = -3e38
    bias[LAT_TILES - 1, :, P:] = -3e38
    out["swa_bias"] = bias.reshape(LAT_TILES * P, 2 * P)
    return out


def kernel(x, c, ctx, c_ctx, w_ada, b_ada, w_in, w_gla_gate, b_gla_gate, gla_norm_g, diff_lambda,
           diff_norm_g, swa_sink, w_out, ln_g, ln_b, w_ffn_gate, w_ffn_up, w_ffn_down):
    import numpy as np
    import concourse.bacc as bacc
    from concourse.bass_utils import run_bass_kernel_spmd

    def tiled(w):
        L, d, n = w.shape
        return np.ascontiguousarray(w.reshape(L, KT, P, n // P, P).transpose(0, 3, 2, 1, 4)).reshape(L, n, D)

    at = np.cumsum([0, 256, 256, 256, 256, 16, 16, 256, 256, 256, 512, 128, 128])
    gq, gk, gv, go, z, _, dq, dk, dv, sq, sk, sv = [np.arange(a, b) for a, b in zip(at[:-1], at[1:])]
    z = np.arange(at[4], at[4] + P)
    turn = np.concatenate([np.arange(0, 16), np.arange(32, 48), np.arange(16, 32), np.arange(48, 64)])
    sq = np.concatenate([sq[h * 64 + turn] for j in range(4) for h in (j, 4 + j)])
    sk = np.concatenate([sk[h * 64 + turn] for h in range(2)])
    columns = np.concatenate([z, gq, gk, gv, go, dv, sv, dq, dk, sq, sk])
    groups = [tiled(np.asarray(w)).reshape(LAYERS, FFN_GROUPS, 2, P, D) for w in (w_ffn_gate, w_ffn_up)]
    down = np.asarray(w_ffn_down).reshape(LAYERS, FFN_GROUPS, 2, P, D)
    stream = np.stack([groups[0][:, :, 0], groups[1][:, :, 0], groups[0][:, :, 1], groups[1][:, :, 1],
                       down[:, :, 0], down[:, :, 1]], axis=2)
    arrays = {
        "x": np.asarray(x)[0], "ctx": np.asarray(ctx)[0],
        "cT": np.ascontiguousarray(np.stack([np.asarray(c)[0], np.asarray(c_ctx)]).reshape(2, KT, P).transpose(2, 1, 0)),
        "w_ada": np.asarray(w_ada), "b_ada": np.asarray(b_ada),
        "w_in": tiled(np.asarray(w_in)[:, :, columns]),
        "w_gate": np.asarray(w_gla_gate), "b_gate": np.asarray(b_gla_gate), "gla_norm_g": np.asarray(gla_norm_g),
        "diff_lambda": np.asarray(diff_lambda), "diff_norm_g": np.asarray(diff_norm_g), "swa_sink": np.asarray(swa_sink),
        "w_out": np.asarray(w_out), "ln_g": np.asarray(ln_g), "ln_b": np.asarray(ln_b),
        "w_ffn": stream.reshape(LAYERS, FFN_GROUPS * 6 * P, D),
        **constants(),
    }
    arrays = {n + "_dram": np.ascontiguousarray(a) for n, a in arrays.items()}
    nc = bacc.Bacc("TRN2", target_bir_lowering=False, num_devices=1)
    t = {n[:-5]: nc.dram_tensor(n, a.shape, mybir.dt.from_np(a.dtype), kind="ExternalInput").ap() for n, a in arrays.items()}
    for name, shape in (("mod", (LAYERS, 2, ADA)), ("proj", (IN_TILES * P, PAD_T)), ("mix", (D, T)), ("h_mid", (T, D)), ("h_next", (T, D))):
        t[name] = nc.dram_tensor(name + "_scratch", shape, F32, kind="Internal").ap()
    t["heads"] = nc.dram_tensor("heads_scratch", (2, HEAD_ROWS, PAD_T), F32, kind="Internal").ap()
    t["out"] = nc.dram_tensor("out_dram", (N_LAT, D), F32, kind="ExternalOutput").ap()
    build(nc, t)
    got = run_bass_kernel_spmd(nc, [arrays], core_ids=[0])
    return got.results[0]["out_dram"].reshape(1, N_LAT, D)
```

```python
import math
from contextlib import ExitStack

import concourse.bass as bass
import concourse.mybir as mybir

F32 = mybir.dt.float32
F32R = mybir.dt.float32r
I32 = mybir.dt.int32
ALU = mybir.AluOpType
ACT = mybir.ActivationFunctionType
AX = mybir.AxisListType

P = 128
LAYERS = 2
D = 1024
KT = D // P
N_CTX, N_LAT = 256, 1024
T = N_CTX + N_LAT
CTX_TILES, LAT_TILES = N_CTX // P, N_LAT // P
TILES = CTX_TILES + LAT_TILES
BANK = 512
CHUNKS = [(256, 512), (768, 512), (0, 256)]
LAT_CHUNKS = CHUNKS[:2]

FFN = 2816
FFN_TILES = FFN // P
FFN_GROUPS = FFN_TILES // 2
ADA = 6 * D
ADA_CHUNKS = ADA // BANK

T_Z, T_GQ, T_GK, T_GV, T_GO, T_DV, T_SV = 0, 1, 3, 5, 7, 9, 11
T_DQ, T_DK, T_SQ, T_SK = 12, 14, 16, 20
IN_TILES = 21
PLAIN_TILES = 12
HEAD_DQ, HEAD_DK, HEAD_SQ, HEAD_SK = 0, 2 * P, 4 * P, 8 * P
HEAD_ROWS = 9 * P
PAD_T = T + P

GATE_RANK = 16
GATE_NORM = 16.0
CH = 128
NCH = T // CH
LEVELS = [64, 32, 16, 8, 4, 2, 1]
DIFF_HEADS, DIFF_DH = 4, 32
SWA_HEADS, SWA_DH = 8, 64
SWA_KEYS = N_CTX + 3 * P
EPS = 1e-6
ALPHA = (2.0 * LAYERS) ** 0.25


def peeled(eng, first, end, body):
    body(first, True)
    if end - first > 1:
        with eng.Fori(first + 1, end) as i:
            body(i, False)


def wait_apart(eng, sem, value, passed):
    eng.wait_ge(sem, value)
    eng.sem_inc(passed, 1)


def wait_count(eng, sem, value):
    if not isinstance(value, int) or value > 0:
        eng.wait_ge(sem, value)


class Live:

    def __init__(self, r, units, before):
        self.r, self.units, self.before = r, units, before
        self.starts = before == 0

    def __call__(self, lag):
        return self.r - lag < self.units and (self.before is None or self.r - lag >= -self.before)


def staggered(eng, first, end, units, lag, step, inline=1):
    inline = min(inline, end - first)
    for i in range(first, first + inline):
        for r in range(units):
            step(i, r, Live(r, units, (i - first) * units))
    if end > first + inline:
        with eng.Fori(first + inline, end) as i:
            for r in range(units):
                step(i, r, Live(r, units, None))
    for r in range(units, units + lag):
        step(end - 1, r, Live(r, units, (end - 1 - first) * units))


def allocators(nc, ctx, phase):
    def sb(name, shape, dt=F32):
        return ctx.enter_context(nc.sbuf_tensor(name, shape, dt))

    def ps(name, shape):
        return ctx.enter_context(nc.psum_tensor(name, shape, F32))

    def sem(name):
        return nc.alloc_semaphore(phase + name)
    return sb, ps, sem


def product(pe, out, st_hi, st_lo, mv_hi, mv_lo, start, stop):
    pe.matmul(out, st_hi, mv_hi, start=start, stop=False)
    pe.matmul(out, st_hi, mv_lo, start=False, stop=False)
    return pe.matmul(out, st_lo, mv_hi, start=False, stop=stop)


def modulation(nc, t, res):
    with nc.cleanup_on_exit(), ExitStack() as ctx:
        sb, ps, sem = allocators(nc, ctx, "ada_")
        cs = res["silu_c"]
        cT = sb("ada_c", [P, KT, 2])
        W = sb("ada_w", [P, 4, KT, BANK])
        B = sb("ada_b", [2, 4, BANK])
        R = sb("ada_rows", [2, 4, BANK])
        acc = ps("ada_acc", [P, 4, BANK])
        c_in, c_silu = sem("c_in"), sem("c_silu")
        w_in = [sem(f"ada_w_in{s}") for s in range(4)]
        product_done, row_done = sem("ada_product_done"), sem("ada_row_done")
        row_out = [sem(f"ada_row_out{s}") for s in range(4)]
        chunks = [(0, c) for c in range(4)] + [(1, c) for c in range(2, 4)]
        block = ctx.enter_context(nc.Block())

        @block.sync
        def _(sp):
            sp.dma_start(cT[:, :, :], t["cT"]).then_inc(c_in, 16)
            for n, (l, c) in enumerate(chunks):
                if n >= 4:
                    sp.wait_ge(product_done, n - 3)
                    sp.wait_ge(row_done, n - 3)
                cols = slice(c * BANK, (c + 1) * BANK)
                sp.dma_start(W[:, n % 4, :, :], t["w_ada"][l].rearrange("(k p) n -> p k n", p=P)[:, :, cols]).then_inc(w_in[n % 4], 16)
                sp.dma_start(B[:, n % 4, :], t["b_ada"][l:l + 1, cols].to_broadcast([2, BANK])).then_inc(w_in[n % 4], 16)

        @block.scalar
        def _(act):
            act.wait_ge(c_in, 16)
            act.activation(cs[:, :, :], cT[:, :, :], ACT.Silu).then_inc(c_silu, 1)
            for n, (l, c) in enumerate(chunks):
                act.wait_ge(row_done, n + 1)
                act.dma_start(t["mod"][l, :, c * BANK:(c + 1) * BANK], R[:, n % 4, :]).then_inc(row_out[n % 4], 16)
            for s in range(4):
                act.wait_ge(row_out[s], 16 * len(chunks[s::4]))

        @block.tensor
        def _(pe):
            pe.wait_ge(c_silu, 1)
            for n in range(len(chunks)):
                pe.wait_ge(w_in[n % 4], 32 * (n // 4 + 1))
                if n >= 4:
                    pe.wait_ge(row_done, n - 3)
                for k in range(KT):
                    mm = pe.matmul(acc[0:2, n % 4, :], cs[:, k, :], W[:, n % 4, k, :], start=(k == 0), stop=(k == KT - 1))
                mm.then_inc(product_done, 1)

        @block.vector
        def _(dve):
            for n in range(len(chunks)):
                dve.wait_ge(product_done, n + 1)
                if n >= 4:
                    dve.wait_ge(row_out[n % 4], 16 * (n // 4))
                dve.tensor_tensor(R[:, n % 4, :], acc[0:2, n % 4, :], B[:, n % 4, :], ALU.add).then_inc(row_done, 1)


def norm_tiles(nc, t, res, kind, layer, tiles, last):
    with nc.cleanup_on_exit(), ExitStack() as ctx:
        sb, ps, sem = allocators(nc, ctx, f"norm_{kind}{layer}_")
        nm = f"norm_{kind}{layer}_"
        post = kind != "input"
        attn = kind == "attention"
        modulated = not last
        SUM = 1
        NEXT = 2 if post else 1
        SPLIT = NEXT + 1
        first_pair, end_pair = tiles[0] // 2, tiles[-1] // 2 + 1
        streams = [0, 1] if tiles[0] == 0 else [1]
        next_mod = {"input": (layer, 0, 1), "attention": (layer, 3, 4), "ffn": (layer + 1, 0, 1)}[kind]
        gate_at = 2 if attn else 5
        ln_at = 0 if attn else 1

        uhi, ulo, ident = res["uhi"], res["ulo"], res["ident"]
        hres = sb(nm + "hres", [P, 2, D])
        h = sb(nm + "h", [P, 2, D]) if post else hres
        x = sb(nm + "x", [P, 2, D]) if modulated else None
        gate = sb(nm + "gate", [P, 2, D]) if post else None
        lng = sb(nm + "lng", [P, D]) if post else None
        lnb = sb(nm + "lnb", [P, D]) if post else None
        shift = sb(nm + "shift", [P, 2, KT])
        scale = sb(nm + "scale", [P, 2, KT])
        stats = sb(nm + "stats", [P, 2, 2, 2, 6])
        mv = sb(nm + "mv", [P, 2, 2, 2])
        sd = sb(nm + "sd", [P, 2, 2])
        rstd = sb(nm + "rstd", [P, 2, 2])
        nmu = sb(nm + "nmu", [P, 2, 2])
        eps = sb(nm + "eps", [P, 1])
        if attn:
            wohi = sb(nm + "wohi", [P, KT, D], F32R)
            wolo = sb(nm + "wolo", [P, KT, D], F32R)
            mix = sb(nm + "mix", [P, 1, KT, P])
            mhi = sb(nm + "mhi", [P, 2, KT, P], F32R)
            mlo = sb(nm + "mlo", [P, 2, KT, P], F32R)
            Y = ps(nm + "y", [P, 2, D])
            staging = [h[:, 0, :], h[:, 1, :], x[:, 0, :], x[:, 1, :]]
            NS = len(staging)
        TR = ps(nm + "tr", [P, 2, KT, P])
        chunked = modulated and not attn
        MUL, BIAS = 1, 2
        first_chunks = 0 if kind == "input" else 1
        if chunked:
            aW = sb(nm + "ada_w", [P, 2, KT, BANK])
            aB = sb(nm + "ada_b", [2, 2, BANK])
            aR = sb(nm + "ada_rows", [2, 2, BANK])
            acc = ps(nm + "ada_acc", [P, 2, BANK])

        ada_in = [sem(f"ada_in{s}") for s in range(2)]
        bias_in = [sem(f"bias_in{s}") for s in range(2)]
        product_done, row_done = sem("product_done"), sem("row_done")
        row_out = [sem(f"row_out{s}") for s in range(2)]
        passed, sp_passed = sem("passed"), sem("sp_passed")
        const_in, eps_set, one_plus = sem("const_in"), sem("eps_set"), sem("one_plus")
        h_in = [sem(f"h_in{s}") for s in range(2)]
        mix_in = sem("mix_in")
        wo_in = [sem(f"wo_in{s}") for s in range(4)]
        wo_hi, wo_lo = sem("wo_hi"), sem("wo_lo")
        mix_hi, mix_lo, y_done = sem("mix_hi"), sem("mix_lo"), sem("y_done")
        gated, summed = sem("gated"), sem("summed")
        st_done, mv_done, sd_done, rs_done, nm_done, normed = (
            [sem(n + str(j)) for j in range(2)] for n in ("st_done", "mv_done", "sd_done", "rs_done", "nm_done", "normed"))
        h_scaled, h_done = sem("h_scaled"), sem("h_done")
        turned, u_done, u_hi, u_lo = sem("turned"), sem("u_done"), sem("u_hi"), sem("u_lo")
        h_out = [sem(f"h_out{s}") for s in range(2)]
        block = ctx.enter_context(nc.Block())
        const_loads = 16 * ((2 * len(streams) if modulated else 0) + (2 + len(streams) if post else 0))

        def count(i, u):
            return (i - first_pair) * 2 + u + 1

        def slot_count(i, u):
            return i - first_pair + u // 2

        def has_chunk(i, u, live, lag):
            return chunked and live(lag) and (not isinstance(i, int) or i + u // 2 >= first_chunks)

        def chunk_count(i, u):
            return (i - first_chunks) * 2 + u + 1

        def chunk_slot_count(i, u):
            return i - first_chunks + u // 2

        def chunk(i, u):
            if kind == "input" and isinstance(i, int) and i + u // 2 == 0:
                return 1, bass.ds((i * 2 + u) * BANK, BANK)
            return (layer if kind == "input" else layer + 1), bass.ds(i * 2 * BANK + (u + 2) * BANK, BANK)

        def stream(i, u):
            return 0 if isinstance(i, int) and 2 * i + u < CTX_TILES else 1

        def src_rows(i, s):
            if kind == "input" or (attn and layer == 0):
                return t["ctx"][s * P:(s + 1) * P, :] if stream(i, s) == 0 else t["x"][bass.ds(i * 2 * P + (s * P - N_CTX), P), :]
            return t["h_mid" if not attn else "h_next"][bass.ds(i * 2 * P + s * P, P), :]

        def dst_rows(i, u):
            if last:
                return t["out"][bass.ds(i * 2 * P + (u * P - N_CTX), P), :]
            return t["h_mid" if attn else "h_next"][bass.ds(i * 2 * P + u * P, P), :]

        def stagger(eng, step):
            back = SPLIT if modulated else NEXT
            staggered(eng, first_pair, end_pair, 2, back, step, inline=(back + 1) // 2 + (1 if len(streams) == 2 else 0))

        @block.sync
        def _(sp):
            if attn:
                for k in range(KT):
                    if k >= NS:
                        sp.wait_ge(wo_lo, k - NS + 1)
                    sp.dma_start(staging[k % NS], t["w_out"][layer, k * P:(k + 1) * P, :]).then_inc(wo_in[k % NS], 16)

            def step(i, r, live):
                if has_chunk(i, r, live, 0):
                    l, cols = chunk(i, r)
                    columns = t["w_ada"][l].rearrange("(k p) n -> p k n", p=P)[:, :, cols]
                    if not isinstance(i, int) or chunk_count(i, r) > 2:
                        wait_apart(sp, product_done, chunk_count(i, r) - 2, sp_passed)
                    sp.dma_start(aW[:, r % 2, :, :], columns).then_inc(ada_in[r % 2], 16)
                if has_chunk(i, r - MUL, live, MUL):
                    u = r - MUL
                    l, cols = chunk(i, u)
                    bias = t["b_ada"][l:l + 1, cols].to_broadcast([2, BANK])
                    if not isinstance(i, int) or chunk_count(i, u) > 2:
                        wait_apart(sp, row_done, chunk_count(i, u) - 2, sp_passed)
                    sp.dma_start(aB[:, u % 2, :], bias).then_inc(bias_in[u % 2], 16)
                if live(0):
                    s = r % 2
                    if attn:
                        wait_count(sp, mix_lo, count(i, r) - 1)
                        sp.dma_start(mix[:, 0, :, :], t["mix"].rearrange("(k p) n -> p k n", p=P)[:, :, bass.ds(i * 2 * P + s * P, P)]).then_inc(mix_in, 16)
                    wait_count(sp, summed if post else normed[1], count(i, r) - 2)
                    sp.dma_start(hres[:, s, :], src_rows(i, s)).then_inc(h_in[s], 16)
                if post and live(NEXT):
                    u = r - NEXT
                    sp.wait_ge(h_done, count(i, u))
                    sp.dma_start(dst_rows(i, u), h[:, u % 2, :]).then_inc(h_out[u % 2], 16)
                if has_chunk(i, r - BIAS, live, BIAS):
                    u = r - BIAS
                    l, cols = chunk(i, u)
                    rows = t["mod"][l, :, cols]
                    wait_apart(sp, row_done, chunk_count(i, u), sp_passed)
                    sp.dma_start(rows, aR[:, u % 2, :]).then_inc(row_out[u % 2], 16)
            stagger(sp, step)
            if chunked:
                for s in range(2):
                    sp.wait_ge(row_out[s], 16 * (end_pair - first_chunks))
            if post:
                for s in range(2):
                    sp.wait_ge(h_out[s], 16 * (end_pair - first_pair))

        @block.tensor
        def _(pe):
            if attn:
                pe.wait_ge(wo_lo, KT)

            def step(i, r, live):
                if attn and live(0):
                    s = r % 2
                    pe.wait_ge(mix_lo, count(i, r))
                    wait_count(pe, gated, count(i, r) - 2)
                    for half in range(2):
                        for k in range(KT):
                            cols = slice(half * BANK, (half + 1) * BANK)
                            mm = product(pe, Y[:, s, cols], mhi[:, s, k, :], mlo[:, s, k, :],
                                         wohi[:, k, cols], wolo[:, k, cols], k == 0, k == KT - 1)
                    mm.then_inc(y_done, 1)
                if has_chunk(i, r - MUL, live, MUL):
                    u = r - MUL
                    s = u % 2
                    pe.wait_ge(ada_in[s], 16 * (chunk_slot_count(i, u) + 1))
                    wait_count(pe, row_done, chunk_count(i, u) - 2)
                    for k in range(KT):
                        mm = pe.matmul(acc[0:2, s, :], res["silu_c"][:, k, :], aW[:, s, k, :], start=(k == 0), stop=(k == KT - 1))
                    mm.then_inc(product_done, 1)
                if live(NEXT):
                    u = r - NEXT
                    s = u % 2
                    pe.wait_ge(normed[1], count(i, u))
                    wait_count(pe, u_done, count(i, u) - 2)
                    for k in range(KT):
                        mm = pe.transpose(TR[:, s, k, :], x[:, s, k * P:(k + 1) * P], ident[:, :])
                    mm.then_inc(turned, 1)
            if modulated:
                stagger(pe, step)

        @block.vector
        def _(dve):
            if attn:
                for k in range(KT):
                    dve.wait_ge(wo_hi, k + 1)
                    dve.tensor_tensor(wolo[:, k, :], staging[k % NS], wohi[:, k, :].bitcast(F32), ALU.subtract).then_inc(wo_lo, 1)
            dve.wait_ge(const_in, const_loads)
            if modulated:
                dve.tensor_scalar(scale[:, streams[0]:2, :], scale[:, streams[0]:2, :], 1.0, None, ALU.add).then_inc(one_plus, 1)

            def statistics(i, u, j, src):
                s = u % 2
                for half in range(2):
                    dve.bn_stats(stats[:, s, j, half, :], src[:, s, half * BANK:(half + 1) * BANK]).then_inc(st_done[j], 1)
                wait_apart(dve, st_done[j], 2 * count(i, u), passed)
                dve.bn_aggr(mv[:, s, j, :], stats[:, s, j, :, :]).then_inc(mv_done[j], 1)

            def normalizers(i, u, j):
                s = u % 2
                dve.wait_ge(sd_done[j], count(i, u))
                dve.reciprocal(rstd[:, s, j:j + 1], sd[:, s, j:j + 1]).then_inc(rs_done[j], 1)
                dve.wait_ge(rs_done[j], count(i, u))
                dve.scalar_tensor_tensor(nmu[:, s, j:j + 1], mv[:, s, j, 0:1], -1.0, rstd[:, s, j:j + 1], ALU.mult, ALU.mult).then_inc(nm_done[j], 1)

            def step(i, r, live):
                if post and live(SUM):
                    u, s = r - SUM, (r - SUM) % 2
                    wait_count(dve, h_out[s], 16 * slot_count(i, u))
                    if modulated:
                        wait_count(dve, normed[1], count(i, u) - 2)
                    if attn:
                        dve.wait_ge(y_done, count(i, u))
                        y = Y[:, s, :]
                    else:
                        y = res["y"][:, bass.ds(i * 2 + u, 1), :].rearrange("p a b -> p (a b)")
                    dve.tensor_tensor(h[:, s, :], y, gate[:, stream(i, u), :], ALU.mult).then_inc(gated, 1)
                    dve.wait_ge(gated, count(i, u))
                    dve.wait_ge(h_in[s], 16 * (slot_count(i, u) + 1))
                    dve.scalar_tensor_tensor(h[:, s, :], hres[:, s, :], ALPHA, h[:, s, :], ALU.mult, ALU.add).then_inc(summed, 1)
                    dve.wait_ge(summed, count(i, u))
                    statistics(i, u, 0, h)
                if post and live(NEXT):
                    u, s = r - NEXT, (r - NEXT) % 2
                    dve.wait_ge(h_scaled, count(i, u))
                    dve.tensor_tensor(h[:, s, :], h[:, s, :], lnb[:, :], ALU.add).then_inc(h_done, 1)
                if post and live(SUM):
                    normalizers(i, r - SUM, 0)
                if modulated and live(NEXT):
                    u = r - NEXT
                    if post:
                        dve.wait_ge(h_done, count(i, u))
                    else:
                        dve.wait_ge(h_in[u % 2], 16 * (slot_count(i, u) + 1))
                    statistics(i, u, 1, h)
                if modulated and live(SPLIT):
                    u, s = r - SPLIT, (r - SPLIT) % 2
                    dve.wait_ge(u_done, count(i, u))
                    dve.tensor_copy(uhi[:, :, bass.ds(i * 2 * P + u * P, P)], x[:, s, :].rearrange("p (k n) -> p k n", k=KT)).then_inc(u_hi, 1)
                if modulated and live(NEXT):
                    normalizers(i, r - NEXT, 1)
                if has_chunk(i, r - BIAS, live, BIAS):
                    u = r - BIAS
                    s = u % 2
                    dve.wait_ge(product_done, chunk_count(i, u))
                    dve.wait_ge(bias_in[s], 16 * (chunk_slot_count(i, u) + 1))
                    wait_count(dve, row_out[s], 16 * chunk_slot_count(i, u))
                    dve.tensor_tensor(aR[:, s, :], acc[0:2, s, :], aB[:, s, :], ALU.add).then_inc(row_done, 1)
            stagger(dve, step)

        @block.scalar
        def _(act):
            act.wait_ge(eps_set, 1)
            if attn:
                for k in range(KT):
                    act.wait_ge(wo_in[k % NS], 16 * (k // NS + 1))
                    act.copy(wohi[:, k, :], staging[k % NS]).then_inc(wo_hi, 1)
                act.wait_ge(wo_lo, KT)
            if modulated:
                act.wait_ge(one_plus, 1)

            def normalize(i, u, j, dst):
                s = u % 2
                act.wait_ge(mv_done[j], count(i, u))
                act.activation(sd[:, s, j:j + 1], mv[:, s, j, 1:2], ACT.Sqrt, bias=eps[:, 0:1]).then_inc(sd_done[j], 1)
                act.wait_ge(nm_done[j], count(i, u))
                if j == 1:
                    wait_count(act, u_lo, count(i, u) - 2)
                act.activation(dst[:, s, :], h[:, s, :], ACT.Identity, scale=rstd[:, s, j:j + 1], bias=nmu[:, s, j:j + 1]).then_inc(normed[j], 1)

            def step(i, r, live):
                if attn and live(0):
                    s = r % 2
                    act.wait_ge(mix_in, 16 * count(i, r))
                    wait_count(act, y_done, count(i, r) - 2)
                    act.copy(mhi[:, s, :, :], mix[:, 0, :, :]).then_inc(mix_hi, 1)
                if modulated and live(SPLIT):
                    u, s = r - SPLIT, (r - SPLIT) % 2
                    act.wait_ge(turned, count(i, u))
                    for k in range(KT):
                        m = act.activation(x[:, s, k * P:(k + 1) * P], TR[:, s, k, :], ACT.Identity,
                                           scale=scale[:, stream(i, u), k:k + 1], bias=shift[:, stream(i, u), k:k + 1])
                    m.then_inc(u_done, 1)
                if post and live(SUM):
                    normalize(i, r - SUM, 0, h)
                if modulated and live(NEXT):
                    normalize(i, r - NEXT, 1, x)
            stagger(act, step)

        @block.gpsimd
        def _(pool):
            pool.memset(eps[:, :], EPS).then_inc(eps_set, 1)
            for st in streams:
                if modulated:
                    for dst, at in ((shift, next_mod[1]), (scale, next_mod[2])):
                        pool.dma_start(dst[:, st, :], t["mod"][next_mod[0], 1 - st, at * D:(at + 1) * D].rearrange("(k p) -> p k", p=P)).then_inc(const_in, 16)
                if post:
                    pool.dma_start(gate[:, st, :], t["mod"][layer, 1 - st:2 - st, gate_at * D:(gate_at + 1) * D].to_broadcast([P, D])).then_inc(const_in, 16)
            if post:
                pool.dma_start(lng[:, :], t["ln_g"][layer, ln_at:ln_at + 1, :].to_broadcast([P, D])).then_inc(const_in, 16)
                pool.dma_start(lnb[:, :], t["ln_b"][layer, ln_at:ln_at + 1, :].to_broadcast([P, D])).then_inc(const_in, 16)
            pool.wait_ge(const_in, const_loads)

            def step(i, r, live):
                if attn and live(0):
                    s = r % 2
                    pool.wait_ge(mix_hi, count(i, r))
                    pool.tensor_tensor(mlo[:, s, :, :], mix[:, 0, :, :], mhi[:, s, :, :].bitcast(F32), ALU.subtract).then_inc(mix_lo, 1)
                if post and live(SUM):
                    u, s = r - SUM, (r - SUM) % 2
                    pool.wait_ge(normed[0], count(i, u))
                    pool.tensor_tensor(h[:, s, :], h[:, s, :], lng[:, :], ALU.mult).then_inc(h_scaled, 1)
                if modulated and live(SPLIT):
                    u, s = r - SPLIT, (r - SPLIT) % 2
                    at = bass.ds(i * 2 * P + u * P, P)
                    pool.wait_ge(u_hi, count(i, u))
                    pool.tensor_tensor(ulo[:, :, at], x[:, s, :].rearrange("p (k n) -> p k n", k=KT), uhi[:, :, at].bitcast(F32), ALU.subtract).then_inc(u_lo, 1)
            stagger(pool, step)


def input_projection(nc, t, res, layer):
    with nc.cleanup_on_exit(), ExitStack() as ctx:
        sb, ps, sem = allocators(nc, ctx, f"in{layer}_")
        nm = f"in{layer}_"
        uhi, ulo = res["uhi"], res["ulo"]
        raw = sb(nm + "raw", [P, 2, D])
        whi = sb(nm + "whi", [P, 2, KT, P], F32R)
        wlo = sb(nm + "wlo", [P, 2, KT, P], F32R)
        stage = sb(nm + "stage", [P, 2, T])
        swap = sb(nm + "swap", [P, 2, N_LAT])
        cos = sb(nm + "cos", [P, 2, N_LAT])
        sin = sb(nm + "sin", [P, 2, N_LAT])
        zero = sb(nm + "zero", [P, P])
        shi = sb(nm + "shi", [P, 2, T], F32R)
        slo = sb(nm + "slo", [P, 2, T], F32R)
        acc = ps(nm + "acc", [P, 2, 3, BANK])
        raw_in = [sem(f"raw_in{s}") for s in range(2)]
        passed = sem("passed")
        rope_in, zero_set, pad_out = sem("rope_in"), sem("zero_set"), sem("pad_out")
        w_hi, w_ready, chunk_done, evacuated = sem("w_hi"), sem("w_ready"), sem("chunk_done"), sem("evacuated")
        swapped, cos_done, sin_done, roped = sem("swapped"), sem("cos_done"), sem("sin_done"), sem("roped")
        out_hi, out_lo = sem("out_hi"), sem("out_lo")
        stored = [sem(f"stored{s}") for s in range(2)]
        stored_hl = [sem(f"stored_hl{s}") for s in range(2)]
        NCHK = len(CHUNKS)
        block = ctx.enter_context(nc.Block())
        pairs = IN_TILES // 2
        MASK = list(range(16, 32)) + list(range(16))

        def each_tile(eng, body, pairs_from=0, pairs_to=pairs, tail=True):
            def two(i, first):
                for s in range(2):
                    body(i * 2 + s, i, s, first and pairs_from == 0)
            if pairs_from == 0:
                peeled(eng, 0, pairs_to, two)
            else:
                with eng.Fori(pairs_from, pairs_to) as i:
                    two(i, False)
            if tail:
                body(IN_TILES - 1, pairs, 0, False)

        @block.sync
        def _(sp):
            sp.dma_start(cos[:, :, :], t["rope_cos"].rearrange("a p n -> p a n")).then_inc(rope_in, 16)
            sp.dma_start(sin[:, :, :], t["rope_sin"].rearrange("a p n -> p a n")).then_inc(rope_in, 16)

            def body(n, i, s, first):
                if not first:
                    sp.wait_ge(w_ready, n - 1)
                sp.dma_start(raw[:, s, :], t["w_in"][layer][bass.ds(n * P, P), :]).then_inc(raw_in[s], 16)
            each_tile(sp, body)

        @block.gpsimd
        def _(pool):
            pool.memset(zero[:, :], 0.0).then_inc(zero_set, 1)
            pool.wait_ge(zero_set, 1)
            pool.dma_start(t["proj"][T_SV * P:(T_SV + 1) * P, T:PAD_T], zero[:, :]).then_inc(pad_out, 16)
            for part in range(2):
                pool.dma_start(t["heads"][part, HEAD_SK:HEAD_SK + P, T:PAD_T], zero[:, :]).then_inc(pad_out, 16)
            pool.wait_ge(rope_in, 32)

            def split(n, i, s, first):
                pool.wait_ge(w_hi, n + 1)
                pool.tensor_tensor(wlo[:, s, :, :], raw[:, s, :].rearrange("p (k n) -> p k n", k=KT),
                                   whi[:, s, :, :].bitcast(F32), ALU.subtract).then_inc(w_ready, 1)
            each_tile(pool, split)
            pool.wait_ge(pad_out, 48)

        @block.tensor
        def _(pe):
            def body(n, i, s, first):
                pe.wait_ge(w_ready, n + 1)
                for c, (t0, tn) in enumerate(CHUNKS):
                    if not first:
                        pe.wait_ge(evacuated, (n - 2) * NCHK + c + 1)
                    for k in range(KT):
                        mm = product(pe, acc[:, s, c, 0:tn], whi[:, s, k, :], wlo[:, s, k, :],
                                     uhi[:, k, t0:t0 + tn], ulo[:, k, t0:t0 + tn], k == 0, k == KT - 1)
                    mm.then_inc(chunk_done, 1)
            each_tile(pe, body)

        @block.scalar
        def _(act):
            def split(n, i, s, first):
                act.wait_ge(raw_in[s], i * 16 + 16)
                if not first:
                    act.wait_ge(chunk_done, (n - 1) * NCHK)
                act.copy(whi[:, s, :, :], raw[:, s, :].rearrange("p (k n) -> p k n", k=KT)).then_inc(w_hi, 1)

            def evacuate(n, s):
                for c, (t0, tn) in enumerate(CHUNKS):
                    act.wait_ge(chunk_done, n * NCHK + c + 1)
                    act.copy(stage[:, s, t0:t0 + tn], acc[:, s, c, 0:tn]).then_inc(evacuated, 1)

            def finish_plain(n, i, s, first):
                if not first:
                    act.wait_ge(stored[s], i * 16)
                evacuate(n, s)
                act.wait_ge(evacuated, (n + 1) * NCHK)
                act.dma_start(t["proj"][bass.ds(n * P, P), 0:T], stage[:, s, :]).then_inc(stored[s], 16)

            def finish_rope(n, i, s, first):
                if first:
                    act.wait_ge(stored[s], PLAIN_TILES // 2 * 16)
                else:
                    act.wait_ge(out_lo, n - PLAIN_TILES - 1)
                evacuate(n, s)
                act.wait_ge(out_lo, n - PLAIN_TILES + 1)
                at = bass.ds((n - PLAIN_TILES) * P, P)
                act.dma_start(t["heads"][0, at, 0:T], shi[:, s, :].bitcast(F32)).then_inc(stored_hl[s], 16)
                act.dma_start(t["heads"][1, at, 0:T], slo[:, s, :].bitcast(F32)).then_inc(stored_hl[s], 16)

            split(0, 0, 0, True)
            split(1, 0, 1, True)
            for finish, lo, hi in ((finish_plain, 0, PLAIN_TILES // 2), (finish_rope, PLAIN_TILES // 2, pairs - 1)):
                def two(i, first):
                    for s in range(2):
                        finish(i * 2 + s, i, s, first)
                        split(i * 2 + s + 2, i + 1, s, False)
                peeled(act, lo, hi, two)
            finish_rope(2 * pairs - 2, pairs - 1, 0, False)
            split(2 * pairs, pairs, 0, False)
            finish_rope(2 * pairs - 1, pairs - 1, 1, False)
            finish_rope(2 * pairs, pairs, 0, False)
            for s in range(2):
                act.wait_ge(stored[s], 16 * PLAIN_TILES // 2)
                act.wait_ge(stored_hl[s], 32 * ((IN_TILES - PLAIN_TILES + 1 - s) // 2))

        @block.vector
        def _(dve):
            dve.wait_ge(rope_in, 32)

            def rope(n, i, s, table, first=False):
                m = n - PLAIN_TILES + 1
                x = stage[:, s, N_CTX:T]
                wait_apart(dve, evacuated, (n + 1) * NCHK, passed)
                dve.stream_shuffle(swap[:, s, :], x, MASK).then_inc(swapped, 1)
                dve.wait_ge(swapped, m)
                dve.tensor_tensor(x, x, cos[:, table, :], ALU.mult).then_inc(cos_done, 1)
                dve.tensor_tensor(swap[:, s, :], swap[:, s, :], sin[:, table, :], ALU.mult).then_inc(sin_done, 1)
                dve.wait_ge(cos_done, m)
                dve.wait_ge(sin_done, m)
                dve.tensor_tensor(x, x, swap[:, s, :], ALU.add).then_inc(roped, 1)
                dve.wait_ge(roped, m)
                if not first:
                    dve.wait_ge(stored_hl[s], (i - PLAIN_TILES // 2) * 32)
                dve.tensor_copy(shi[:, s, :], stage[:, s, :]).then_inc(out_hi, 1)
                dve.wait_ge(out_hi, m)
                dve.tensor_tensor(slo[:, s, :], stage[:, s, :], shi[:, s, :].bitcast(F32), ALU.subtract).then_inc(out_lo, 1)
            for s in range(2):
                rope(PLAIN_TILES + s, PLAIN_TILES // 2, s, 0, True)
            for lo, hi, table in ((T_DQ // 2 + 1, T_SQ // 2, 0), (T_SQ // 2, pairs, 1)):
                with dve.Fori(lo, hi) as i:
                    for s in range(2):
                        rope(i * 2 + s, i, s, table)
            rope(IN_TILES - 1, pairs, 0, 1)


def gated_linear_attention(nc, t, res, layer):
    with nc.cleanup_on_exit(), ExitStack() as ctx:
        sb, ps, sem = allocators(nc, ctx, f"gla{layer}_")
        nm = f"gla{layer}_"
        ident = res["ident"]
        FLAT = [(0, 512), (512, 512), (1024, 256)]
        DI = [(d, i) for d in range(2) for i in range(2)]
        q = sb(nm + "q", [P, 2, T])
        k = sb(nm + "k", [P, 2, T])
        vT = sb(nm + "vT", [P, 2, T])
        V = sb(nm + "V", [P, TILES, 2 * P])
        z = sb(nm + "z", [2 * GATE_RANK, T])
        wg = sb(nm + "wg", [2 * GATE_RANK, 2, 2 * P])
        bg = sb(nm + "bg", [P, 2, 2])
        normg = sb(nm + "normg", [P, 1])
        reset = sb(nm + "reset", [P, T])
        B = sb(nm + "B", [P, 4, T])
        Dc = sb(nm + "D", [P, 2, T])
        X = sb(nm + "X", [P, 2, T])
        Qe = sb(nm + "Qe", [P, 4, T])
        KeT = sb(nm + "KeT", [P, 2, NCH, P])
        dec = sb(nm + "dec", [P, 4, NCH])
        S = sb(nm + "S", [P, 4, NCH, P])
        A = sb(nm + "A", [P, 2, 2, NCH, CH])
        masks = sb(nm + "masks", [P, 2 * len(LEVELS) + 1, CH], I32)
        block_mean = sb(nm + "block_mean", [P, P])
        eps = sb(nm + "eps", [P, 1])
        UNIT = ps(nm + "unit", [P, 2, 3 * BANK])
        TR = ps(nm + "tr", [P, 2, BANK])

        load = {n: sem(f"gla_{n}_in") for n in ("q", "k", "v", "z", "w", "b", "mask", "bm", "g", "go")}
        zeroed, wg_zero = sem("zeroed"), sem("wg_zero")
        reset_one, reset_set, q_scaled = sem("reset_one"), sem("reset_set"), sem("q_scaled")
        v_turned, v_copied = sem("v_turned"), sem("v_copied")
        logits, abs_done, exp_of_abs, log_done, min_done, gate_done, scanned = (
            sem("logits"), sem("abs_done"), sem("exp_of_abs"), sem("log_done"), sem("min_done"), sem("gate_done"), sem("scanned"))
        d_done, e_done, x_done, unit_done, copied = sem("d_done"), sem("e_done"), sem("x_done"), sem("unit_done"), sem("copied")
        qe_e, qe_done, ke_turned, ke_copied, dec_done = sem("qe_e"), sem("qe_done"), sem("ke_turned"), sem("ke_copied"), sem("dec_done")
        u_done, state = sem("u_done"), sem("state")
        o_done, o_copied, squared, mean_done, rms_done = sem("o_done"), sem("o_copied"), sem("squared"), sem("mean_done"), sem("rms_done")
        inv_done, silu_done, gate_ready, normed, gated, stored = (
            sem("inv_done"), sem("silu_done"), sem("gate_ready"), sem("normed"), sem("gated"), sem("stored"))
        block = ctx.enter_context(nc.Block())
        NL = len(LEVELS)
        UNITS0 = 4
        NPAIR = 4 * NL
        BORDER = [1, 0] + list(range(NCH - 1, 1, -1))
        ORDER = [list(range(NCH)), BORDER]

        def halves(ap, m):
            return ap.rearrange("p (n h m) -> p n h m", h=2, m=m)

        def min_steps(g):
            per = [4, 4, 1]
            return (g // 3) * (NCH - 1) + sum(per[:g % 3 + 1])

        proj = t["proj"]

        @block.sync
        def _(sp):
            sp.dma_start(z[:, :], proj[T_Z * P:T_Z * P + 2 * GATE_RANK, 0:T]).then_inc(load["z"], 16)
            sp.wait_ge(wg_zero, 1)
            for d in range(2):
                sp.dma_start(wg[d * GATE_RANK:(d + 1) * GATE_RANK, d, :], t["w_gate"][layer, d]).then_inc(load["w"], 16)
                sp.dma_start(bg[:, d, :], t["b_gate"][layer, d:d + 1, :].rearrange("a (i p) -> p (a i)", p=P)).then_inc(load["b"], 16)
            sp.dma_start(k[:, :, :], proj[T_GK * P:(T_GK + 2) * P, 0:T].rearrange("(i p) n -> p i n", p=P)).then_inc(load["k"], 16)
            sp.dma_start(q[:, :, :], proj[T_GQ * P:(T_GQ + 2) * P, 0:T].rearrange("(i p) n -> p i n", p=P)).then_inc(load["q"], 16)
            sp.dma_start(masks[:, :, :], t["gla_masks"]).then_inc(load["mask"], 16)
            sp.dma_start(vT[:, :, :], proj[T_GV * P:(T_GV + 2) * P, 0:T].rearrange("(i p) n -> p i n", p=P)).then_inc(load["v"], 16)
            sp.dma_start(block_mean[:, :], t["block_mean"]).then_inc(load["bm"], 16)
            for h in range(2):
                sp.dma_start(normg[h * 64:(h + 1) * 64, :], t["gla_norm_g"][layer].rearrange("(p a) -> p a", a=1)).then_inc(load["g"], 16)
            sp.wait_ge(v_turned, 6)
            sp.dma_start(vT[:, :, :], proj[T_GO * P:(T_GO + 2) * P, 0:T].rearrange("(i p) n -> p i n", p=P)).then_inc(load["go"], 16)
            for i in range(2):
                sp.wait_ge(gated, i + 1)
                sp.dma_start(t["mix"][i * P:(i + 1) * P, :], X[:, i, :]).then_inc(stored, 16)
            sp.wait_ge(stored, 32)

        @block.gpsimd
        def _(pool):
            pool.memset(wg[:, :, :], 0.0).then_inc(wg_zero, 1)
            pool.memset(eps[:, :], EPS).then_inc(zeroed, 1)
            pool.memset(A[:, :, :, :, :], 0.0).then_inc(zeroed, 1)
            pool.memset(S[:, :, :, :], 0.0).then_inc(zeroed, 1)
            pool.wait_ge(load["k"], 16)
            pool.wait_ge(q_scaled, 1)
            n = 0
            for i in range(2):
                for d in range(2):
                    for m in LEVELS:
                        pool.wait_ge(e_done, n + 1)
                        if n >= 2:
                            pool.wait_ge(unit_done, UNITS0 + 2 * (n - 1))
                        e, x = halves(Dc[:, n % 2, :], m), halves(X[:, n % 2, :], m)
                        kk, qq = halves(k[:, i, :], m), halves(q[:, i, :], m)
                        first, second = (kk, qq) if d == 0 else (qq, kk)
                        pool.tensor_tensor(x[:, :, 0, :], first[:, :, 0, :], e[:, :, 0, :], ALU.mult).then_inc(x_done, 1)
                        pool.tensor_tensor(x[:, :, 1, :], second[:, :, 1, :], e[:, :, 1, :], ALU.mult).then_inc(x_done, 1)
                        n += 1
            for j, (d, i) in enumerate(DI):
                pool.wait_ge(e_done, NPAIR + j + 1)
                pool.wait_ge(unit_done, UNITS0 + 2 * NPAIR)
                if j >= 2:
                    pool.wait_ge(ke_turned, j - 1)
                pool.tensor_tensor(X[:, j % 2, :], k[:, i, :], Dc[:, j % 2, :], ALU.mult).then_inc(x_done, 1)

        @block.tensor
        def _(pe):
            pe.wait_ge(load["z"], 16)
            pe.wait_ge(load["w"], 32)
            for n, (d, i) in enumerate(DI):
                if n >= 2:
                    pe.wait_ge(min_done, n - 1)
                    pe.wait_ge(abs_done, n - 1)
                for t0, tn in FLAT:
                    mm = pe.matmul(UNIT[:, n % 2, t0:t0 + tn], wg[:, d, i * P:(i + 1) * P], z[:, t0:t0 + tn], start=True, stop=True)
                mm.then_inc(logits, 1)
            pe.wait_ge(load["v"], 16)
            g = 0
            for i in range(2):
                for c0 in range(0, TILES, 4):
                    if g >= 2:
                        pe.wait_ge(v_copied, g - 1)
                    for c in range(c0, min(c0 + 4, TILES)):
                        mm = pe.transpose(TR[:, g % 2, (c - c0) * P:(c - c0 + 1) * P], vT[:, i, c * P:(c + 1) * P], ident[:, :])
                    mm.then_inc(v_turned, 1)
                    g += 1
            pe.wait_ge(q_scaled, 2)
            pe.wait_ge(min_done, 4)
            pe.wait_ge(abs_done, 4)
            for i in range(2):
                for h in range(2):
                    if i:
                        pe.wait_ge(copied, 2 * i + h - 1)
                    rows = slice(64 * h, 64 * h + 64)
                    for c in range(NCH):
                        cols = slice(c * CH, (c + 1) * CH)
                        mm = pe.matmul(UNIT[:, h, cols], k[rows, i, cols], Qe[rows, i, cols], start=True, stop=True)
                    mm.then_inc(unit_done, 1)
            with pe.Fori(0, NPAIR // 2) as j:
                for s in range(2):
                    pe.wait_ge(x_done, j * 4 + 2 * s + 2)
                    for h in range(2):
                        pe.wait_ge(copied, j * 4 + 2 * s + h + UNITS0 - 1)
                        rows = slice(64 * h, 64 * h + 64)
                        for c in range(NCH):
                            cols = slice(c * CH, (c + 1) * CH)
                            mm = pe.matmul(UNIT[:, h, cols], X[rows, s, cols], X[rows, s, cols], start=True, stop=True)
                        mm.then_inc(unit_done, 1)
            pe.wait_ge(v_copied, 6)
            pe.wait_ge(copied, UNITS0 + 2 * NPAIR)
            g = 0
            for j, (d, i) in enumerate(DI):
                pe.wait_ge(x_done, 2 * NPAIR + j + 1)
                if j >= 2:
                    pe.wait_ge(ke_copied, j - 1)
                for c in range(NCH):
                    mm = pe.transpose(UNIT[:, j % 2, c * P:(c + 1) * P], X[:, j % 2, c * P:(c + 1) * P], ident[:, :])
                mm.then_inc(ke_turned, 1)
                pe.wait_ge(ke_copied, j + 1)
                order = ORDER[d][:-1]
                for c0 in range(0, len(order), 4):
                    if g >= 2:
                        pe.wait_ge(state, 2 * min_steps(g - 2))
                    for a, c in enumerate(order[c0:c0 + 4]):
                        mm = pe.matmul(TR[:, g % 2, a * P:(a + 1) * P], KeT[:, j % 2, c, :], V[:, c, i * P:(i + 1) * P], start=True, stop=True)
                    mm.then_inc(u_done, 1)
                    g += 1
            pe.wait_ge(qe_done, 4)
            pe.wait_ge(state, 2 * 4 * (NCH - 1))
            pe.wait_ge(ke_copied, 4)
            for i in range(2):
                for c in range(NCH):
                    cols = slice(c * CH, (c + 1) * CH)
                    pe.matmul(UNIT[:, i, cols], S[:, i, c, :], Qe[:, i, cols], start=True, stop=False, skip_group_check=True)
                    pe.matmul(UNIT[:, i, cols], S[:, 2 + i, c, :], Qe[:, 2 + i, cols], start=False, stop=True, skip_group_check=True)
                    for h in range(2):
                        mm = pe.matmul(UNIT[64 * h:64 * h + 64, i, cols], V[:, c, i * P + 64 * h:i * P + 64 * h + 64], A[:, i, h, c, :],
                                       start=False, stop=True, skip_group_check=True)
                mm.then_inc(o_done, 1)
            pe.wait_ge(load["bm"], 16)
            for i in range(2):
                pe.wait_ge(squared, i + 1)
                pe.wait_ge(o_copied, i + 1)
                for t0, tn in FLAT:
                    mm = pe.matmul(UNIT[:, i, t0:t0 + tn], block_mean[:, :], Dc[:, i, t0:t0 + tn], start=True, stop=True)
                mm.then_inc(mean_done, 1)

        @block.scalar
        def _(act):
            act.wait_ge(load["b"], 32)
            for n, (d, i) in enumerate(DI):
                act.wait_ge(logits, n + 1)
                if n >= 2:
                    act.wait_ge(gate_done, n - 1)
                x = Dc[:, n % 2, :]
                act.activation(x, UNIT[:, n % 2, 0:T], ACT.Abs, bias=bg[:, d, i:i + 1]).then_inc(abs_done, 1)
                act.wait_ge(abs_done, n + 1)
                act.activation(x, x, ACT.Exp, scale=-1.0).then_inc(exp_of_abs, 1)
                act.wait_ge(exp_of_abs, n + 1)
                act.activation(x, x, ACT.Ln, bias=1.0).then_inc(log_done, 1)
            g = 0
            for i in range(2):
                for c0 in range(0, TILES, 4):
                    n = min(4, TILES - c0)
                    act.wait_ge(v_turned, g + 1)
                    act.copy(V[:, c0:c0 + n, i * P:(i + 1) * P], TR[:, g % 2, 0:n * P].rearrange("p (c f) -> p c f", f=P)).then_inc(v_copied, 1)
                    g += 1
            for n in range(NPAIR + 4):
                act.wait_ge(d_done, 2 * n + 2 if n < NPAIR else 2 * NPAIR + (n - NPAIR) + 1)
                act.activation(Dc[:, n % 2, :], Dc[:, n % 2, :], ACT.Exp, scale=1.0 / GATE_NORM).then_inc(e_done, 1)
            for j, (d, i) in enumerate(DI):
                end = B[:, j, :].rearrange("p (c n) -> p c n", n=CH)[:, :, CH - 1 if d == 0 else 0]
                act.activation(dec[:, j, :], end, ACT.Exp, scale=1.0 / GATE_NORM).then_inc(dec_done, 1)
            act.wait_ge(unit_done, UNITS0)
            for j in range(4):
                act.activation(Qe[:, j, :], B[:, j, :], ACT.Exp, scale=1.0 / GATE_NORM).then_inc(qe_e, 1)
                act.wait_ge(ke_turned, j + 1)
                if j >= 2:
                    act.wait_ge(u_done, 3 * (j - 1))
                act.copy(KeT[:, j % 2, :, :], UNIT[:, j % 2, 0:T].rearrange("p (c f) -> p c f", f=P)).then_inc(ke_copied, 1)
            act.wait_ge(load["go"], 16)
            act.activation(vT[:, :, :], vT[:, :, :], ACT.Silu).then_inc(silu_done, 1)
            act.wait_ge(zeroed, 3)
            for i in range(2):
                act.wait_ge(o_done, i + 1)
                act.copy(X[:, i, :], UNIT[:, i, 0:T]).then_inc(o_copied, 1)
                act.activation(Dc[:, i, :], UNIT[:, i, 0:T], ACT.Square).then_inc(squared, 1)
            for i in range(2):
                act.wait_ge(mean_done, i + 1)
                act.activation(Dc[:, i, :], UNIT[:, i, 0:T], ACT.Sqrt, bias=eps[:, 0:1]).then_inc(rms_done, 1)

        @block.vector
        def _(dve):
            dve.memset(reset[:, :], 1.0).then_inc(reset_one, 1)
            dve.wait_ge(reset_one, 1)
            dve.memset(reset[:, :].rearrange("p (c n) -> p c n", n=CH)[:, :, 0:1], 0.0).then_inc(reset_set, 1)
            dve.wait_ge(reset_set, 1)
            dve.wait_ge(load["b"], 32)
            for n, (d, i) in enumerate(DI):
                dve.wait_ge(abs_done, n + 1)
                dve.tensor_scalar(B[:, n, :], UNIT[:, n % 2, 0:T], bg[:, d, i:i + 1], 0.0, ALU.add, ALU.min).then_inc(min_done, 1)
                dve.wait_ge(min_done, n + 1)
                dve.wait_ge(log_done, n + 1)
                if n >= 2:
                    dve.wait_ge(scanned, n - 1)
                dve.tensor_tensor(X[:, n % 2, :], B[:, n, :], Dc[:, n % 2, :], ALU.subtract).then_inc(gate_done, 1)
                dve.wait_ge(gate_done, n + 1)
                step = 1 if d == 0 else -1
                dve.tensor_tensor_scan(B[:, n, ::step], reset[:, :], X[:, n % 2, ::step], 0.0, ALU.mult, ALU.add).then_inc(scanned, 1)
            dve.wait_ge(load["q"], 16)
            dve.tensor_scalar(q[:, :, :], q[:, :, :], 64 ** -0.5, None, ALU.mult).then_inc(q_scaled, 1)
            dve.wait_ge(q_scaled, 1)
            dve.tensor_scalar(Qe[:, 0:2, :], q[:, :, :], 2.0, None, ALU.mult).then_inc(q_scaled, 1)
            dve.wait_ge(scanned, 4)
            dve.wait_ge(load["mask"], 16)
            dve.wait_ge(zeroed, 3)

            def distances(n):
                i, d, m = n // (2 * NL), n // NL % 2, LEVELS[n % NL]
                b = halves(B[:, 2 * d + i, :], m)
                x = halves(Dc[:, n % 2, :], m)
                nb = T // (2 * m)
                mid = (b[:, :, 0, m - 1:m] if d == 0 else b[:, :, 1, 0:1]).to_broadcast([P, nb, m])
                if n >= 2:
                    dve.wait_ge(x_done, 2 * (n - 1))
                lo, hi = (0, 1) if d == 0 else (1, 0)
                dve.tensor_tensor(x[:, :, lo, :], mid, b[:, :, lo, :], ALU.subtract).then_inc(d_done, 1)
                dve.tensor_tensor(x[:, :, hi, :], b[:, :, hi, :], mid, ALU.subtract).then_inc(d_done, 1)

            def take(unit, i, h, mask):
                dve.wait_ge(unit_done, unit + 1)
                dve.copy_predicated(A[:, i, h, :, :], masks[:, mask:mask + 1, :].to_broadcast([P, NCH, CH]),
                                    UNIT[:, h, 0:T].rearrange("p (c n) -> p c n", n=CH)).then_inc(copied, 1)

            distances(0)
            distances(1)
            for i in range(2):
                for h in range(2):
                    if i or h:
                        dve.wait_ge(copied, 2 * i + h)
                    take(2 * i + h, i, h, 2 * NL)
            for n in range(NPAIR):
                if n + 2 < NPAIR:
                    distances(n + 2)
                for h in range(2):
                    dve.wait_ge(copied, UNITS0 + 2 * n + h)
                    take(UNITS0 + 2 * n + h, n // (2 * NL), h, n % (2 * NL))
            for j, (d, i) in enumerate(DI):
                dve.wait_ge(x_done, 2 * (NPAIR - 1) + 2 + max(0, j - 1))
                b = B[:, j, :].rearrange("p (c n) -> p c n", n=CH)
                end = (b[:, :, CH - 1:CH] if d == 0 else b[:, :, 0:1]).to_broadcast([P, NCH, CH])
                dve.tensor_tensor(Dc[:, j % 2, :].rearrange("p (c n) -> p c n", n=CH), end, b, ALU.subtract).then_inc(d_done, 1)
            dve.wait_ge(dec_done, 4)
            g, n = 0, 0
            for j, (d, i) in enumerate(DI):
                order = ORDER[d]
                for c0 in range(0, NCH - 1, 4):
                    dve.wait_ge(u_done, g + 1)
                    for a in range(min(4, NCH - 1 - c0)):
                        c, nxt = order[c0 + a], order[c0 + a + 1]
                        if n:
                            dve.wait_ge(state, n)
                        for h in range(2):
                            r = slice(64 * h, 64 * h + 64)
                            dve.scalar_tensor_tensor(S[r, j, nxt, r], S[r, j, c, r], dec[r, j, c:c + 1],
                                                     TR[r, g % 2, a * P + 64 * h:a * P + 64 * h + 64], ALU.mult, ALU.add).then_inc(state, 1)
                        n += 2
                    g += 1
            for j, (d, i) in enumerate(DI):
                dve.wait_ge(qe_e, j + 1)
                dve.tensor_tensor(Qe[:, j, :], Qe[:, j, :], q[:, i, :], ALU.mult).then_inc(qe_done, 1)
            dve.wait_ge(silu_done, 1)
            dve.wait_ge(load["g"], 32)
            dve.tensor_scalar(vT[:, :, :], vT[:, :, :], normg[:, 0:1], None, ALU.mult).then_inc(gate_ready, 1)
            for i in range(2):
                dve.wait_ge(rms_done, i + 1)
                dve.reciprocal(Dc[:, i, :], Dc[:, i, :]).then_inc(inv_done, 1)
                dve.wait_ge(inv_done, i + 1)
                dve.tensor_tensor(X[:, i, :], X[:, i, :], Dc[:, i, :], ALU.mult).then_inc(normed, 1)
                dve.wait_ge(normed, i + 1)
                dve.wait_ge(gate_ready, 1)
                dve.tensor_tensor(X[:, i, :], X[:, i, :], vT[:, i, :], ALU.mult).then_inc(gated, 1)


def sliding_window_attention(nc, t, res, layer, tiles):
    with nc.cleanup_on_exit(), ExitStack() as ctx:
        sb, ps, sem = allocators(nc, ctx, f"swa{layer}_")
        nm = f"swa{layer}_"
        ident = res["ident"]
        H, G = SWA_HEADS, SWA_HEADS // 2
        UN = 2 * H
        DIVIDE, TURN, WEIGH, TAKE, OUT_TURN, STORE = 1, 2, 3, 4, 5, 6
        first_pair, end_pair = tiles[0] // 2, tiles[-1] // 2 + 1
        first_latent = CTX_TILES // 2
        pairs = end_pair - first_pair
        RING = 4
        khh = sb(nm + "khh", [P, 2, PAD_T], F32R)
        klo = sb(nm + "klo", [64, 2, PAD_T], F32R)
        qhl = sb(nm + "qhl", [P, 2, H, P], F32R)
        bias = sb(nm + "bias", [P, 2, 2 * P])
        vT = sb(nm + "vT", [P, PAD_T])
        V = sb(nm + "V", [P, TILES + 1, P])
        sink = sb(nm + "sink", [P, H])
        nsink = sb(nm + "nsink", [P, H])
        mx = sb(nm + "mx", [P, 2])
        neg = sb(nm + "negmax", [P, 2])
        den = sb(nm + "den", [P, RING])
        es = sb(nm + "esink", [P, RING])
        den2 = sb(nm + "den2", [P, RING])
        rden = sb(nm + "rden", [P, RING])
        pr = sb(nm + "p", [P, RING, SWA_KEYS])
        pT = sb(nm + "pT", [P, 2, SWA_KEYS])
        o = sb(nm + "o", [P, 2, H * SWA_DH])
        oT = sb(nm + "oT", [P, 2, G, P])
        SC = ps(nm + "scores", [P, 2, 2 * BANK])
        TR = ps(nm + "tr", [P, 2 * BANK])
        O = ps(nm + "o_acc", [P, 2, BANK])
        const_in, k_in = sem("const_in"), sem("k_in")
        tile_in = [sem(f"tile_in{s}") for s in range(2)]
        nsink_done, v_turned, v_copied = sem("nsink_done"), sem("v_turned"), sem("v_copied")
        scores, masked, max_done, neg_done, exp_done, sink_done = (
            sem("scores"), sem("masked"), sem("max_done"), sem("neg_done"), sem("exp_done"), sem("sink_done"))
        den_done, rden_done, p_done, turned, copied, pv_done = (
            sem("den_done"), sem("rden_done"), sem("p_done"), sem("turned"), sem("copied"), sem("pv_done"))
        o_taken, o_turned, o_copied, passed = sem("o_taken"), sem("o_turned"), sem("o_copied"), sem("passed")
        stored = [sem(f"stored{s}") for s in range(2)]
        scale = SWA_DH ** -0.5
        block = ctx.enter_context(nc.Block())
        VG = [(0, 8), (8, 3)]

        def done(i, u):
            return (i - first_pair) * UN + u + 1

        def blocks(i, u):
            return (i - first_pair) * 2 + u // H + 1

        def is_ctx(i):
            return isinstance(i, int) and i == 0

        def ends_block(r, lag):
            return (r - lag) % H == H - 1

        def stagger(eng, step):
            if first_pair < first_latent:
                staggered(eng, first_pair, first_latent, UN, STORE, step)
            staggered(eng, first_latent, end_pair, UN, STORE, step)

        @block.sync
        def _(sp):
            heads = t["heads"]
            for half in range(2):
                sp.dma_start(khh[64 * half:64 * half + 64, :, :].bitcast(F32), heads[0, HEAD_SK:HEAD_SK + P, :].rearrange("(g p) n -> p g n", p=64)).then_inc(k_in, 16)
            sp.dma_start(klo[:, :, :].bitcast(F32), heads[1, HEAD_SK:HEAD_SK + P, :].rearrange("(g p) n -> p g n", p=64)).then_inc(k_in, 16)

            def body(i, first):
                for s in range(2):
                    if not first:
                        sp.wait_ge(scores, done(i, s * H + H - 1) - UN)
                        sp.wait_ge(max_done, done(i, s * H + H - 1) - UN)
                    at = i * 2 * P + s * P
                    for part in range(2):
                        sp.dma_start(qhl[64 * part:64 * part + 64, s, :, :].bitcast(F32),
                                     heads[part, HEAD_SQ:HEAD_SQ + G * P, bass.ds(at, P)].rearrange("(a p) n -> p a n", p=64)).then_inc(tile_in[s], 16)
                    sp.dma_start(bias[:, s, :], t["swa_bias"][bass.ds(0 if is_ctx(i) else at - N_CTX, P), :]).then_inc(tile_in[s], 16)
            peeled(sp, first_pair, end_pair, body)

        @block.gpsimd
        def _(pool):
            pool.dma_start(vT[:, :], t["proj"][T_SV * P:(T_SV + 1) * P, :]).then_inc(const_in, 16)
            pool.dma_start(sink[:, :], t["swa_sink"][layer:layer + 1, :].to_broadcast([P, H])).then_inc(const_in, 16)
            pool.wait_ge(const_in, 32)

            def step(i, r, live):
                keys = N_CTX if is_ctx(i) else SWA_KEYS
                if live(DIVIDE):
                    u = r - DIVIDE
                    b = u % RING
                    wait_apart(pool, rden_done, done(i, u), passed)
                    pool.tensor_scalar(pr[:, b, 0:keys], pr[:, b, 0:keys], rden[:, b:b + 1], 1.0, ALU.mult, ALU.mult).then_inc(p_done, 1)
            stagger(pool, step)

        @block.tensor
        def _(pe):
            pe.wait_ge(const_in, 32)
            for g, (a, n) in enumerate(VG):
                if g:
                    pe.wait_ge(v_copied, g)
                for c in range(n):
                    mm = pe.transpose(TR[:, c * P:(c + 1) * P], vT[:, (a + c) * P:(a + c + 1) * P], ident[:, :])
                mm.then_inc(v_turned, 1)
            pe.wait_ge(v_copied, 2)
            pe.wait_ge(k_in, 48)

            def step(i, r, live):
                kt = 2 if is_ctx(i) else 5
                if live(0):
                    s, h = r // H, r % H
                    g, j = h // G, h % G
                    if h == 0:
                        pe.wait_ge(tile_in[s], (i - first_pair) * 48 + 48)
                    wait_count(pe, exp_done, done(i, r) - 2)
                    parts = [(slice(0, N_CTX), slice(0, N_CTX))]
                    if kt == 5:
                        at = i * 2 * P + (s - 1) * P
                        parts += [(slice(N_CTX, BANK), bass.ds(at, 2 * P)), (slice(BANK, BANK + P), bass.ds(at + 2 * P, P))]
                    for cols, keys in parts:
                        pe.matmul(SC[:, r % 2, cols], qhl[:, s, 2 * j + g, :], khh[:, g, keys], start=True, stop=False)
                        mm = pe.matmul(SC[:, r % 2, cols], qhl[0:64, s, 2 * j + g, :], klo[:, g, keys], start=False, stop=True)
                    mm.then_inc(scores, 1)
                if live(TURN):
                    u = r - TURN
                    pe.wait_ge(p_done, done(i, u))
                    wait_count(pe, copied, done(i, u) - 1)
                    for c in range(kt):
                        mm = pe.transpose(TR[:, c * P:(c + 1) * P], pr[:, u % RING, c * P:(c + 1) * P], ident[:, :])
                    mm.then_inc(turned, 1)
                if live(WEIGH):
                    u = r - WEIGH
                    s, h = u // H, u % H
                    pe.wait_ge(copied, done(i, u))
                    if h == 0:
                        wait_count(pe, o_copied, blocks(i, u) - 2)
                    vcols = slice(64 * (h // G), 64 * (h // G) + 64)
                    for c in range(kt):
                        v = V[:, c, vcols] if c < 2 else V[:, bass.ds(i * 2 + (s - 1 + c - 2), 1), vcols].rearrange("p a b -> p (a b)")
                        mm = pe.matmul(O[:, s % 2, 64 * h:64 * h + 64], pT[:, u % 2, c * P:(c + 1) * P], v, start=(c == 0), stop=(c == kt - 1))
                    mm.then_inc(pv_done, 1)
                if ends_block(r, OUT_TURN) and live(OUT_TURN):
                    u = r - OUT_TURN
                    s = u // H % 2
                    pe.wait_ge(o_taken, blocks(i, u))
                    for g in range(G):
                        mm = pe.transpose(O[:, s, g * P:(g + 1) * P], o[:, s, g * P:(g + 1) * P], ident[:, :])
                    mm.then_inc(o_turned, 1)
            stagger(pe, step)

        @block.scalar
        def _(act):
            for g, (a, n) in enumerate(VG):
                act.wait_ge(v_turned, g + 1)
                act.copy(V[:, a:a + n, :], TR[:, 0:n * P].rearrange("p (c f) -> p c f", f=P)).then_inc(v_copied, 1)
            act.wait_ge(const_in, 32)

            def step(i, r, live):
                keys = N_CTX if is_ctx(i) else SWA_KEYS
                if live(TURN):
                    u = r - TURN
                    act.wait_ge(turned, done(i, u))
                    wait_count(act, pv_done, done(i, u) - 2)
                    act.copy(pT[:, u % 2, 0:keys], TR[:, 0:keys]).then_inc(copied, 1)
                if ends_block(r, TAKE) and live(TAKE):
                    u = r - TAKE
                    s = u // H % 2
                    act.wait_ge(pv_done, done(i, u))
                    wait_count(act, o_turned, blocks(i, u) - 2)
                    act.copy(o[:, s, :], O[:, s, :]).then_inc(o_taken, 1)
                if live(0):
                    b = r % RING
                    act.wait_ge(neg_done, done(i, r))
                    wait_count(act, turned, done(i, r) - RING)
                    wait_count(act, den_done, done(i, r) - RING)
                    act.activation(pr[:, b, 0:keys], SC[:, r % 2, 0:keys], ACT.Exp, bias=neg[:, r % 2:r % 2 + 1],
                                   scale=scale, accum_out=den[:, b:b + 1]).then_inc(exp_done, 1)
                    act.activation(es[:, b:b + 1], sink[:, r % H:r % H + 1], ACT.Exp, bias=neg[:, r % 2:r % 2 + 1]).then_inc(sink_done, 1)
                if ends_block(r, STORE) and live(STORE):
                    u = r - STORE
                    s = u // H % 2
                    act.wait_ge(o_turned, blocks(i, u))
                    wait_count(act, stored[s], ((i - first_pair) + u // (2 * H)) * 16)
                    act.copy(oT[:, s, :, :], O[:, s, :].rearrange("p (g n) -> p g n", g=G)).then_inc(o_copied, 1)
                    act.wait_ge(o_copied, blocks(i, u))
                    act.dma_start(t["mix"][4 * P:D, bass.ds(i * 2 * P + u // H * P, P)].rearrange("(g p) n -> p g n", p=P), oT[:, s, :, :]).then_inc(stored[s], 16)
            stagger(act, step)
            for s in range(2):
                act.wait_ge(stored[s], 16 * pairs)

        @block.vector
        def _(dve):
            dve.wait_ge(const_in, 32)
            dve.tensor_scalar(nsink[:, :], sink[:, :], -1.0, None, ALU.mult).then_inc(nsink_done, 1)
            dve.wait_ge(nsink_done, 1)

            def step(i, r, live):
                if live(0):
                    b = r % 2
                    s, h = r // H, r % H
                    if h == 0:
                        dve.wait_ge(tile_in[s], (i - first_pair) * 48 + 48)
                    dve.wait_ge(scores, done(i, r))
                    keys = N_CTX
                    if not is_ctx(i):
                        keys = SWA_KEYS
                        for a, c in ((0, N_CTX), (P, BANK)):
                            dve.tensor_tensor(SC[:, b, c:c + P], SC[:, b, c:c + P], bias[:, s, a:a + P], ALU.add).then_inc(masked, 1)
                        dve.wait_ge(masked, (done(i, r) - (first_latent - first_pair) * UN) * 2)
                    wait_count(dve, sink_done, done(i, r) - 2)
                    dve.reduce_max(mx[:, b:b + 1], SC[:, b, 0:keys], AX.X).then_inc(max_done, 1)
                    dve.wait_ge(max_done, done(i, r))
                    dve.scalar_tensor_tensor(neg[:, b:b + 1], mx[:, b:b + 1], -scale, nsink[:, h:h + 1], ALU.mult, ALU.min).then_inc(neg_done, 1)
                if live(DIVIDE):
                    u = r - DIVIDE
                    b = u % RING
                    dve.wait_ge(sink_done, done(i, u))
                    wait_count(dve, p_done, done(i, u) - RING)
                    dve.tensor_tensor(den2[:, b:b + 1], den[:, b:b + 1], es[:, b:b + 1], ALU.add).then_inc(den_done, 1)
                    dve.wait_ge(den_done, done(i, u))
                    dve.reciprocal(rden[:, b:b + 1], den2[:, b:b + 1]).then_inc(rden_done, 1)
            stagger(dve, step)


def differential_attention(nc, t, res, layer, tiles):
    with nc.cleanup_on_exit(), ExitStack() as ctx:
        sb, ps, sem = allocators(nc, ctx, f"diff{layer}_")
        nm = f"diff{layer}_"
        ident = res["ident"]
        H = DIFF_HEADS
        UN = 2 * H
        LAG = 3
        lam_init = 0.8 - 0.6 * math.exp(-0.3 * layer)
        scale = DIFF_DH ** -0.5
        first_pair, end_pair = tiles[0] // 2, tiles[-1] // 2 + 1
        first_latent = CTX_TILES // 2
        KEYCH = [(0, 512), (512, 512), (1024, 256)]
        t0, tn = tiles[0] * P, len(tiles) * P
        ks = sb(nm + "k", [96, UN, T], F32R)
        qs = sb(nm + "q", [96, 2, UN, P], F32R)
        vT = sb(nm + "vT", [P, 2, T])
        V = sb(nm + "V", [P, TILES, 2 * P])
        lamv = sb(nm + "lamv", [P, 4, DIFF_DH])
        lprod = sb(nm + "lprod", [P, 2, DIFF_DH])
        lsum = sb(nm + "lsum", [P, 2])
        lexp = sb(nm + "lexp", [P, 2])
        ldiff = sb(nm + "ldiff", [P, 1])
        nlam = sb(nm + "nlam", [P, 1])
        g1 = sb(nm + "g", [P, 1])
        block_mean = sb(nm + "block_mean", [P, P])
        eps = sb(nm + "eps", [P, 1])
        mx = sb(nm + "mx", [P, 2])
        ng = sb(nm + "negmax", [P, 2])
        den = sb(nm + "den", [P, 2, 2])
        rden = sb(nm + "rden", [P, 2, 2])
        r1 = sb(nm + "r1", [P, 2])
        E = sb(nm + "e", [P, 2, 2, T])
        W = sb(nm + "w", [P, 2, T])
        WT = sb(nm + "wT", [P, 2, T])
        oT = sb(nm + "oT", [P, 2, T])
        SC = ps(nm + "scores", [P, 2, 3 * BANK])
        TR = ps(nm + "tr", [P, 2, BANK])
        const_in, k_in, eps_set = sem("const_in"), sem("k_in"), sem("eps_set")
        q_in = [sem(f"q_in{s}") for s in range(2)]
        lam, lam_exp = sem("lam"), sem("lam_exp")
        v_turned, v_copied = sem("v_turned"), sem("v_copied")
        scores, max_done, neg_done, exp_done, rden_done, r1_done, w0_done, w_done = (
            sem("scores"), sem("max_done"), sem("neg_done"), sem("exp_done"), sem("rden_done"), sem("r1_done"), sem("w0_done"), sem("w_done"))
        turned = [sem(f"turned{g}") for g in range(3)]
        copied = [sem(f"copied{g}") for g in range(3)]
        pv_done, o_done, passed = sem("pv_done"), sem("o_done"), sem("passed")
        sq_done, mean_done, rms_done, inv_done, normed, stored = (
            sem("sq_done"), sem("mean_done"), sem("rms_done"), sem("inv_done"), sem("normed"), sem("stored"))
        block = ctx.enter_context(nc.Block())
        VG = [(i, a, min(4, TILES - a)) for i in range(2) for a in range(0, TILES, 4)]
        units = (end_pair - first_pair) * UN

        def done(i, u):
            return (i - first_pair) * UN + u + 1

        def is_ctx(i):
            return isinstance(i, int) and i == 0

        def groups(i):
            return [(0, 1), (1, 1)] if is_ctx(i) else [(0, 3), (3, 4), (7, 3)]

        def third(i, u):
            return done(i, u) - (first_latent - first_pair) * UN

        def stagger(eng, step):
            if first_pair < first_latent:
                staggered(eng, first_pair, first_latent, UN, LAG, step)
            staggered(eng, first_latent, end_pair, UN, LAG, step)

        @block.sync
        def _(sp):
            heads = t["heads"]
            for j, part in enumerate((0, 1, 0)):
                sp.dma_start(ks[32 * j:32 * j + 32, :, :].bitcast(F32), heads[part, HEAD_DK:HEAD_DK + 2 * P, 0:T].rearrange("(a p) n -> p a n", p=32)).then_inc(k_in, 16)

            def body(i, first):
                for s in range(2):
                    if not first:
                        sp.wait_ge(scores, 2 * (done(i, s * H + H - 1) - UN))
                    for j, part in enumerate((0, 0, 1)):
                        sp.dma_start(qs[32 * j:32 * j + 32, s, :, :].bitcast(F32),
                                     heads[part, HEAD_DQ:HEAD_DQ + 2 * P, bass.ds(i * 2 * P + s * P, P)].rearrange("(a p) n -> p a n", p=32)).then_inc(q_in[s], 16)
            peeled(sp, first_pair, end_pair, body)
            for i in range(2):
                sp.wait_ge(normed, i + 1)
                sp.dma_start(t["mix"][(2 + i) * P:(3 + i) * P, t0:t0 + tn], oT[:, i, t0:t0 + tn]).then_inc(stored, 16)
            sp.wait_ge(stored, 32)

        @block.tensor
        def _(pe):
            pe.wait_ge(const_in, 80)
            for g, (i, a, n) in enumerate(VG):
                if g >= 2:
                    pe.wait_ge(v_copied, g - 1)
                for c in range(n):
                    mm = pe.transpose(TR[:, g % 2, c * P:(c + 1) * P], vT[:, i, (a + c) * P:(a + c + 1) * P], ident[:, :])
                mm.then_inc(v_turned, 1)
            pe.wait_ge(v_copied, len(VG))
            pe.wait_ge(k_in, 48)

            def turn(i, u, g):
                a, n = groups(i)[g]
                for c in range(n):
                    mm = pe.transpose(TR[:, g % 2, c * P:(c + 1) * P], W[:, u % 2, (a + c) * P:(a + c + 1) * P], ident[:, :])
                mm.then_inc(turned[g], 1)

            def step(i, r, live):
                if live(0):
                    s, h = r // H, r % H
                    if h == 0:
                        pe.wait_ge(q_in[s], (i - first_pair) * 48 + 48)
                    for c in range(2):
                        wait_count(pe, exp_done, 2 * (done(i, r) - 1) + c - 1)
                        for a, n in KEYCH[:1 if is_ctx(i) else 3]:
                            n = min(n, N_CTX) if is_ctx(i) else n
                            mm = pe.matmul(SC[:, c, a:a + n], qs[:, s, 2 * h + c, :], ks[:, 2 * h + c, a:a + n], start=True, stop=True)
                        mm.then_inc(scores, 1)
                if live(2):
                    u = r - 2
                    pe.wait_ge(w_done, done(i, u))
                    wait_count(pe, copied[0], done(i, u) - 1)
                    if not is_ctx(i):
                        wait_count(pe, copied[2], third(i, u) - 1)
                    turn(i, u, 0)
                    wait_count(pe, o_done, done(i, u) - (1 if live.starts and u == 0 else 2))
                    turn(i, u, 1)
                    if not is_ctx(i):
                        pe.wait_ge(copied[0], done(i, u))
                        turn(i, u, 2)
                if live(3):
                    u, h = r - 3, (r - 3) % H
                    pe.wait_ge(copied[1], done(i, u) + (1 if live(2) else 0))
                    wait_count(pe, o_done, done(i, u) - 1)
                    if not is_ctx(i):
                        pe.wait_ge(copied[2], third(i, u))
                    tiles_ = groups(i)[-1][0] + groups(i)[-1][1]
                    for c in range(tiles_):
                        mm = pe.matmul(TR[64 * (h % 2):64 * (h % 2) + 64, 1, 0:P], V[:, c, 64 * h:64 * h + 64],
                                       WT[:, u % 2, c * P:(c + 1) * P], start=(c == 0), stop=(c == tiles_ - 1))
                    mm.then_inc(pv_done, 1)
            stagger(pe, step)

            for i in range(2):
                pe.wait_ge(sq_done, i + 1)
                for a, n in KEYCH:
                    n = min(n, tn - a)
                    if n > 0:
                        mm = pe.matmul(SC[:, i, a:a + n], block_mean[:, :], E[:, 0, i, a:a + n], start=True, stop=True)
                mm.then_inc(mean_done, 1)

        @block.scalar
        def _(act):
            for g, (i, a, n) in enumerate(VG):
                act.wait_ge(v_turned, g + 1)
                act.copy(V[:, a:a + n, i * P:(i + 1) * P], TR[:, g % 2, 0:n * P].rearrange("p (c f) -> p c f", f=P)).then_inc(v_copied, 1)
            act.wait_ge(lam, 4)
            act.activation(lexp[:, :], lsum[:, :], ACT.Exp).then_inc(lam_exp, 1)
            act.wait_ge(eps_set, 1)

            def step(i, r, live):
                keys = (CTX_TILES if is_ctx(i) else TILES) * P

                def exponentials(c):
                    act.wait_ge(neg_done, 2 * (done(i, r) - 1) + c + 1)
                    if c == 0:
                        wait_count(act, w_done, done(i, r) - 2)
                    act.activation(E[:, r % 2, c, 0:keys], SC[:, c, 0:keys], ACT.Exp, bias=ng[:, c:c + 1], scale=scale,
                                   accum_out=den[:, r % 2, c:c + 1]).then_inc(exp_done, 1)

                def take(u, g):
                    a, n = groups(i)[g]
                    act.wait_ge(turned[g], third(i, u) if g == 2 else done(i, u))
                    if g == 0:
                        wait_count(act, pv_done, done(i, u) - 2)
                    act.copy(WT[:, u % 2, a * P:(a + n) * P], TR[:, g % 2, 0:n * P]).then_inc(copied[g], 1)

                if live(2):
                    take(r - 2, 0)
                    take(r - 2, 1)
                if live(0):
                    exponentials(0)
                if live(2) and not is_ctx(i):
                    take(r - 2, 2)
                if live(0):
                    exponentials(1)
            stagger(act, step)

            act.wait_ge(o_done, units)
            act.wait_ge(w_done, units)
            for i in range(2):
                act.activation(E[:, 0, i, 0:tn], oT[:, i, t0:t0 + tn], ACT.Square).then_inc(sq_done, 1)
            for i in range(2):
                act.wait_ge(mean_done, i + 1)
                act.activation(E[:, 1, i, 0:tn], SC[:, i, 0:tn], ACT.Sqrt, bias=eps[:, 0:1]).then_inc(rms_done, 1)

        @block.gpsimd
        def _(pool):
            pool.dma_start(vT[:, :, :], t["proj"][T_DV * P:(T_DV + 2) * P, 0:T].rearrange("(i p) n -> p i n", p=P)).then_inc(const_in, 16)
            pool.dma_start(lamv[:, :, :].rearrange("p a b -> p (a b)"), t["diff_lambda"][layer:layer + 1, :, :].rearrange("l a b -> l (a b)").to_broadcast([P, 4 * DIFF_DH])).then_inc(const_in, 16)
            for h in range(2):
                pool.dma_start(g1[h * 64:(h + 1) * 64, :], t["diff_norm_g"][layer].rearrange("(p a) -> p a", a=1)).then_inc(const_in, 16)
            pool.dma_start(block_mean[:, :], t["block_mean"]).then_inc(const_in, 16)
            pool.memset(eps[:, :], EPS).then_inc(eps_set, 1)
            pool.wait_ge(const_in, 80)

            def step(i, r, live):
                keys = (CTX_TILES if is_ctx(i) else TILES) * P
                if live(1):
                    u = r - 1
                    if is_ctx(i) or (live.starts and u < 2):
                        wait_count(pool, turned[1], done(i, u) - 2)
                    else:
                        pool.wait_ge(turned[2], third(i, u) - 2)
                    wait_apart(pool, rden_done, done(i, u), passed)
                    pool.tensor_scalar(W[:, u % 2, 0:keys], E[:, u % 2, 0, 0:keys], rden[:, u % 2, 0:1], 1.0, ALU.mult, ALU.mult).then_inc(w0_done, 1)
            stagger(pool, step)

        @block.vector
        def _(dve):
            dve.wait_ge(const_in, 80)
            for a in range(2):
                dve.tensor_tensor(lprod[:, a, :], lamv[:, 2 * a, :], lamv[:, 2 * a + 1, :], ALU.mult).then_inc(lam, 1)
            dve.tensor_scalar(g1[:, :], g1[:, :], 1.0 - lam_init, None, ALU.mult).then_inc(lam, 1)
            dve.wait_ge(lam, 3)
            dve.reduce_sum(lsum[:, :], lprod[:, :, :], AX.X).then_inc(lam, 1)
            dve.wait_ge(lam_exp, 1)
            dve.tensor_tensor(ldiff[:, :], lexp[:, 1:2], lexp[:, 0:1], ALU.subtract).then_inc(lam, 1)
            dve.wait_ge(lam, 5)
            dve.tensor_scalar(nlam[:, :], ldiff[:, :], -lam_init, None, ALU.add).then_inc(lam, 1)
            dve.wait_ge(lam, 6)

            def step(i, r, live):
                keys = (CTX_TILES if is_ctx(i) else TILES) * P
                for c in range(2):
                    if live(0):
                        n = 2 * (done(i, r) - 1) + c + 1
                        dve.wait_ge(scores, n)
                        dve.reduce_max(mx[:, c:c + 1], SC[:, c, 0:keys], AX.X).then_inc(max_done, 1)
                        dve.wait_ge(max_done, n)
                        dve.tensor_scalar(ng[:, c:c + 1], mx[:, c:c + 1], -scale, None, ALU.mult).then_inc(neg_done, 1)
                    if live(1) and c == 0:
                        u, b = r - 1, (r - 1) % 2
                        dve.wait_ge(exp_done, 2 * done(i, u))
                        dve.reciprocal(rden[:, b, :], den[:, b, :]).then_inc(rden_done, 1)
                        dve.wait_ge(rden_done, done(i, u))
                        dve.tensor_scalar(r1[:, b:b + 1], rden[:, b, 1:2], nlam[:, 0:1], None, ALU.mult).then_inc(r1_done, 1)
                if live(1):
                    u, b = r - 1, (r - 1) % 2
                    dve.wait_ge(w0_done, done(i, u))
                    dve.wait_ge(r1_done, done(i, u))
                    dve.scalar_tensor_tensor(W[:, b, 0:keys], E[:, b, 1, 0:keys], r1[:, b:b + 1], W[:, b, 0:keys], ALU.mult, ALU.add).then_inc(w_done, 1)
                if live(3):
                    u = r - 3
                    h, rows = u % H, slice(64 * (u % 2), 64 * (u % 2) + 64)
                    dve.wait_ge(pv_done, done(i, u))
                    dve.tensor_copy(oT[rows, h // 2, bass.ds(i * 2 * P + u // H * P, P)], TR[rows, 1, 0:P]).then_inc(o_done, 1)
            stagger(dve, step)

            for i in range(2):
                o = oT[:, i, t0:t0 + tn]
                dve.wait_ge(rms_done, i + 1)
                dve.reciprocal(E[:, 1, i, 0:tn], E[:, 1, i, 0:tn]).then_inc(inv_done, 1)
                dve.wait_ge(inv_done, i + 1)
                dve.scalar_tensor_tensor(o, o, g1[:, 0:1], E[:, 1, i, 0:tn], ALU.mult, ALU.mult).then_inc(normed, 1)


def swiglu(nc, t, res, layer, chunks):
    with nc.cleanup_on_exit(), ExitStack() as ctx:
        sb, ps, sem = allocators(nc, ctx, f"ffn{layer}_")
        nm = f"ffn{layer}_"
        uhi, ulo, Y = res["uhi"], res["ulo"], res["y"]
        NC = len(chunks)
        order = [tt for t0, tn in chunks for tt in range(t0 // P, (t0 + tn) // P)]
        chunk_of = {tt: c for c, (t0, tn) in enumerate(chunks) for tt in range(t0 // P, (t0 + tn) // P)}
        NY = 2 * len(order)
        raw = sb(nm + "raw", [P, 3, D])
        whi = sb(nm + "whi", [P, 3, D], F32R)
        wlo = sb(nm + "wlo", [P, 3, D], F32R)
        sg = sb(nm + "silu", [P, NC, BANK])
        hf = sb(nm + "hid", [P, NC, BANK])
        hhi = sb(nm + "hhi", [P, 2, T], F32R)
        hlo = sb(nm + "hlo", [P, 2, T], F32R)
        GT = ps(nm + "gate", [P, 3, BANK])
        UP = ps(nm + "up", [P, 3, BANK])
        ACC = ps(nm + "acc", [P, 2, BANK])
        raw_in = [sem(f"raw_in{s}") for s in range(3)]
        passed = sem("passed")
        w_hi, w_ready = sem("w_hi"), sem("w_ready")
        gate_done, up_done, silu_done, mul_done = sem("gate_done"), sem("up_done"), sem("silu_done"), sem("mul_done")
        hid_hi, hid_ready, y_done, y_added, y_zero = sem("hid_hi"), sem("hid_ready"), sem("y_done"), sem("y_added"), sem("y_zero")
        block = ctx.enter_context(nc.Block())
        G = FFN_GROUPS

        def grouped(eng, body):
            body(0, True, False)
            with eng.Fori(1, G - 1) as g:
                body(g, False, False)
            body(G - 1, False, True)

        @block.sync
        def _(sp):
            def body(g, first, last):
                for j in range(6):
                    if not (first and j < 3):
                        sp.wait_ge(w_ready, g * 6 + j - 2)
                    sp.dma_start(raw[:, j % 3, :], t["w_ffn"][layer][bass.ds(g * 6 * P + j * P, P), :]).then_inc(raw_in[j % 3], 16)
            grouped(sp, body)

        def release(eng, g, j):
            if j == 0:
                eng.wait_ge(up_done, g * 2 * NC)
            elif j in (1, 2):
                eng.wait_ge(y_done, g * NY)
            elif j == 3:
                eng.wait_ge(gate_done, g * 2 * NC + NC)
            elif j == 4:
                eng.wait_ge(up_done, g * 2 * NC + NC)
            else:
                eng.wait_ge(gate_done, g * 2 * NC + 2 * NC)

        @block.scalar
        def _(act):
            def split(g, j, reused=True):
                if reused:
                    release(act, g, j)
                act.wait_ge(raw_in[j % 3], g * 32 + (j // 3) * 16 + 16)
                act.copy(whi[:, j % 3, :], raw[:, j % 3, :]).then_inc(w_hi, 1)

            def silu(g, f, first):
                for c, (t0, tn) in enumerate(chunks):
                    n = g * 2 * NC + f * NC + c
                    act.wait_ge(gate_done, n + 1)
                    if not (first and f == 0):
                        act.wait_ge(mul_done, n + 1 - NC)
                    act.activation(sg[:, c, 0:tn], GT[:, c, 0:tn], ACT.Silu).then_inc(silu_done, 1)

            def body(g, first, last):
                silu(g, 0, first)
                split(g, 3)
                split(g, 4)
                silu(g, 1, first)
                split(g, 5)
                if not last:
                    for j in range(3):
                        split(g + 1, j)
            for j in range(3):
                split(0, j, False)
            grouped(act, body)

        @block.gpsimd
        def _(pool):
            pool.memset(Y[:, :, :], 0.0).then_inc(y_zero, 1)

            def split(g, j):
                pool.wait_ge(w_hi, g * 6 + j + 1)
                pool.tensor_tensor(wlo[:, j % 3, :], raw[:, j % 3, :], whi[:, j % 3, :].bitcast(F32), ALU.subtract).then_inc(w_ready, 1)

            def hidden(g, f):
                for c, (t0, tn) in enumerate(chunks):
                    n = g * 2 * NC + f * NC + c + 1
                    wait_apart(pool, mul_done, n, passed)
                    pool.tensor_copy(hhi[:, f, t0:t0 + tn], hf[:, c, 0:tn]).then_inc(hid_hi, 1)
                    pool.wait_ge(hid_hi, n)
                    pool.tensor_tensor(hlo[:, f, t0:t0 + tn], hf[:, c, 0:tn], hhi[:, f, t0:t0 + tn].bitcast(F32), ALU.subtract).then_inc(hid_ready, 1)

            def body(g, first, last):
                split(g, 3)
                hidden(g, 0)
                split(g, 4)
                split(g, 5)
                hidden(g, 1)
                if not last:
                    for j in range(3):
                        split(g + 1, j)
            for j in range(3):
                split(0, j)
            grouped(pool, body)

        @block.tensor
        def _(pe):
            def body(g, first, last):
                for f in range(2):
                    for which, (bank, done, freed) in enumerate(((GT, gate_done, silu_done), (UP, up_done, mul_done))):
                        j = 2 * f + which
                        w = [x[:, j % 3, :].rearrange("p (k n) -> p k n", k=KT) for x in (whi, wlo)]
                        pe.wait_ge(w_ready, g * 6 + j + 1)
                        for c, (t0, tn) in enumerate(chunks):
                            if not (first and f == 0):
                                pe.wait_ge(freed, g * 2 * NC + f * NC + c + 1 - NC)
                            for k in range(KT):
                                mm = product(pe, bank[:, c, 0:tn], w[0][:, k, :], w[1][:, k, :],
                                             uhi[:, k, t0:t0 + tn], ulo[:, k, t0:t0 + tn], k == 0, k == KT - 1)
                            mm.then_inc(done, 1)
                pe.wait_ge(w_ready, g * 6 + 6)
                for n, tt in enumerate(order):
                    pe.wait_ge(hid_ready, g * 2 * NC + NC + chunk_of[tt] + 1)
                    for half in range(2):
                        if not (first and n == 0):
                            pe.wait_ge(y_added, g * NY + 2 * n + half - 1)
                        cols, rows = slice(half * BANK, (half + 1) * BANK), slice(tt * P, (tt + 1) * P)
                        for f in range(2):
                            s = (4 + f) % 3
                            mm = product(pe, ACC[:, half, :], hhi[:, f, rows], hlo[:, f, rows],
                                         whi[:, s, cols], wlo[:, s, cols], f == 0, f == 1)
                        mm.then_inc(y_done, 1)
            grouped(pe, body)

        @block.vector
        def _(dve):
            dve.wait_ge(y_zero, 1)

            def body(g, first, last):
                for f in range(2):
                    for c, (t0, tn) in enumerate(chunks):
                        n = g * 2 * NC + f * NC + c + 1
                        dve.wait_ge(silu_done, n)
                        dve.wait_ge(up_done, n)
                        if not (first and f == 0):
                            dve.wait_ge(hid_ready, n - NC)
                        dve.tensor_tensor(hf[:, c, 0:tn], UP[:, c, 0:tn], sg[:, c, 0:tn], ALU.mult).then_inc(mul_done, 1)
                for n, tt in enumerate(order):
                    for half in range(2):
                        cols = slice(half * BANK, (half + 1) * BANK)
                        dve.wait_ge(y_done, g * NY + 2 * n + half + 1)
                        dve.tensor_tensor(Y[:, tt, cols], ACC[:, half, :], Y[:, tt, cols], ALU.add).then_inc(y_added, 1)
            grouped(dve, body)


def build(nc, t):
    with ExitStack() as outer:
        outer.enter_context(nc.allow_non_contiguous_dma(reason="columns of modulation and gate biases: a few KB"))
        ident = outer.enter_context(nc.sbuf_tensor("ident", [P, P], F32))
        res = {"ident": ident, "silu_c": outer.enter_context(nc.sbuf_tensor("silu_c", [P, KT, 2], F32))}
        with nc.cleanup_on_exit(), ExitStack() as ctx:
            ident_in = nc.alloc_semaphore("ident_in")
            block = ctx.enter_context(nc.Block())

            @block.sync
            def _(sp):
                sp.dma_start(ident[:, :], t["ident"]).then_inc(ident_in, 16)
                sp.wait_ge(ident_in, 16)

        def operand(ctx, name):
            res["uhi"] = ctx.enter_context(nc.sbuf_tensor(name + "_uhi", [P, KT, T], F32R))
            res["ulo"] = ctx.enter_context(nc.sbuf_tensor(name + "_ulo", [P, KT, T], F32R))

        everything = list(range(TILES))
        modulation(nc, t, res)
        for layer in range(LAYERS):
            last = layer == LAYERS - 1
            tiles = everything[CTX_TILES:] if last else everything
            if layer == 0:
                with ExitStack() as ctx:
                    operand(ctx, "first")
                    norm_tiles(nc, t, res, "input", layer, everything, False)
                    input_projection(nc, t, res, layer)
            gated_linear_attention(nc, t, res, layer)
            differential_attention(nc, t, res, layer, tiles)
            sliding_window_attention(nc, t, res, layer, tiles)
            with ExitStack() as ctx:
                operand(ctx, f"second{layer}")
                norm_tiles(nc, t, res, "attention", layer, tiles, False)
                with ExitStack() as inner:
                    res["y"] = inner.enter_context(nc.sbuf_tensor(f"y{layer}", [P, TILES, D], F32))
                    swiglu(nc, t, res, layer, LAT_CHUNKS if last else CHUNKS)
                    norm_tiles(nc, t, res, "ffn", layer, tiles, last)
                if not last:
                    input_projection(nc, t, res, layer + 1)


def constants():
    import numpy as np
    f = np.float32
    out = {"ident": np.eye(P, dtype=f)}
    bm = np.zeros((P, P), f)
    bm[:64, :64] = bm[64:, 64:] = 1.0 / 64
    out["block_mean"] = bm
    grid_w, base = 64, 10000.0
    rows = N_LAT // grid_w
    row = np.repeat(np.arange(rows, dtype=f), grid_w)
    col = np.tile(np.arange(grid_w, dtype=f), rows)
    cos, sin = np.zeros((2, P, N_LAT), f), np.zeros((2, P, N_LAT), f)
    for which, dim in enumerate((DIFF_DH, SWA_DH)):
        nf = dim // 4
        inv = np.power(f(base), -np.arange(nf, dtype=f) / f(nf)).astype(f)
        ang = np.concatenate([row[:, None] * inv, col[:, None] * inv], axis=-1)
        for p in range(P):
            r = p % 32
            j = r % 16 + (16 * (p // 32 % 2) if dim == SWA_DH else 0)
            cos[which, p] = np.cos(ang[:, j])
            sin[which, p] = np.sin(ang[:, j]) * (-1.0 if r < 16 else 1.0)
    out["rope_cos"], out["rope_sin"] = cos, sin
    s, tt = np.arange(CH)[:, None], np.arange(CH)[None, :]
    masks = []
    for m in LEVELS:
        masks.append((s // (2 * m) == tt // (2 * m)) & (s % (2 * m) < m) & (tt % (2 * m) >= m))
    masks += [x.T for x in masks]
    masks.append(s == tt)
    out["gla_masks"] = np.ascontiguousarray(np.stack(masks, 1).astype(np.int32))
    q, kk = np.arange(P)[:, None], np.arange(P)[None, :]
    bias = np.zeros((LAT_TILES, P, 2 * P), f)
    bias[:, :, :P][:, kk < q] = -3e38
    bias[:, :, P:][:, kk > q] = -3e38
    bias[0, :, :P] = -3e38
    bias[LAT_TILES - 1, :, P:] = -3e38
    out["swa_bias"] = bias.reshape(LAT_TILES * P, 2 * P)
    return out


def kernel(x, c, ctx, c_ctx, w_ada, b_ada, w_in, w_gla_gate, b_gla_gate, gla_norm_g, diff_lambda,
           diff_norm_g, swa_sink, w_out, ln_g, ln_b, w_ffn_gate, w_ffn_up, w_ffn_down):
    import numpy as np
    import concourse.bacc as bacc
    from concourse.bass_utils import run_bass_kernel_spmd

    def tiled(w):
        L, d, n = w.shape
        return np.ascontiguousarray(w.reshape(L, KT, P, n // P, P).transpose(0, 3, 2, 1, 4)).reshape(L, n, D)

    at = np.cumsum([0, 256, 256, 256, 256, 16, 16, 256, 256, 256, 512, 128, 128])
    gq, gk, gv, go, z, _, dq, dk, dv, sq, sk, sv = [np.arange(a, b) for a, b in zip(at[:-1], at[1:])]
    z = np.arange(at[4], at[4] + P)
    turn = np.concatenate([np.arange(0, 16), np.arange(32, 48), np.arange(16, 32), np.arange(48, 64)])
    sq = np.concatenate([sq[h * 64 + turn] for j in range(4) for h in (j, 4 + j)])
    sk = np.concatenate([sk[h * 64 + turn] for h in range(2)])
    columns = np.concatenate([z, gq, gk, gv, go, dv, sv, dq, dk, sq, sk])
    groups = [tiled(np.asarray(w)).reshape(LAYERS, FFN_GROUPS, 2, P, D) for w in (w_ffn_gate, w_ffn_up)]
    down = np.asarray(w_ffn_down).reshape(LAYERS, FFN_GROUPS, 2, P, D)
    stream = np.stack([groups[0][:, :, 0], groups[1][:, :, 0], groups[0][:, :, 1], groups[1][:, :, 1],
                       down[:, :, 0], down[:, :, 1]], axis=2)
    arrays = {
        "x": np.asarray(x)[0], "ctx": np.asarray(ctx)[0],
        "cT": np.ascontiguousarray(np.stack([np.asarray(c)[0], np.asarray(c_ctx)]).reshape(2, KT, P).transpose(2, 1, 0)),
        "w_ada": np.asarray(w_ada), "b_ada": np.asarray(b_ada),
        "w_in": tiled(np.asarray(w_in)[:, :, columns]),
        "w_gate": np.asarray(w_gla_gate), "b_gate": np.asarray(b_gla_gate), "gla_norm_g": np.asarray(gla_norm_g),
        "diff_lambda": np.asarray(diff_lambda), "diff_norm_g": np.asarray(diff_norm_g), "swa_sink": np.asarray(swa_sink),
        "w_out": np.asarray(w_out), "ln_g": np.asarray(ln_g), "ln_b": np.asarray(ln_b),
        "w_ffn": stream.reshape(LAYERS, FFN_GROUPS * 6 * P, D),
        **constants(),
    }
    arrays = {n + "_dram": np.ascontiguousarray(a) for n, a in arrays.items()}
    nc = bacc.Bacc("TRN2", target_bir_lowering=False, num_devices=1)
    t = {n[:-5]: nc.dram_tensor(n, a.shape, mybir.dt.from_np(a.dtype), kind="ExternalInput").ap() for n, a in arrays.items()}
    for name, shape in (("mod", (LAYERS, 2, ADA)), ("proj", (IN_TILES * P, PAD_T)), ("mix", (D, T)), ("h_mid", (T, D)), ("h_next", (T, D))):
        t[name] = nc.dram_tensor(name + "_scratch", shape, F32, kind="Internal").ap()
    t["heads"] = nc.dram_tensor("heads_scratch", (2, HEAD_ROWS, PAD_T), F32, kind="Internal").ap()
    t["out"] = nc.dram_tensor("out_dram", (N_LAT, D), F32, kind="ExternalOutput").ap()
    build(nc, t)
    got = run_bass_kernel_spmd(nc, [arrays], core_ids=[0])
    return got.results[0]["out_dram"].reshape(1, N_LAT, D)
```
